# Optimizing a Trainium2 kernel written in Bass

```python
import math
import jax, jax.numpy as jnp
from jax import lax
import numpy as np

D_MODEL = 2048
BATCH = 1
SEQ = 256
DEPTH = 1
DEC_BATCH = 8
DEC_SEQ = 1
PAST_LEN = 256
PAGE_SIZE = 128

MIX_WIDTH = D_MODEL
ATT_WIDTH = MIX_WIDTH // 2
CONV_WIDTH = MIX_WIDTH - ATT_WIDTH
V_DIM = 128
N_ATT_HEADS = ATT_WIDTH // V_DIM
QK_HALF = V_DIM // 2
QK_DIM = 2 * QK_HALF
CONV_K = 3
N_GROUPS = 4
EXPERTS_PER_GROUP = 8
N_EXPERTS = N_GROUPS * EXPERTS_PER_GROUP
TOP_K = 2
D_EXPERT = D_MODEL // 4
MOE_BLOCK = 128
Q_BLOCK = 128
EPS = 1e-6
IN_COLS = 3 * ATT_WIDTH + 3 * CONV_WIDTH

kernel_name = "hybrid_diffattn_shortconv_hiermoe_step"

def rms_norm(x, g):
    xf = x.astype(jnp.float32)
    y = xf * lax.rsqrt(jnp.mean(xf * xf, axis=-1, keepdims=True) + EPS)
    return (y * g.astype(jnp.float32)).astype(x.dtype)

def alibi_slopes():
    return 2.0 ** (-8.0 * jnp.arange(1, N_ATT_HEADS + 1, dtype=jnp.float32) / N_ATT_HEADS)

def diff_lambda(lq1, lk1, lq2, lk2, lam_init):
    f = lambda a: a.astype(jnp.float32)
    return jnp.exp(jnp.sum(f(lq1) * f(lk1))) - jnp.exp(jnp.sum(f(lq2) * f(lk2))) + lam_init

def project(h, w_in, g_q, g_k):
    b, t, _ = h.shape
    p = h @ w_in
    a = ATT_WIDTH
    q, k, v, bg, cg, xc = jnp.split(p, [a, 2 * a, 3 * a, 3 * a + CONV_WIDTH, 3 * a + 2 * CONV_WIDTH], axis=-1)
    q = rms_norm(q.reshape(b, t, N_ATT_HEADS, 2, QK_HALF), g_q)
    k = rms_norm(k.reshape(b, t, N_ATT_HEADS, 2, QK_HALF), g_k)
    v = v.reshape(b, t, N_ATT_HEADS, V_DIM)
    return q, k, v, bg, cg, xc

def diff_scores(q, k, q_pos, k_pos):
    s = jnp.einsum("bqhcd,bkhcd->bhcqk", q, k, preferred_element_type=jnp.float32) * (QK_HALF ** -0.5)
    dist = q_pos[:, None] - k_pos[None, :]
    s = s - alibi_slopes()[:, None, None, None] * dist.astype(jnp.float32)
    return jnp.where(dist >= 0, s, -jnp.inf)

def diff_weights(s, lam):
    p = jax.nn.softmax(s, axis=-1)
    return p[:, :, 0] - lam * p[:, :, 1]

def prompt_attention(q, k, v, lam):
    b, s = q.shape[:2]
    nblk = s // Q_BLOCK
    qb = jnp.moveaxis(q.reshape(b, nblk, Q_BLOCK, N_ATT_HEADS, 2, QK_HALF), 1, 0)
    pos = jnp.arange(s, dtype=jnp.int32)
    pb = pos.reshape(nblk, Q_BLOCK)

    def block(args):
        q_blk, p_blk = args
        a = diff_weights(diff_scores(q_blk, k, p_blk, pos), lam).astype(v.dtype)
        return jnp.einsum("bhqk,bkhd->bqhd", a, v)

    o = lax.map(block, (qb, pb))
    return jnp.moveaxis(o, 0, 1).reshape(b, s, N_ATT_HEADS, V_DIM)

def sample_attention(q, k_new, v_new, k_pages, v_pages, lam):
    nb, t = q.shape[:2]
    past = k_pages.shape[1] * PAGE_SIZE
    k_past = k_pages.reshape(nb, past, N_ATT_HEADS, 2, QK_HALF)
    v_past = v_pages.reshape(nb, past, N_ATT_HEADS, V_DIM)
    q_pos = past + jnp.arange(t, dtype=jnp.int32)
    s = jnp.concatenate([diff_scores(q, k_past, q_pos, jnp.arange(past, dtype=jnp.int32)),
                         diff_scores(q, k_new, q_pos, q_pos)], axis=-1)
    a = diff_weights(s, lam).astype(v_new.dtype)
    return (jnp.einsum("bhqk,bkhd->bqhd", a[..., :past], v_past)
            + jnp.einsum("bhqk,bkhd->bqhd", a[..., past:], v_new))

def short_conv(bg, cg, xc, conv_w, prev):
    u = cg * xc
    u_pad = jnp.concatenate([prev.astype(u.dtype), u], axis=1)
    t = u.shape[1]
    y = conv_w[0] * u_pad[:, 0:t]
    for j in range(1, CONV_K):
        y = y + conv_w[j] * u_pad[:, j:j + t]
    return bg * y, u_pad[:, -(CONV_K - 1):]

def merge_heads(o_att, y_conv, g_sub, lam_init, w_out):
    b, t = y_conv.shape[:2]
    o = rms_norm(o_att, g_sub) * (1.0 - lam_init)
    cat = jnp.concatenate([o.reshape(b, t, ATT_WIDTH), y_conv], axis=-1)
    return cat @ w_out

def grouped_experts(x, e_idx, gate, w_gate, w_up, w_down):
    n_tok, d = x.shape
    n_assign = n_tok * TOP_K
    flat_e = e_idx.reshape(n_assign)
    flat_tok = jnp.repeat(jnp.arange(n_tok, dtype=jnp.int32), TOP_K)
    flat_w = gate.reshape(n_assign)
    order = jnp.argsort(flat_e, stable=True)
    sorted_e = flat_e[order]
    counts = jnp.bincount(flat_e, length=N_EXPERTS)
    padded = (counts + MOE_BLOCK - 1) // MOE_BLOCK * MOE_BLOCK
    pad_end = jnp.cumsum(padded)
    pad_start = pad_end - padded
    start = jnp.cumsum(counts) - counts
    dest = pad_start[sorted_e] + (jnp.arange(n_assign, dtype=jnp.int32) - start[sorted_e])
    n_blocks = -(-n_assign // MOE_BLOCK) + N_EXPERTS
    n_slots = n_blocks * MOE_BLOCK
    slot_tok = jnp.full((n_slots,), n_tok, jnp.int32).at[dest].set(flat_tok[order])
    slot_w = jnp.zeros((n_slots,), x.dtype).at[dest].set(flat_w[order])
    block_e = jnp.minimum(jnp.searchsorted(pad_end, jnp.arange(n_blocks) * MOE_BLOCK, side="right"), N_EXPERTS - 1)
    x_pad = jnp.concatenate([x, jnp.zeros((1, d), x.dtype)], axis=0)
    xb = x_pad[slot_tok].reshape(n_blocks, MOE_BLOCK, d)

    def expert_block(args):
        xblk, e = args
        return (jax.nn.silu(xblk @ w_gate[e]) * (xblk @ w_up[e])) @ w_down[e]

    yb = lax.map(expert_block, (xb, block_e)).reshape(n_slots, d) * slot_w[:, None]
    return jax.ops.segment_sum(yb, slot_tok, num_segments=n_tok + 1)[:n_tok]

def hier_moe(h, w_rg, b_rg, w_re, b_re, w_gate, w_up, w_down):
    b, t, d = h.shape
    x = h.reshape(b * t, d)
    xf = x.astype(jnp.float32)
    lg = xf @ w_rg.astype(jnp.float32) + b_rg.astype(jnp.float32)
    pg = jax.nn.softmax(lg, axis=-1)
    g_star = jnp.argmax(lg, axis=-1)
    p_group = jnp.take_along_axis(pg, g_star[:, None], axis=1)
    le = (xf @ w_re.astype(jnp.float32) + b_re.astype(jnp.float32)).reshape(b * t, N_GROUPS, EXPERTS_PER_GROUP)
    le = jnp.take_along_axis(le, g_star[:, None, None], axis=1)[:, 0]
    pe = jax.nn.softmax(le, axis=-1)
    top_p, top_i = lax.top_k(pe, TOP_K)
    w = p_group * top_p / jnp.sum(top_p, axis=-1, keepdims=True)
    e_idx = g_star[:, None].astype(jnp.int32) * EXPERTS_PER_GROUP + top_i.astype(jnp.int32)
    y = grouped_experts(x, e_idx, w.astype(x.dtype), w_gate, w_up, w_down)
    return y.reshape(b, t, d)

def setup_inputs(seed: int = 0) -> dict:
    key = jax.random.key(seed)
    ks = jax.random.split(key, 26)
    f32 = jnp.float32

    def nrm(k, shape, scale):
        return jax.random.normal(k, shape, f32) * scale

    n_pages = PAST_LEN // PAGE_SIZE
    n_used = DEC_BATCH * n_pages
    n_pool = n_used + max(1, n_used // 4)
    page_table = jax.random.permutation(ks[5], n_pool)[:n_used].reshape(DEC_BATCH, n_pages).astype(jnp.int32)
    return {
        "x_prompt": nrm(ks[0], (BATCH, SEQ, D_MODEL), 1.0),
        "x_sample": nrm(ks[1], (DEC_BATCH, DEC_SEQ, D_MODEL), 1.0),
        "cache_k": nrm(ks[2], (DEPTH, n_pool, PAGE_SIZE, N_ATT_HEADS, QK_DIM), 1.0),
        "cache_v": nrm(ks[3], (DEPTH, n_pool, PAGE_SIZE, N_ATT_HEADS, V_DIM), 1.0),
        "state_conv": nrm(ks[4], (DEPTH, DEC_BATCH, CONV_K - 1, CONV_WIDTH), 1.0),
        "page_table": page_table,
        "norm_mix": 1.0 + nrm(ks[6], (DEPTH, D_MODEL), 0.02),
        "w_in": nrm(ks[7], (DEPTH, D_MODEL, IN_COLS), D_MODEL ** -0.5),
        "g_q": 1.0 + nrm(ks[8], (DEPTH, QK_HALF), 0.02),
        "g_k": 1.0 + nrm(ks[9], (DEPTH, QK_HALF), 0.02),
        "lam_q1": nrm(ks[10], (DEPTH, QK_HALF), 0.1),
        "lam_k1": nrm(ks[11], (DEPTH, QK_HALF), 0.1),
        "lam_q2": nrm(ks[12], (DEPTH, QK_HALF), 0.1),
        "lam_k2": nrm(ks[13], (DEPTH, QK_HALF), 0.1),
        "g_sub": 1.0 + nrm(ks[14], (DEPTH, V_DIM), 0.02),
        "conv_w": nrm(ks[15], (DEPTH, CONV_K, CONV_WIDTH), CONV_K ** -0.5),
        "w_out": nrm(ks[16], (DEPTH, MIX_WIDTH, D_MODEL), MIX_WIDTH ** -0.5),
        "norm_ffn": 1.0 + nrm(ks[17], (DEPTH, D_MODEL), 0.02),
        "w_router_group": nrm(ks[18], (DEPTH, D_MODEL, N_GROUPS), D_MODEL ** -0.5),
        "b_router_group": nrm(ks[19], (DEPTH, N_GROUPS), 0.01),
        "w_router_expert": nrm(ks[20], (DEPTH, D_MODEL, N_EXPERTS), D_MODEL ** -0.5),
        "b_router_expert": nrm(ks[21], (DEPTH, N_EXPERTS), 0.01),
        "w_gate": nrm(ks[22], (DEPTH, N_EXPERTS, D_MODEL, D_EXPERT), D_MODEL ** -0.5),
        "w_up": nrm(ks[23], (DEPTH, N_EXPERTS, D_MODEL, D_EXPERT), D_MODEL ** -0.5),
        "w_down": nrm(ks[24], (DEPTH, N_EXPERTS, D_EXPERT, D_MODEL), D_EXPERT ** -0.5),
    }

def reference(x_prompt, x_sample, cache_k, cache_v, state_conv, page_table,
              norm_mix, w_in, g_q, g_k, lam_q1, lam_k1, lam_q2, lam_k2, g_sub, conv_w, w_out,
              norm_ffn, w_router_group, b_router_group, w_router_expert, b_router_expert,
              w_gate, w_up, w_down):
    xp, xs = x_prompt, x_sample
    kp, vp, cp, ksm, vsm, csm = [], [], [], [], [], []
    for l in range(DEPTH):
        lam_init = 0.8 - 0.6 * math.exp(-0.3 * l)
        lam = diff_lambda(lam_q1[l], lam_k1[l], lam_q2[l], lam_k2[l], lam_init)

        b, t = xp.shape[:2]
        q, k, v, bg, cg, xc = project(rms_norm(xp, norm_mix[l]), w_in[l], g_q[l], g_k[l])
        o = prompt_attention(q, k, v, lam)
        yc, conv_new = short_conv(bg, cg, xc, conv_w[l], jnp.zeros((b, CONV_K - 1, CONV_WIDTH), xp.dtype))
        xp = xp + merge_heads(o, yc, g_sub[l], lam_init, w_out[l])
        xp = xp + hier_moe(rms_norm(xp, norm_ffn[l]), w_router_group[l], b_router_group[l],
                           w_router_expert[l], b_router_expert[l], w_gate[l], w_up[l], w_down[l])
        kp.append(k.reshape(b, t, N_ATT_HEADS, QK_DIM))
        vp.append(v)
        cp.append(conv_new)

        nb, ts = xs.shape[:2]
        q, k, v, bg, cg, xc = project(rms_norm(xs, norm_mix[l]), w_in[l], g_q[l], g_k[l])
        o = sample_attention(q, k, v, cache_k[l, page_table], cache_v[l, page_table], lam)
        yc, conv_new = short_conv(bg, cg, xc, conv_w[l], state_conv[l])
        xs = xs + merge_heads(o, yc, g_sub[l], lam_init, w_out[l])
        xs = xs + hier_moe(rms_norm(xs, norm_ffn[l]), w_router_group[l], b_router_group[l],
                           w_router_expert[l], b_router_expert[l], w_gate[l], w_up[l], w_down[l])
        ksm.append(k.reshape(nb, ts, N_ATT_HEADS, QK_DIM))
        vsm.append(v)
        csm.append(conv_new)

    k_prompt = jnp.stack(kp, axis=0)
    v_prompt = jnp.stack(vp, axis=0)
    conv_prompt = jnp.stack(cp, axis=0)
    k_sample = jnp.stack(ksm, axis=0)
    v_sample = jnp.stack(vsm, axis=0)
    conv_sample = jnp.stack(csm, axis=0)
    return (xp, xs, k_prompt, v_prompt, conv_prompt, k_sample, v_sample, conv_sample)


_drawn_inputs = setup_inputs


def setup_inputs(seed=0):
    import zlib

    import numpy as np

    out = dict(_drawn_inputs(seed))
    spreads = {}
    factors = {'g_q': 3.228,
     'lam_q1': 5.193,
     'g_sub': 8.403,
     'b_router_group': 4.504,
     'b_router_expert': 26.83,
     'norm_ffn': 4.018}
    for name, (base, spread) in spreads.items():
        noise = np.random.default_rng([zlib.crc32(name.encode()), seed]).standard_normal(out[name].shape)
        drawn = base * np.exp(spread * noise) if base else spread * noise
        out[name] = __import__('jax').numpy.asarray(drawn.astype(out[name].dtype))
    for name, factor in factors.items():
        out[name] = (out[name] * factor).astype(out[name].dtype)
    return out
```

```python
from contextlib import ExitStack

import concourse.bass as bass
from concourse import mybir

F32 = mybir.dt.float32
I32 = mybir.dt.int32
ALU = mybir.AluOpType
ACT = mybir.ActivationFunctionType
AX = mybir.AxisListType

P = 128
D = 2048
KT = D // P
SEQ = 256
NB = 8
T = SEQ + NB
TT = 3
H = 8
HD = 128
HALF = HD // 2
ATT = H * HD
CONV = D - ATT
CT = CONV // P
PAST = 256
PAGE = 128
NPG = PAST // PAGE
GROUPS = 4
EPG = 8
NE = GROUPS * EPG
F = D // 4
FC = F // P
EPS = 1e-6
LAM_INIT = 0.8 - 0.6
FAR = -1e30

SLOTS = 8
UNIT = 4096
UC = UNIT // KT
TPU = UC // P

EG = 4
C = P // EG
NG = NE // EG
PASS_SLOTS = NE * C
MAXPASS = -(-T // C)
UPE = 6
UPG = UPE * EG

FRONT = ([("q", u) for u in range(4)] + [("k", u) for u in range(4)] + [("v", u) for u in range(4)]
         + [("C", 0), ("X", 0), ("B", 0), ("QB", 0), ("KP", 0), ("KP", 1),
            ("C", 1), ("X", 1), ("B", 1), ("QB", 1), ("KP", 2),
            ("C", 2), ("X", 2), ("B", 2), ("KP", 3),
            ("C", 3), ("X", 3), ("B", 3)]
         + [("VP", u) for u in range(4)] + [("W", u) for u in range(8)])
NFRONT = len(FRONT)
COLUMN = {"q": 0, "k": ATT, "v": 2 * ATT, "B": 3 * ATT, "C": 3 * ATT + CONV, "X": 3 * ATT + 2 * CONV}
TILES = ([("q", h) for h in range(H)] + [("k", h) for h in range(H)] + [("v", h) for h in range(H)]
         + [(c, i) for i in range(CT) for c in "CXB"] + [("W", j) for j in range(KT)])
TILE_AT = {t: n for n, t in enumerate(TILES)}
BCX = 3 * H
PAGES_AT = [3, 3, 3, 3, 2, 2, 0, 0]
PAGES_BY = [sum(PAGES_AT[:i]) for i in range(CT + 1)]
NPAGES = NB * NPG
PPU = 4

CONSTS = [("ident", P), ("ones", P), ("fold", C), ("blk", P), ("sel", H * NB), ("dist", SEQ), ("kpos", PAST),
          ("slope", 1), ("neg_c1", 1), ("c0", 1), ("valid", TT), ("kth", MAXPASS), ("eps", 1)]
CONST_AT, _n = {}, 0
for _name, _w in CONSTS:
    CONST_AT[_name] = (_n, _n + _w)
    _n += _w
NCONST = _n
LATE = [("iota", P), ("tri", P), ("base", NE), ("down32", NE), ("down4", GROUPS), ("pad", 512 - 2 * P - 2 * NE - GROUPS)]
LATE_AT, _n = {}, 0
for _name, _w in LATE:
    LATE_AT[_name] = (_n, _n + _w)
    _n += _w
SLOPES = [2.0 ** (-8.0 * (h + 1) / H) for h in range(H)]


class Steps:

    def __init__(self, eng, sem):
        self.eng, self.sem, self.n, self.base = eng, sem, 0, 0

    def add(self, ins):
        ins.then_inc(self.sem, 1)
        self.n += 1

    def wait(self):
        self.eng.wait_ge(self.sem, self.base + self.n)

    def do(self, ins):
        self.add(ins)
        self.wait()


def build(nc, ins, outs):
    ctx = ExitStack()
    with ctx:
        def sb(name, shape, dt=F32):
            return ctx.enter_context(nc.sbuf_tensor(name, shape, dt))

        def sem(name):
            return ctx.enter_context(nc.semaphore(name))

        ring = sb("ring", [P, SLOTS, UNIT])
        xa = sb("xa", [P, TT, D])
        bc = sb("bc", [P, 2 * KT * T])
        cat = sb("cat", [P, KT, T])
        consts = sb("consts", [P, NCONST])
        small = sb("small", [P, 440])
        gains = sb("gains", [P, 2 * KT])
        pages = sb("pages", [1, NPAGES], I32)
        npass_sb = sb("npass_sb", [1, 1], I32)
        qrows_dram = nc.dram_tensor("qrows_scratch", [NB, ATT], F32).ap()

        bank = [ctx.enter_context(nc.psum_tensor(f"bank{i}", [P, 512], F32)) for i in range(8)]

        def const(name):
            a, b = CONST_AT[name]
            return consts[:, a:b]

        late0 = CONST_AT["dist"][0]

        def late(name):
            a, b = LATE_AT[name]
            return consts[:, late0 + a:late0 + b]

        ident = const("ident")

        hT = bc[:, 0:KT * T].rearrange("p (k t) -> p k t", t=T)
        qkT = bc[:, KT * T:].rearrange("p (k t) -> p k t", t=T)
        vrow = xa[:, 0, :].rearrange("p (t c) -> p t c", t=2)
        tmp = xa[:, 1:3, :].rearrange("p a n -> p (a n)")
        kvstage = [tmp[:, 384 * i:384 * i + 384] for i in range(2)]
        prob = tmp[:, 0:768]
        qz = tmp[:, 768:1280].rearrange("p (c q) -> p c q", c=2)
        vT = [tmp[:, 768 + T * i:768 + T * i + T] for i in range(2)]
        osq = tmp[:, 1296:1552]
        ord_ = tmp[:, 1560:1816]
        sq = [tmp[:, 1296 + T * i:1296 + T * i + T] for i in range(2)]
        diff = tmp[:, 1824:2208]
        diffT = tmp[:, 2208:2592]
        rstd = [tmp[:, 1824 + T * i:1824 + T * i + T] for i in range(2)]
        ctmp = tmp[:, 2592:2592 + T]
        upad = tmp[:, 2856:2856 + T + 2]
        conv = tmp[:, 3122:3122 + T]
        keysc = tmp[:, 3386:3642].rearrange("p (g c h b) -> p g c h b", g=NPG, c=2, h=H)
        rowsc = tmp[:, 3642:3642 + PAST + 1]
        selfqk = tmp[:, 3902:4030]
        selfsel = tmp[:, 4030:4094]
        pairw = selfqk

        o = [0]

        def piece(n):
            o[0] += n
            return small[:, o[0] - n:o[0]]

        convwT = piece(3 * CT)
        prevT = piece(NB * 2 * CT)
        stash = piece((2 + NB) * CT)
        vTs = piece(H * NB)
        ssum = piece(4)
        srstd = piece(4)
        lamv = piece(4)
        nmax = piece(4)
        esum = piece(4)
        rsum = piece(4)
        gqk = piece(2)
        gsub = piece(2)
        route = piece(4 * TT)
        gmix = gains[:, 0:KT]
        gffn = gains[:, KT:2 * KT]

        rawrows = ring[:, SLOTS - 1, 0:256]
        lamraw = ring[:, SLOTS - 1, 256:256 + 4 * HALF]
        lamprod = ring[:, SLOTS - 1, 512:512 + HALF]
        sqjunk = ring[:, SLOTS - 2, 0:D]
        sqjunk2 = ring[:, SLOTS - 3, 0:D]

        yT = [bc[:, T * i:T * i + T] for i in range(2)]
        junk_act = bc[:, 4224:4224 + D]
        junk_dve = bc[:, 6272:6272 + D]
        h2 = bc[:, 0:TT * D].rearrange("p (t d) -> p t d", t=TT)
        h2T = [bc[:, 6144 + T * i:6144 + T * i + T] for i in range(3)]
        sel = bc[:, 6144:6528].rearrange("p (t s) -> p t s", t=TT)
        gate = bc[:, 6528:6912].rearrange("p (t s) -> p t s", t=TT)
        gateT = bc[:, 6912:7296].rearrange("p (t s) -> p t s", t=TT)
        g_sb = bc[:, 7296:7808]
        u_sb = bc[:, 7808:8320]
        actT = bc[:, 8320:8448].rearrange("p (c s) -> p c s", c=FC)
        catf = cat[:, :, :].rearrange("p k t -> p (k t)")
        xeT = catf[:, 0:D].rearrange("p (k s) -> p k s", k=KT)
        ye = catf[:, D:2 * D]
        wr = catf[:, 0:KT * (GROUPS + NE)]
        wrg = wr[:, 0:KT * GROUPS].rearrange("p (k e) -> p k e", e=GROUPS)
        wre = wr[:, KT * GROUPS:].rearrange("p (k e) -> p k e", e=NE)
        rbias = catf[:, 600:600 + GROUPS + NE]
        o[0] = 0

        def rt(n):
            o[0] += n
            return catf[:, D + o[0] - n:D + o[0]].rearrange("p (t e) -> p t e", t=TT)

        logits = rt(TT * (GROUPS + NE))
        gm, gi, gs, pg, m1, m2, i1, i2, ew, wn = (rt(TT) for _ in range(10))
        geq, goh, gex, geneg = (rt(TT * GROUPS) for _ in range(4))
        lem, eq, oh1, oh2, both, rank, work, rb = (rt(TT * NE) for _ in range(8))
        rk1, rk2, ov, over = (rt(TT) for _ in range(4))
        exc = rt(TT * MAXPASS)
        tot = catf[:, D + o[0]:D + o[0] + NE]
        cmax = catf[:, D + o[0] + NE:D + o[0] + NE + 1]
        cpass = catf[:, D + o[0] + NE + 1:D + o[0] + NE + 2]
        cwork = catf[:, D + o[0] + NE + 2:D + o[0] + NE + 2 + MAXPASS]
        pos1, pos2, w1, w2 = (route[:, TT * i:TT * i + TT] for i in range(4))

        slot_full = [sem(f"slot_full{i}") for i in range(SLOTS)]
        x_in = [sem(f"x_in{i}") for i in range(TT)]
        consts_in = sem("consts_in")
        vecs_in = sem("vecs_in")
        late_in = sem("late_in")
        wr_in = sem("wr_in")
        pages_in = sem("pages_in")
        x_again = sem("x_again")
        x2_zero = sem("x2_zero")
        x_clear = sem("x_clear")
        raw_T = sem("raw_T")
        raw_copied = sem("raw_copied")
        sums1_dve = sem("sums1_dve")
        sums1 = sem("sums1")
        h_rows = sem("h_rows")
        sqrt1 = sem("sqrt1")
        h_T = sem("h_T")
        h_ready = sem("h_ready")
        tile_done = sem("tile_done")
        squared = sem("squared")
        summed = sem("summed")
        rooted = sem("rooted")
        qk_ready = sem("qk_ready")
        v_copied = sem("v_copied")
        rows_T = sem("rows_T")
        rows_out = sem("rows_out")
        v_rows = sem("v_rows")
        vs_ready = sem("vs_ready")
        stored = [sem("stored0"), sem("stored1")]
        c_copied = sem("c_copied")
        u_ready = sem("u_ready")
        conv_ready = sem("conv_ready")
        stash_T = sem("stash_T")
        stash_out = sem("stash_out")
        stash_ready = sem("stash_ready")
        qz_ready = sem("qz_ready")
        qz_zero = sem("qz_zero")
        scores = sem("scores")
        biased = sem("biased")
        exped = sem("exped")
        diffed = sem("diffed")
        diff_T = sem("diff_T")
        diffT_copied = sem("diffT_copied")
        pv = sem("pv")
        o_squared = sem("o_squared")
        o_summed = sem("o_summed")
        o_rooted = sem("o_rooted")
        o_ready = sem("o_ready")
        page_mul = sem("page_mul")
        page_sum = sem("page_sum")
        self_ready = sem("self_ready")
        s_T = sem("s_T")
        s_biased = sem("s_biased")
        s_exped = sem("s_exped")
        s_probs = sem("s_probs")
        s_pair = sem("s_pair")
        s_pair_copied = sem("s_pair_copied")
        s_pv = sem("s_pv")
        y_copied = sem("y_copied")
        y_T = sem("y_T")
        y_added = sem("y_added")
        sums2_dve = sem("sums2_dve")
        sums2 = sem("sums2")
        sqrt2 = sem("sqrt2")
        h2_rows = sem("h2_rows")
        h2_T = sem("h2_T")
        h2_ready = sem("h2_ready")
        router = sem("router")
        gex_ready = sem("gex_ready")
        gexed = sem("gexed")
        assigned = sem("assigned")
        ranked = sem("ranked")
        routed = sem("routed")
        sel_ready = sem("sel_ready")
        gate_ready = sem("gate_ready")
        gathered = sem("gathered")
        xe_ready = sem("xe_ready")
        gate_T = sem("gate_T")
        gateT_copied = sem("gateT_copied")
        g_done = sem("g_done")
        u_done = sem("u_done")
        g_copied = sem("g_copied")
        u_copied = sem("u_copied")
        folded = sem("folded")
        silu_done = sem("silu_done")
        act_ready = sem("act_ready")
        unit_used = sem("unit_used")
        down_done = sem("down_done")
        ye_act = sem("ye_act")
        ye_dve = sem("ye_dve")
        mixed = sem("mixed")
        mix_added = sem("mix_added")
        y_stored = sem("y_stored")
        state_stored = sem("state_stored")
        dve_step = sem("dve_step")
        act_step = sem("act_step")

        def slot_of(n):
            return n % SLOTS

        front_total = [0] * SLOTS
        front_at = {}
        for n, unit in enumerate(FRONT):
            front_total[slot_of(n)] += 16 * (PPU if unit[0] in ("KP", "VP") else 1)
            front_at[unit] = (slot_of(n), front_total[slot_of(n)])

        def arrived(eng, unit):
            s, value = front_at[unit]
            eng.wait_ge(slot_full[s], value)

        def used_wait(eng, n):
            kind, u = FRONT[n]
            if kind == "KP":
                eng.wait_ge(page_sum, PPU * (u + 1))
            elif kind == "QB":
                eng.wait_ge(page_mul, 8 * (u + 1))
            elif kind == "VP":
                eng.wait_ge(s_pv, u + 1)
            else:
                eng.wait_ge(tile_done, TILE_AT[(kind, TPU * u + TPU - 1)] + 1)

        block = ctx.enter_context(nc.Block())

        @block.sync
        def _(sp):
            w_in = ins["w_in"].rearrange("l (p k) n -> (l p) k n", k=KT)
            w_out = ins["w_out"].rearrange("l (k p) n -> (l p) k n", p=P)
            xp = ins["x_prompt"].rearrange("o (t p) d -> (o t) p d", p=P)
            for t in range(2):
                sp.dma_start(xa[:, t, :], xp[t]).then_inc(x_in[t], 16)
            sp.dma_start(pages[:, :], ins["page_table"].rearrange("(o b) g -> o (b g)", o=1)).then_inc(pages_in, 16)

            for n, (kind, u) in enumerate(FRONT):
                s = slot_of(n)
                if n == SLOTS - 3:
                    sp.wait_ge(h_rows, TT)
                    sp.wait_ge(raw_T, 1)
                if n >= SLOTS:
                    used_wait(sp, n - SLOTS)
                if kind == "W":
                    sp.dma_start(ring[:, s, :].rearrange("p (k c) -> p k c", k=KT),
                                 w_out[:, :, u * UC:(u + 1) * UC]).then_inc(slot_full[s], 16)
                elif kind == "QB":
                    for i in range(4):
                        sp.wait_ge(stored[i % 2], 16 * (H // 2))
                    sp.dma_start(ring[:, s, :].rearrange("p (b c) -> p b c", b=4),
                                 qrows_dram[4 * u:4 * u + 4, :].partition_broadcast(P)).then_inc(slot_full[s], 16)
                elif kind in ("KP", "VP"):
                    if (kind, u) == ("KP", 0):
                        sp.wait_ge(pages_in, 16)
                    pool_rows = ins["cache_k" if kind == "KP" else "cache_v"].rearrange("l n s h c -> (l n) s (h c)")
                    for i in range(PPU):
                        j = u * PPU + i
                        page = sp.value_load(pages[0:1, j:j + 1], min_val=0, max_val=pool_rows.shape[0] - 1)
                        sp.dma_start(ring[:, s, i * ATT:(i + 1) * ATT],
                                     pool_rows[bass.ds(page, 1), :, :].rearrange("o s c -> s (o c)")
                                     ).then_inc(slot_full[s], 16)
                else:
                    c0 = COLUMN[kind] + u * UC
                    sp.dma_start(ring[:, s, :].rearrange("p (k c) -> p k c", k=KT),
                                 w_in[:, :, c0:c0 + UC]).then_inc(slot_full[s], 16)

            wg = ins["w_gate"].rearrange("l (g j) (p k) f -> (l g) p j (k f)", j=EG, k=KT)
            wu = ins["w_up"].rearrange("l (g j) (p k) f -> (l g) p j (k f)", j=EG, k=KT)
            wd = ins["w_down"].rearrange("l (g j) (p k) d -> (l g) p j (k d)", j=EG, k=FC)

            def expert_used(m, it):
                j, i = divmod(m, UPE)
                if i % 2 == 0:
                    sp.wait_ge(unit_used, it * (3 * EG) + (3 * j + i // 2 + 1))
                else:
                    sp.wait_ge((g_done, u_done, down_done)[i // 2], it * EG + (j + 1))

            def group(g, it):
                for j in range(EG):
                    for i in range(UPE):
                        m = j * UPE + i
                        s = slot_of(NFRONT + m)
                        src = (wg, wg, wu, wu, wd, wd)[i]
                        expert_used(m - SLOTS, it)
                        sp.dma_start(ring[:, s, :], src[bass.ds(g, 1), :, j, (i % 2) * UNIT:(i % 2 + 1) * UNIT]
                                     .rearrange("o p n -> p (o n)")).then_inc(slot_full[s], 16)

            for m in range(UPG):
                s = slot_of(NFRONT + m)
                j, i = divmod(m, UPE)
                if m < SLOTS:
                    used_wait(sp, NFRONT + m - SLOTS)
                else:
                    expert_used(m - SLOTS, 0)
                src = (wg, wg, wu, wu, wd, wd)[i]
                sp.dma_start(ring[:, s, :], src[0, :, j, (i % 2) * UNIT:(i % 2 + 1) * UNIT]).then_inc(slot_full[s], 16)
            with sp.Fori(1, NG) as g:
                group(g, g)
            sp.wait_ge(routed, 1)
            npass = sp.value_load(npass_sb[0:1, 0:1], min_val=1, max_val=MAXPASS)
            with sp.If(npass > 1):
                with sp.Fori(1, npass) as r:
                    with sp.Fori(0, NG) as g:
                        group(g, r * NG + g)
            with sp.Else():
                pass

            sp.wait_ge(mix_added, npass * (NG * TT * 4) + 2)
            for t in range(2):
                sp.dma_start(outs["y_prompt"].rearrange("o (t p) d -> (o t) p d", p=P)[t], xa[:, t, :]).then_inc(y_stored, 16)
            sp.dma_start(outs["y_sample"].rearrange("b o d -> b (o d)"), xa[0:NB, 2, :]).then_inc(y_stored, 16)
            sp.wait_ge(y_stored, 48)
            sp.wait_ge(state_stored, 16)
            sp.wait_ge(stored[0], STORED[0] + 16)
            sp.wait_ge(stored[1], STORED[1] + 16 * NB)

        @block.tensor
        def _(pe):
            pe.wait_ge(consts_in, 16)
            pe.wait_ge(vecs_in, VECS * 16)
            pe.transpose(bank[7][:, 0:3 * CT], rawrows[0:3 * CT, 0:P], ident[0:3 * CT, 0:3 * CT])
            pe.transpose(bank[7][:, P:2 * P], rawrows[:, P:2 * P], ident).then_inc(raw_T, 1)

            pe.wait_ge(h_rows, TT)
            for k in range(KT):
                if k >= 4:
                    pe.wait_ge(h_ready, k - 3)
                for t in range(TT):
                    m = pe.transpose(bank[3 + k % 4][:, P * t:P * t + P], xa[:, t, k::KT], ident)
                m.then_inc(h_T, 1)

            def bank_free(n):
                if n < 3:
                    return
                kind, i = TILES[n - 3]
                s, value = {"q": (qk_ready, i + 1), "k": (qk_ready, H + i + 1), "v": (v_copied, i + 1),
                            "C": (c_copied, i + 1), "X": (u_ready, i + 1), "B": (conv_ready, i + 1),
                            "W": (y_copied, i + 1)}[kind]
                pe.wait_ge(s, value)

            def tile(n):
                kind, i = TILES[n]
                unit = (kind, i // TPU)
                arrived(pe, unit)
                bank_free(n)
                w = ring[:, front_at[unit][0], :].rearrange("p (k c) -> p k c", k=KT)
                order = range(KT)
                src = hT
                if kind == "W":
                    order = [*range(H, KT), *range(H)]
                    src = cat
                for n_k, k in enumerate(order):
                    if kind == "W" and n_k == 0 and i == 0:
                        pe.wait_ge(conv_ready, CT)
                    if kind == "W" and n_k == H and i == 0:
                        pe.wait_ge(o_ready, H + 1)
                    m = pe.matmul(bank[n % 3][:, 0:T], w[:, k, (i % TPU) * P:(i % TPU + 1) * P], src[:, k, :],
                                  start=n_k == 0, stop=n_k == KT - 1)
                m.then_inc(tile_done, 1)

            def half_sums(t):
                pe.wait_ge(squared, t + 1)
                if t >= 1:
                    pe.wait_ge(rooted, t)
                pe.matmul(bank[3][:, 0:T], const("blk"), sq[t % 2], start=True, stop=True).then_inc(summed, 1)

            def rows(t):
                src = qkT[:, t, :] if t < 2 * H else vT[t % 2]
                if t < 2 * H:
                    pe.wait_ge(qk_ready, t + 1)
                else:
                    pe.wait_ge(v_copied, t - 2 * H + 1)
                if t >= 1:
                    pe.wait_ge(rows_out, t)
                if t >= H:
                    for i in range(2):
                        pe.transpose(bank[4][:, i * P:i * P + P], src[:, i * P:i * P + P], ident)
                pe.transpose(bank[4][0:NB, 2 * P:3 * P], src[:, SEQ:T], ident).then_inc(rows_T, 1)

            pe.wait_ge(h_ready, KT)
            for n in range(BCX):
                tile(n)
                if 1 <= n <= 2 * H:
                    half_sums(n - 1)
                if n >= 2:
                    rows(n - 2)

            def head_sums(h):
                pe.wait_ge(o_squared, h + 1)
                pe.matmul(bank[3][:, 0:SEQ], const("ones"), osq, start=True, stop=True).then_inc(o_summed, 1)

            def head_scores(h):
                pe.wait_ge(qz_ready, h + 1)
                if h >= 1:
                    pe.wait_ge(biased, h)
                for c in range(2):
                    pe.matmul(bank[5][:, c * SEQ:(c + 1) * SEQ], qz[:, c, P:SEQ], qkT[:, H + h, 0:SEQ],
                              start=True, stop=True)
                for c in range(2):
                    m = pe.matmul(bank[6][:, c * P:(c + 1) * P], qz[:, c, 0:P], qkT[:, H + h, 0:P],
                                  start=True, stop=True)
                m.then_inc(scores, 1)

            def head_turn(h):
                pe.wait_ge(diffed, h + 1)
                if h >= 1:
                    pe.wait_ge(diffT_copied, h)
                pe.transpose(bank[7][:, 0:P], diff[:, 2 * P:3 * P], ident)
                pe.transpose(bank[7][:, P:2 * P], diff[:, 0:P], ident)
                pe.transpose(bank[7][:, 2 * P:3 * P], diff[:, P:2 * P], ident).then_inc(diff_T, 1)

            def head_pv(h):
                pe.wait_ge(diffT_copied, h + 1)
                if h >= 1:
                    pe.wait_ge(o_ready, h)
                pe.matmul(bank[4][:, 0:SEQ], vrow[:, 0, h * HD:(h + 1) * HD], diffT[:, 0:SEQ], start=True, stop=False)
                pe.matmul(bank[4][:, P:SEQ], vrow[:, 1, h * HD:(h + 1) * HD], diffT[:, SEQ:SEQ + P],
                          start=False, stop=True).then_inc(pv, 1)

            for i in range(CT):
                tile(BCX + 3 * i)
                if i == 0:
                    rows(3 * H - 2)
                else:
                    head_sums(i - 1)
                if i == 0:
                    rows(3 * H - 1)
                    pe.wait_ge(v_rows, H)
                head_scores(i)
                tile(BCX + 3 * i + 1)
                head_turn(i)
                tile(BCX + 3 * i + 2)
                head_pv(i)
            head_sums(H - 1)

            pe.wait_ge(page_sum, NPAGES)
            pe.wait_ge(biased, H)
            for g in range(NPG):
                pe.transpose(bank[5][:, g * PAGE:(g + 1) * PAGE],
                             keysc[:, g, :, :, :].rearrange("p c h b -> p (c h b)"), ident)
            pe.wait_ge(self_ready, 1)
            pe.wait_ge(diffT_copied, H)
            pe.matmul(bank[7][:, 0:1], selfqk, const("ones")[:, 0:1], start=True, stop=True).then_inc(s_T, 1)
            pe.wait_ge(s_probs, 1)
            for g in range(NPG):
                pe.matmul(bank[6][:, g * H * NB:(g + 1) * H * NB], rowsc[:, g * PAGE:(g + 1) * PAGE], const("sel"),
                          start=True, stop=True)
            pe.matmul(bank[6][:, 2 * H * NB:3 * H * NB], const("ones"), selfsel, start=True, stop=True).then_inc(s_pair, 1)
            pe.wait_ge(s_pair_copied, 1)
            for u in range(4):
                arrived(pe, ("VP", u))
                for b in range(2 * u, 2 * u + 2):
                    for h in range(H):
                        for g in range(NPG):
                            page = ((b % 2) * NPG + g) * ATT
                            m = pe.matmul(bank[7][:, h * NB + b:h * NB + b + 1],
                                          ring[:, front_at[("VP", u)][0], page + h * HD:page + (h + 1) * HD],
                                          pairw[:, g * H * NB + h * NB + b:g * H * NB + h * NB + b + 1],
                                          start=g == 0, stop=g == NPG - 1)
                m.then_inc(s_pv, 1)
            pe.wait_ge(o_squared, H + 1)
            pe.wait_ge(o_rooted, H)
            pe.matmul(bank[3][:, 0:H * NB], const("ones"), osq[:, 0:H * NB], start=True, stop=True).then_inc(o_summed, 1)

            pe.wait_ge(stash_ready, 1)
            pe.transpose(bank[5][0:(2 + NB) * CT, 0:P], stash, ident).then_inc(stash_T, 1)

            def y_turn(j):
                pe.wait_ge(y_copied, j + 1)
                b = bank[3 + j % 2]
                if j >= 2:
                    pe.wait_ge(y_added, j - 1)
                if j == 0:
                    pe.wait_ge(o_rooted, H + 1)
                if j == 1:
                    pe.wait_ge(o_ready, H)
                for t in range(2):
                    pe.transpose(b[:, t * P:(t + 1) * P], yT[j % 2][:, t * P:(t + 1) * P], ident)
                pe.transpose(b[0:NB, 2 * P:3 * P], yT[j % 2][:, SEQ:T], ident).then_inc(y_T, 1)

            for j in range(KT):
                tile(TILE_AT[("W", j)])
                if j >= 1:
                    y_turn(j - 1)
            y_turn(KT - 1)

            pe.wait_ge(h2_rows, TT)
            pe.wait_ge(wr_in, 64)
            pe.wait_ge(y_added, KT)
            pe.wait_ge(stash_out, 1)
            for k in range(KT + 2):
                if k < KT:
                    if k >= 3:
                        pe.wait_ge(h2_ready, k - 2)
                    for t in range(TT):
                        m = pe.transpose(bank[k % 3][:, P * t:P * t + P], h2[:, t, k::KT], ident)
                    m.then_inc(h2_T, 1)
                if k >= 2:
                    kk = k - 2
                    pe.wait_ge(h2_ready, kk + 1)
                    for t in range(TT):
                        n = P if t < 2 else NB
                        pe.matmul(bank[5 + t][0:n, 0:GROUPS], h2T[kk % 3][:, t * P:t * P + n], wrg[:, kk, :],
                                  start=kk == 0, stop=kk == KT - 1, skip_group_check=True)
                        m = pe.matmul(bank[5 + t][0:n, GROUPS:GROUPS + NE], h2T[kk % 3][:, t * P:t * P + n], wre[:, kk, :],
                                      start=False, stop=kk == KT - 1, skip_group_check=True)
            m.then_inc(router, 1)
            pe.wait_ge(assigned, 1)
            pe.wait_ge(late_in, 16)
            for t in range(TT + 1):
                for s in range(min(t, TT - 1) + 1):
                    m = pe.matmul(bank[3][:, t * NE:(t + 1) * NE], late("tri") if s == t else const("ones"), both[:, s, :],
                                  start=s == 0, stop=s == min(t, TT - 1))
            m.then_inc(ranked, 1)

            pe.wait_ge(routed, 1)
            npass = pe.value_load(npass_sb[0:1, 0:1], min_val=1, max_val=MAXPASS)
            with pe.Fori(0, npass) as r:
                with pe.Fori(0, NG) as g:
                    it = r * NG + g

                    pe.wait_ge(sel_ready, it + 1)
                    for q in range(4):
                        if q >= 2:
                            pe.wait_ge(xe_ready, it * 4 + (q - 1))
                        for k in range(4 * q, 4 * q + 4):
                            for t in range(TT):
                                m = pe.matmul(bank[4 + q % 2][:, (k % 4) * P:(k % 4 + 1) * P], h2[:, t, k::KT], sel[:, t, :],
                                              start=t == 0, stop=t == TT - 1)
                        m.then_inc(gathered, 1)
                    pe.wait_ge(gate_ready, it + 1)
                    for t in range(TT):
                        m = pe.transpose(bank[3][:, t * P:(t + 1) * P], gate[:, t, :], ident)
                    m.then_inc(gate_T, 1)
                    pe.wait_ge(xe_ready, it * 4 + 4)
                    pe.wait_ge(gateT_copied, it + 1)

                    for j in range(EG):
                        e = it * EG + j

                        def weights(i):
                            m = j * UPE + i
                            s = slot_of(NFRONT + m)
                            before = sum(slot_of(NFRONT + x) == s for x in range(m + 1))
                            pe.wait_ge(slot_full[s], it * (16 * UPG // SLOTS) + (front_total[s] + 16 * before))
                            return ring[:, s, :]

                        for half, b in ((0, 0), (2, 1)):
                            for i in range(2):
                                w = weights(half + i).rearrange("p (k f) -> p k f", f=F)
                                for k in range(8):
                                    c = k % 4
                                    m = pe.matmul(bank[b][c * C:(c + 1) * C, :], xeT[:, 8 * i + k, j * C:(j + 1) * C], w[:, k, :],
                                                  start=i == 0 and k < 4, stop=i == 1 and k >= 4, skip_group_check=True)
                                if i == 0:
                                    m.then_inc(unit_used, 1)
                            m.then_inc(g_done if b == 0 else u_done, 1)
                        for x, (src, copied) in enumerate(((g_sb, g_copied), (u_sb, u_copied))):
                            pe.wait_ge(copied, e + 1)
                            for c in range(FC):
                                m = pe.matmul(bank[3][:, (x * FC + c) * C:(x * FC + c + 1) * C], src[:, c::FC], const("fold"),
                                              start=True, stop=True)
                        m.then_inc(folded, 1)
                        pe.wait_ge(act_ready, e + 1)
                        if j >= 1:
                            pe.wait_ge(ye_act, (it * EG + j) * 2)
                            pe.wait_ge(ye_dve, (it * EG + j) * 2)
                        for i in range(2):
                            w = weights(4 + i).rearrange("p (c n d) -> p c n d", c=2, n=4)
                            for c in range(2):
                                for n in range(4):
                                    m = pe.matmul(bank[2][n * C:(n + 1) * C, :], actT[:, 2 * i + c, :], w[:, c, n, :],
                                                  start=i == 0 and c == 0, stop=i == 1 and c == 1, skip_group_check=True)
                            if i == 0:
                                m.then_inc(unit_used, 1)
                        m.then_inc(down_done, 1)

                    pe.wait_ge(ye_act, (it + 1) * EG * 2)
                    pe.wait_ge(ye_dve, (it + 1) * EG * 2)
                    for t in range(TT):
                        for n in range(4):
                            m = t * 4 + n
                            pe.wait_ge(mix_added, it * (4 * TT) + (m + 1))
                            pe.matmul(bank[6 + m % 2][:, :], gateT[:, t, :], ye[:, n * 512:(n + 1) * 512],
                                      start=True, stop=True).then_inc(mixed, 1)

        @block.scalar
        def _(act):
            A = nc.scalar.activation
            act.dma_start(consts[:, :], ins["consts"]).then_inc(consts_in, 16)
            n_vecs = [0]

            def vec(dst, src):
                act.dma_start(dst, src).then_inc(vecs_in, 16)
                n_vecs[0] += 1

            vec(gmix, ins["norm_mix"].rearrange("l (p k) -> (l p) k", k=KT))
            vec(gffn, ins["norm_ffn"].rearrange("l (p k) -> (l p) k", k=KT))
            for c in range(2):
                vec(gqk[c * HALF:(c + 1) * HALF, 0:1], ins["g_q"].rearrange("l (d o) -> (l d) o", o=1))
                vec(gqk[c * HALF:(c + 1) * HALF, 1:2], ins["g_k"].rearrange("l (d o) -> (l d) o", o=1))
            vec(gsub[:, 0:1], ins["g_sub"].rearrange("l (d o) -> (l d) o", o=1))
            for i, name in enumerate(("lam_q1", "lam_k1", "lam_q2", "lam_k2")):
                vec(lamraw[:, i * HALF:(i + 1) * HALF], ins[name].partition_broadcast(P).rearrange("p l d -> p (l d)"))
            vec(rawrows[0:3 * CT, 0:P], ins["conv_w"].rearrange("l j (i p) -> (l j i) p", p=P))
            vec(rawrows[:, P:2 * P], ins["state_conv"].rearrange("l b j (i p) -> (l b j i) p", p=P))
            assert n_vecs[0] == VECS

            act.wait_ge(x_in[0], 16)
            A(sqjunk, xa[:, 0, :], ACT.Square, accum_out=ssum[:, 0:1]).then_inc(sums1, 1)
            act.wait_ge(x_in[2], 16)
            act.wait_ge(sums1, 1)
            A(sqjunk, xa[:, 2, :], ACT.Square, accum_out=ssum[:, 2:3]).then_inc(sums1, 1)
            act.wait_ge(consts_in, 16)
            act.wait_ge(sums1, 2)
            act.wait_ge(sums1_dve, 1)
            A(srstd[:, 0:TT], ssum[:, 0:TT], ACT.Sqrt, bias=const("eps"), scale=1.0 / D).then_inc(sqrt1, 1)
            act.wait_ge(act_step, 1)
            A(lamv[:, 0:2], lamv[:, 0:2], ACT.Exp).then_inc(act_step, 1)
            act.wait_ge(raw_T, 1)
            A(convwT, bank[7][:, 0:3 * CT], ACT.Copy)
            A(prevT, bank[7][:, P:2 * P], ACT.Copy).then_inc(raw_copied, 1)

            n_stored = [0, 0]

            def square(t):
                act.wait_ge(tile_done, t + 1)
                if t >= 2:
                    act.wait_ge(summed, t - 1)
                A(sq[t % 2], bank[t % 3][:, 0:T], ACT.Square).then_inc(squared, 1)

            def root(t):
                act.wait_ge(summed, t + 1)
                if t >= 2:
                    act.wait_ge(qk_ready, t - 1)
                A(rstd[t % 2], bank[3][:, 0:T], ACT.Sqrt, bias=const("eps")).then_inc(rooted, 1)

            def copy_v(h):
                t = 2 * H + h
                act.wait_ge(tile_done, t + 1)
                if h >= 2:
                    act.wait_ge(rows_T, t - 1)
                A(vT[t % 2], bank[t % 3][:, 0:T], ACT.Copy)
                A(vTs[:, h * NB:(h + 1) * NB], bank[t % 3][:, SEQ:T], ACT.Copy).then_inc(v_copied, 1)

            def rows_outgoing(t):
                stage, s = kvstage[t % 2], stored[t % 2]
                cols = slice((t % H) * HD, (t % H + 1) * HD)
                act.wait_ge(rows_T, t + 1)
                if t >= 2:
                    act.wait_ge(s, n_stored[t % 2])
                if t >= 2 * H:
                    A(vrow[:, :, cols], bank[4][:, 0:2 * P].rearrange("p (t c) -> p t c", t=2), ACT.Copy).then_inc(v_rows, 1)
                elif t >= H:
                    A(stage[:, 0:2 * P], bank[4][:, 0:2 * P], ACT.Copy)
                A(stage[0:NB, 2 * P:3 * P], bank[4][0:NB, 2 * P:3 * P], ACT.Copy).then_inc(rows_out, 1)
                act.wait_ge(rows_out, t + 1)
                if t < H:
                    act.dma_start(qrows_dram[:, cols], stage[0:NB, 2 * P:3 * P]).then_inc(s, 16)
                    n_stored[t % 2] += 16
                    return
                name = "k" if t < 2 * H else "v"
                src = stage[:, 0:2 * P].rearrange("p (t c) -> p t c", t=2) if t < 2 * H else vrow[:, :, cols]
                if t >= 2 * H:
                    act.wait_ge(v_rows, t - 2 * H + 1)
                act.dma_start(outs[name + "_prompt"].rearrange("l o (t p) h d -> p (l o t) (h d)", p=P)[:, :, cols],
                              src).then_inc(s, 16)
                act.dma_start(outs[name + "_sample"].rearrange("l b o h d -> (l b o) (h d)")[:, cols],
                              stage[0:NB, 2 * P:3 * P]).then_inc(s, 16)
                n_stored[t % 2] += 32

            for n in range(BCX + 2):
                if n < 2 * H:
                    square(n)
                elif n < BCX:
                    copy_v(n - 2 * H)
                if 1 <= n <= 2 * H:
                    root(n - 1)
                if n == BCX:
                    act.wait_ge(tile_done, BCX + 1)
                    A(ctmp, bank[BCX % 3][:, 0:T], ACT.Copy).then_inc(c_copied, 1)
                if n >= 2:
                    rows_outgoing(n - 2)
            assert tuple(n_stored) == STORED

            def head_root(h, cols=SEQ):
                act.wait_ge(o_summed, h + 1)
                if h >= 1:
                    act.wait_ge(o_ready, h)
                A(ord_[:, 0:cols], bank[3][:, 0:cols], ACT.Sqrt, bias=const("eps"), scale=1.0 / HD).then_inc(o_rooted, 1)

            for i in range(CT):
                if i >= 1:
                    act.wait_ge(tile_done, BCX + 3 * i + 1)
                    act.wait_ge(u_ready, i)
                    A(ctmp, bank[(BCX + 3 * i) % 3][:, 0:T], ACT.Copy).then_inc(c_copied, 1)
                    head_root(i - 1)
                act.wait_ge(biased, i + 1)
                for x in range(4):
                    a, b = ((0, 256), (256, 512), (512, 640), (640, 768))[x]
                    A(prob[:, a:b], prob[:, a:b], ACT.Exp, bias=nmax[:, x:x + 1], accum_out=esum[:, x:x + 1]).then_inc(exped, 1)
                act.wait_ge(diff_T, i + 1)
                A(diffT, bank[7][:, 0:3 * P], ACT.Copy).then_inc(diffT_copied, 1)
                act.wait_ge(pv, i + 1)
                A(osq, bank[4][:, 0:SEQ], ACT.Square).then_inc(o_squared, 1)
            head_root(H - 1)

            act.wait_ge(s_biased, 1)
            A(rowsc, rowsc, ACT.Exp, bias=nmax[:, 0:1], accum_out=esum[:, 0:1]).then_inc(s_exped, 1)
            act.wait_ge(s_pv, 5)
            A(osq[:, 0:H * NB], conv[:, 0:H * NB], ACT.Square).then_inc(o_squared, 1)
            head_root(H, H * NB)
            act.wait_ge(stash_T, 1)
            A(junk_act[0:(2 + NB) * CT, 0:P], bank[5][0:(2 + NB) * CT, 0:P], ACT.Copy).then_inc(stash_out, 1)
            act.wait_ge(stash_out, 1)
            act.dma_start(outs["conv_prompt"].rearrange("l o r (i p) -> (l o r i) p", p=P), junk_act[0:2 * CT, 0:P]
                          ).then_inc(stored[0], 16)
            for b in range(NB):
                act.dma_start(outs["conv_sample"].rearrange("l b r (i p) -> (l b) r i p", p=P)[b, 1],
                              junk_act[(2 + b) * CT:(3 + b) * CT, 0:P]).then_inc(stored[1], 16)

            for j in range(KT):
                n = TILE_AT[("W", j)]
                act.wait_ge(tile_done, n + 1)
                if j >= 2:
                    act.wait_ge(y_T, j - 1)
                A(yT[j % 2], bank[n % 3][:, 0:T], ACT.Copy).then_inc(y_copied, 1)
            act.dma_start(wrg, ins["w_router_group"].rearrange("l (p k) e -> (l p) k e", k=KT)).then_inc(wr_in, 16)
            act.dma_start(wre, ins["w_router_expert"].rearrange("l (p k) e -> (l p) k e", k=KT)).then_inc(wr_in, 16)
            act.dma_start(rbias[:, 0:GROUPS], ins["b_router_group"].partition_broadcast(P).rearrange("p l e -> p (l e)")
                          ).then_inc(wr_in, 16)
            act.dma_start(rbias[:, GROUPS:], ins["b_router_expert"].partition_broadcast(P).rearrange("p l e -> p (l e)")
                          ).then_inc(wr_in, 16)
            act.wait_ge(stored[0], STORED[0] + 16)
            act.wait_ge(stored[1], STORED[1] + 16 * NB)
            act.wait_ge(y_added, KT)
            A(junk_act, xa[:, 0, :], ACT.Square, accum_out=ssum[:, 0:1]).then_inc(sums2, 1)
            act.wait_ge(sums2, 1)
            A(junk_act, xa[:, 2, :], ACT.Square, accum_out=ssum[:, 2:3]).then_inc(sums2, 1)
            act.wait_ge(sums2, 2)
            act.wait_ge(sums2_dve, 1)
            A(srstd[:, 0:TT], ssum[:, 0:TT], ACT.Sqrt, bias=const("eps"), scale=1.0 / D).then_inc(sqrt2, 1)
            act.wait_ge(gex_ready, 1)
            A(gex, gex, ACT.Exp).then_inc(gexed, 1)
            A(ew, ew, ACT.Exp).then_inc(gexed, 1)

            act.wait_ge(routed, 1)
            npass = act.value_load(npass_sb[0:1, 0:1], min_val=1, max_val=MAXPASS)
            with act.Fori(0, npass) as r:
                with act.Fori(0, NG) as g:
                    it = r * NG + g
                    act.wait_ge(gate_T, it + 1)
                    A(gateT, bank[3][:, 0:TT * P].rearrange("p (t s) -> p t s", t=TT), ACT.Copy).then_inc(gateT_copied, 1)
                    for j in range(EG):
                        act.wait_ge(g_done, it * EG + (j + 1))
                        A(g_sb, bank[0][:, :], ACT.Copy).then_inc(g_copied, 1)
                        act.wait_ge(folded, it * EG + (j + 1))
                        A(actT, bank[3][:, 0:P].rearrange("p (c s) -> p c s", c=FC), ACT.Silu).then_inc(silu_done, 1)
                        act.wait_ge(down_done, it * EG + (j + 1))
                        for n in range(2):
                            A(ye[j * C:(j + 1) * C, n * 512:(n + 1) * 512], bank[2][n * C:(n + 1) * C, :], ACT.Copy
                              ).then_inc(ye_act, 1)

        @block.vector
        def _(dve):
            V = nc.vector
            st = Steps(dve, dve_step)
            dve.wait_ge(vecs_in, VECS * 16)
            for i in range(2):
                st.do(V.tensor_tensor_reduce(lamprod, lamraw[:, 2 * i * HALF:(2 * i + 1) * HALF],
                                             lamraw[:, (2 * i + 1) * HALF:(2 * i + 2) * HALF], 1.0, 0.0,
                                             ALU.mult, ALU.add, lamv[:, i:i + 1]))
            V.tensor_scalar(gqk[:, 0:1], gqk[:, 0:1], HALF ** -0.5, None, ALU.mult).then_inc(act_step, 1)
            st.add(V.tensor_scalar(gsub[:, 1:2], gsub[:, 0:1], 1.0 - LAM_INIT, None, ALU.mult))

            dve.wait_ge(x_in[1], 16)
            V.tensor_tensor_reduce(sqjunk2, xa[:, 1, :], xa[:, 1, :], 1.0, 0.0, ALU.mult, ALU.add, ssum[:, 1:2]
                                   ).then_inc(sums1_dve, 1)
            dve.wait_ge(act_step, 2)
            st.do(V.tensor_tensor(lamv[:, 2:3], lamv[:, 0:1], lamv[:, 1:2], ALU.subtract))
            st.do(V.tensor_scalar(lamv[:, 2:3], lamv[:, 2:3], LAM_INIT, None, ALU.add))
            st.do(V.tensor_scalar(lamv[:, 3:4], lamv[:, 2:3], -1.0, None, ALU.mult))
            dve.wait_ge(consts_in, 16)
            st.do(V.tensor_tensor(lamv[:, 0:1], lamv[:, 2:3], const("neg_c1"), ALU.mult))
            st.do(V.tensor_tensor(lamv[:, 0:1], lamv[:, 0:1], const("c0"), ALU.add))
            dve.wait_ge(sqrt1, 1)
            st.do(V.reciprocal(srstd[:, 0:TT], srstd[:, 0:TT]))
            for t in range(TT):
                V.tensor_scalar(xa[:, t, :], xa[:, t, :], srstd[:, t:t + 1], None, ALU.mult).then_inc(h_rows, 1)
            for k in range(KT):
                dve.wait_ge(h_T, k + 1)
                V.tensor_scalar(hT[:, k, :], bank[3 + k % 4][:, 0:T], gmix[:, k:k + 1], None, ALU.mult).then_inc(h_ready, 1)

            for t in range(2 * H):
                r = rstd[t % 2]
                dve.wait_ge(rooted, t + 1)
                st.do(V.reciprocal(r, r))
                V.scalar_tensor_tensor(qkT[:, t, :], bank[t % 3][:, 0:T], gqk[:, t // H:t // H + 1], r,
                                       ALU.mult, ALU.mult).then_inc(qk_ready, 1)

            st.add(V.memset(upad[:, 0:2], 0.0))
            dve.wait_ge(raw_copied, 1)
            prev = prevT.rearrange("p (b j i) -> p b j i", b=NB, j=2)
            out = stash.rearrange("p (r i) -> p r i", i=CT)

            def page(j):
                b, g = divmod(j, NPG)
                dve.wait_ge(page_mul, j + 1)
                s, _ = front_at[("KP", j // PPU)]
                src = ring[:, s, (j % PPU) * ATT:(j % PPU + 1) * ATT].rearrange("p (h c d) -> p h c d", h=H, c=2)
                V.tensor_reduce(keysc[:, g, :, :, b].rearrange("p c h -> p h c"), src, AX.X, ALU.add).then_inc(page_sum, 1)

            def head_out(h):
                dve.wait_ge(o_rooted, h + 1)
                st.do(V.reciprocal(ord_, ord_))
                V.scalar_tensor_tensor(cat[:, h, 0:SEQ], bank[4][:, 0:SEQ], gsub[:, 1:2], ord_, ALU.mult, ALU.mult
                                       ).then_inc(o_ready, 1)

            for i in range(CT):
                dve.wait_ge(scores, i + 1)
                if i == 0:
                    for x in range(2):
                        dve.wait_ge(stored[x], STORED[x])
                else:
                    dve.wait_ge(diff_T, i)
                for c in range(2):
                    st.add(V.scalar_tensor_tensor(prob[:, c * SEQ:(c + 1) * SEQ], const("dist"), SLOPES[i],
                                                  bank[5][:, c * SEQ:(c + 1) * SEQ], ALU.mult, ALU.add))
                for c in range(2):
                    st.add(V.scalar_tensor_tensor(prob[:, 512 + c * P:512 + (c + 1) * P], const("dist")[:, P:2 * P], SLOPES[i],
                                                  bank[6][:, c * P:(c + 1) * P], ALU.mult, ALU.add))
                st.wait()
                st.do(V.tensor_reduce(nmax[:, 0:2], prob[:, 0:512].rearrange("p (c k) -> p c k", c=2), AX.X, ALU.max, negate=True))
                V.tensor_reduce(nmax[:, 2:4], prob[:, 512:768].rearrange("p (c k) -> p c k", c=2), AX.X, ALU.max, negate=True
                                ).then_inc(biased, 1)
                if i >= 1:
                    head_out(i - 1)
                for j in range(PAGES_BY[i], PAGES_BY[i + 1]):
                    page(j)
                dve.wait_ge(exped, 4 * (i + 1))
                st.do(V.reciprocal(rsum, esum))
                st.do(V.tensor_scalar(rsum[:, 1:2], rsum[:, 1:2], lamv[:, 3:4], None, ALU.mult))
                st.do(V.tensor_scalar(rsum[:, 3:4], rsum[:, 3:4], lamv[:, 3:4], None, ALU.mult))
                st.add(V.tensor_scalar(diff[:, 0:256], prob[:, 0:256], rsum[:, 0:1], None, ALU.mult))
                st.do(V.tensor_scalar(diff[:, 256:384], prob[:, 512:640], rsum[:, 2:3], None, ALU.mult))
                st.add(V.scalar_tensor_tensor(diff[:, 0:256], prob[:, 256:512], rsum[:, 1:2], diff[:, 0:256], ALU.mult, ALU.add))
                V.scalar_tensor_tensor(diff[:, 256:384], prob[:, 640:768], rsum[:, 3:4], diff[:, 256:384], ALU.mult, ALU.add
                                       ).then_inc(diffed, 1)
                n = BCX + 3 * i
                dve.wait_ge(tile_done, n + 2)
                dve.wait_ge(c_copied, i + 1)
                V.tensor_tensor(upad[:, 2:T + 2], ctmp, bank[(n + 1) % 3][:, 0:T], ALU.mult).then_inc(u_ready, 1)
                dve.wait_ge(u_ready, i + 1)
                tap = [convwT[:, j * CT + i:j * CT + i + 1] for j in range(3)]
                st.add(V.tensor_scalar(conv[:, 0:SEQ], upad[:, 0:SEQ], tap[0], None, ALU.mult))
                st.do(V.tensor_scalar(conv[:, SEQ:T], prev[:, :, 0, i], tap[0], None, ALU.mult))
                st.add(V.scalar_tensor_tensor(conv[:, 0:SEQ], upad[:, 1:SEQ + 1], tap[1], conv[:, 0:SEQ], ALU.mult, ALU.add))
                st.do(V.scalar_tensor_tensor(conv[:, SEQ:T], prev[:, :, 1, i], tap[1], conv[:, SEQ:T], ALU.mult, ALU.add))
                st.do(V.scalar_tensor_tensor(conv, upad[:, 2:T + 2], tap[2], conv, ALU.mult, ALU.add))
                st.add(V.tensor_copy(out[:, :, i], upad[:, SEQ:T + 2]))
                dve.wait_ge(tile_done, n + 3)
                V.tensor_tensor(cat[:, CT + i, :], conv, bank[(n + 2) % 3][:, 0:T], ALU.mult).then_inc(conv_ready, 1)
            dve.wait_ge(conv_ready, CT)
            V.tensor_copy(selfsel[:, 0:1], lamv[:, 0:1]).then_inc(stash_ready, 1)

            st.do(V.memset(selfqk, 0.0))
            for c in range(2):
                q = slice(c * HALF, (c + 1) * HALF)
                V.tensor_tensor(selfqk[q, c * H * NB:(c + 1) * H * NB].rearrange("p (h b) -> p h b", h=H),
                                qkT[q, 0:H, SEQ:T], qkT[q, H:2 * H, SEQ:T], ALU.mult).then_inc(*((self_ready, 1) if c else (dve_step, 1)))
                if not c:
                    st.n += 1
            head_out(H - 1)
            dve.wait_ge(s_T, 1)
            st.add(V.scalar_tensor_tensor(rowsc[:, 0:PAST], const("kpos"), const("slope"), bank[5][:, 0:PAST], ALU.mult, ALU.add))
            st.do(V.tensor_copy(rowsc[:, PAST:PAST + 1], bank[7][:, 0:1]))
            V.tensor_reduce(nmax[:, 0:1], rowsc, AX.X, ALU.max, negate=True).then_inc(s_biased, 1)
            dve.wait_ge(s_exped, 1)
            st.do(V.reciprocal(rsum[:, 0:1], esum[:, 0:1]))
            st.do(V.tensor_tensor(rsum[:, 0:1], rsum[:, 0:1], lamv[:, 0:1], ALU.mult))
            st.do(V.tensor_scalar(rowsc, rowsc, rsum[:, 0:1], None, ALU.mult))
            V.tensor_scalar(selfsel, const("sel"), rowsc[:, PAST:PAST + 1], None, ALU.mult).then_inc(s_probs, 1)
            dve.wait_ge(s_pair, 1)
            st.add(V.tensor_tensor(conv[:, 0:H * NB], bank[6][:, 2 * H * NB:3 * H * NB], vTs, ALU.mult))
            V.tensor_copy(pairw, bank[6][:, 0:2 * H * NB]).then_inc(s_pair_copied, 1)
            dve.wait_ge(s_pv, 4)
            st.wait()
            V.tensor_tensor(conv[:, 0:H * NB], conv[:, 0:H * NB], bank[7][:, 0:H * NB], ALU.add).then_inc(s_pv, 1)
            dve.wait_ge(s_pv, 5)
            dve.wait_ge(o_rooted, H + 1)
            st.do(V.reciprocal(ord_[:, 0:H * NB], ord_[:, 0:H * NB]))
            V.scalar_tensor_tensor(cat[:, 0:H, SEQ:T], conv[:, 0:H * NB].rearrange("p (h b) -> p h b", h=H), gsub[:, 1:2],
                                   ord_[:, 0:H * NB].rearrange("p (h b) -> p h b", h=H), ALU.mult, ALU.mult).then_inc(o_ready, 1)

            dve.wait_ge(x_again, 48)
            for j in range(KT):
                dve.wait_ge(y_T, j + 1)
                b = bank[3 + j % 2]
                cols = slice(j * P, (j + 1) * P)
                st.add(V.tensor_tensor(xa[:, 0:2, cols], xa[:, 0:2, cols], b[:, 0:2 * P].rearrange("p (t c) -> p t c", t=2), ALU.add))
                V.tensor_tensor(xa[0:NB, 2, cols], xa[0:NB, 2, cols], b[0:NB, 2 * P:3 * P], ALU.add).then_inc(y_added, 1)
            dve.wait_ge(y_added, KT)
            st.wait()
            V.tensor_tensor_reduce(junk_dve, xa[:, 1, :], xa[:, 1, :], 1.0, 0.0, ALU.mult, ALU.add, ssum[:, 1:2]
                                   ).then_inc(sums2_dve, 1)
            dve.wait_ge(sqrt2, 1)
            st.do(V.reciprocal(srstd[:, 0:TT], srstd[:, 0:TT]))
            for t in range(TT):
                V.tensor_scalar(h2[:, t, :], xa[:, t, :], srstd[:, t:t + 1], None, ALU.mult).then_inc(h2_rows, 1)
            for k in range(KT):
                dve.wait_ge(h2_T, k + 1)
                V.tensor_scalar(h2T[k % 3], bank[k % 3][:, 0:T], gffn[:, k:k + 1], None, ALU.mult).then_inc(h2_ready, 1)

            def grouped(x):
                return x.rearrange("p t (g e) -> p t g e", g=GROUPS)

            def wide(x, n):
                return x.to_broadcast([P, TT, n])

            def rows_of(x, n):
                return x.unsqueeze(1).to_broadcast([P, TT, n])

            dve.wait_ge(late_in, 16)
            st.do(V.memset(logits, 0.0))
            dve.wait_ge(router, 1)
            for t in range(TT):
                n = P if t < 2 else NB
                st.add(V.tensor_tensor(logits[0:n, t, :], bank[5 + t][0:n, 0:GROUPS + NE], rbias[0:n, :], ALU.add))
            st.wait()
            lg, le = logits[:, :, 0:GROUPS], logits[:, :, GROUPS:]

            def first_max(x, best, onehot, at, down, n):
                st.do(V.tensor_reduce(best, x, AX.X, ALU.max))
                st.do(V.tensor_tensor(onehot, x, wide(best, n), ALU.is_equal))
                st.do(V.tensor_tensor(onehot, onehot, rows_of(down, n), ALU.mult))
                st.do(V.tensor_reduce(at, onehot, AX.X, ALU.max))
                st.do(V.tensor_tensor(onehot, wide(at, n), rows_of(down, n), ALU.is_equal))

            first_max(lg, gm, goh, gi, late("down4"), GROUPS)
            st.do(V.tensor_tensor(gex, lg, wide(gm, GROUPS), ALU.subtract))
            st.do(V.tensor_scalar(geneg, goh, -1.0, -FAR, ALU.add, ALU.mult))
            for t in range(TT):
                st.add(V.tensor_tensor(lem[:, t, :].rearrange("p (g e) -> p g e", g=GROUPS),
                                       le[:, t, :].rearrange("p (g e) -> p g e", g=GROUPS),
                                       geneg[:, t, :].unsqueeze(2).to_broadcast([P, GROUPS, EPG]), ALU.add))
            st.wait()
            first_max(lem, m1, oh1, i1, late("down32"), NE)
            st.do(V.tensor_scalar(work, oh1, -3e38, None, ALU.mult))
            st.do(V.tensor_tensor(work, lem, work, ALU.add))
            first_max(work, m2, oh2, i2, late("down32"), NE)
            V.tensor_tensor(ew, m2, m1, ALU.subtract).then_inc(gex_ready, 1)
            st.do(V.tensor_tensor(both, oh1, oh2, ALU.add))
            V.tensor_tensor(both, both, const("valid").unsqueeze(2).to_broadcast([P, TT, NE]), ALU.mult).then_inc(assigned, 1)
            dve.wait_ge(gexed, 2)
            st.do(V.tensor_reduce(gs, gex, AX.X, ALU.add))
            st.do(V.tensor_scalar(wn, ew, 1.0, None, ALU.add))
            st.do(V.tensor_tensor(wn, wn, gs, ALU.mult))
            st.do(V.reciprocal(w1.unsqueeze(2), wn))
            st.do(V.tensor_tensor(w2.unsqueeze(2), w1.unsqueeze(2), ew, ALU.mult))
            dve.wait_ge(ranked, 1)
            st.do(V.tensor_copy(rank, bank[3][:, 0:TT * NE].rearrange("p (t e) -> p t e", t=TT)))
            st.do(V.tensor_copy(tot, bank[3][:, TT * NE:(TT + 1) * NE]))
            for oh, rk, pos in ((oh1, rk1, pos1), (oh2, rk2, pos2)):
                st.do(V.tensor_tensor(work, oh, rank, ALU.mult))
                st.do(V.tensor_reduce(rk, work, AX.X, ALU.add))
                st.do(V.tensor_tensor(work, oh, rows_of(late("base"), NE), ALU.mult))
                st.do(V.tensor_reduce(ov, work, AX.X, ALU.add))
                st.do(V.tensor_tensor(rk, rk, ov, ALU.subtract))
                st.do(V.tensor_tensor(over, rk, ov, ALU.add))
                st.do(V.tensor_tensor(exc, wide(over, MAXPASS), rows_of(const("kth"), MAXPASS), ALU.is_ge))
                st.do(V.tensor_reduce(over, exc, AX.X, ALU.add))
                st.do(V.tensor_scalar(over, over, -1.0, float(PASS_SLOTS - C), ALU.add, ALU.mult))
                st.do(V.tensor_tensor(pos.unsqueeze(2), rk, over, ALU.add))
            st.do(V.tensor_scalar(over, const("valid").unsqueeze(2), -1.0, 1e6, ALU.add, ALU.mult))
            st.add(V.tensor_tensor(pos1.unsqueeze(2), pos1.unsqueeze(2), over, ALU.add))
            st.add(V.tensor_tensor(pos2.unsqueeze(2), pos2.unsqueeze(2), over, ALU.add))
            st.do(V.tensor_reduce(cmax, tot, AX.X, ALU.max))
            st.do(V.tensor_scalar(cwork, const("kth"), cmax, None, ALU.is_lt))
            st.do(V.tensor_reduce(cpass, cwork, AX.X, ALU.add))
            V.memset(esum[:, 0:1], 0.0).then_inc(mix_added, 2)
            V.tensor_copy(npass_sb[0:1, 0:1], cpass[0:1, :]).then_inc(routed, 1)
            dve.wait_ge(routed, 1)

            npass = dve.value_load(npass_sb[0:1, 0:1], min_val=1, max_val=MAXPASS)
            before = st.n
            with dve.Fori(0, npass) as r:
                with dve.Fori(0, NG) as g:
                    it = r * NG + g
                    st.base = it * LOOP_STEPS
                    iota = late("iota")
                    for t in range(TT):
                        st.add(V.tensor_scalar(gateT[:, t, :], iota, pos2[:, t:t + 1], None, ALU.is_equal))
                        st.add(V.tensor_scalar(gate[:, t, :], iota, pos1[:, t:t + 1], w1[:, t:t + 1], ALU.is_equal, ALU.mult))
                    st.wait()
                    for t in range(TT):
                        ins_ = V.scalar_tensor_tensor(sel[:, t, :], iota, pos1[:, t:t + 1], gateT[:, t, :], ALU.is_equal, ALU.add)
                        if t < TT - 1:
                            st.add(ins_)
                        else:
                            ins_.then_inc(sel_ready, 1)
                    for t in range(TT):
                        ins_ = V.scalar_tensor_tensor(gate[:, t, :], gateT[:, t, :], w2[:, t:t + 1], gate[:, t, :], ALU.mult, ALU.add)
                        if t < TT - 1:
                            st.add(ins_)
                        else:
                            ins_.then_inc(gate_ready, 1)
                    st.wait()
                    dve.wait_ge(sel_ready, it + 1)
                    dve.wait_ge(gate_ready, it + 1)
                    st.do(V.tensor_scalar(route[:, 0:2 * TT], route[:, 0:2 * TT], -float(P), None, ALU.add))
                    for q in range(4):
                        dve.wait_ge(gathered, it * 4 + (q + 1))
                        V.tensor_tensor(xeT[:, 4 * q:4 * q + 4, :], bank[4 + q % 2][:, :].rearrange("p (k s) -> p k s", k=4),
                                        gffn[:, 4 * q:4 * q + 4].unsqueeze(2).to_broadcast([P, 4, P]), ALU.mult).then_inc(xe_ready, 1)
                    for j in range(EG):
                        dve.wait_ge(u_done, it * EG + (j + 1))
                        V.tensor_copy(u_sb, bank[1][:, :]).then_inc(u_copied, 1)
                        dve.wait_ge(silu_done, it * EG + (j + 1))
                        V.tensor_tensor(actT, actT, bank[3][:, P:2 * P].rearrange("p (c s) -> p c s", c=FC), ALU.mult
                                        ).then_inc(act_ready, 1)
                        dve.wait_ge(down_done, it * EG + (j + 1))
                        for n in range(2, 4):
                            V.tensor_copy(ye[j * C:(j + 1) * C, n * 512:(n + 1) * 512], bank[2][n * C:(n + 1) * C, :]
                                          ).then_inc(ye_dve, 1)
                    for t in range(TT):
                        n_rows = P if t < 2 else NB
                        for n in range(4):
                            m = t * 4 + n
                            cols = slice(n * 512, (n + 1) * 512)
                            dve.wait_ge(mixed, it * (4 * TT) + (m + 1))
                            V.tensor_tensor(xa[0:n_rows, t, cols], xa[0:n_rows, t, cols], bank[6 + m % 2][0:n_rows, :], ALU.add
                                            ).then_inc(mix_added, 1)
            assert st.n - before == LOOP_STEPS, st.n - before

        @block.gpsimd
        def _(pool):
            G = nc.gpsimd
            G.memset(xa[:, 2, :], 0.0).then_inc(x_clear, 1)
            pool.wait_ge(x_clear, 1)
            xs = ins["x_sample"].rearrange("b o d -> b (o d)")
            pool.dma_start(xa[0:NB, 2, :], xs).then_inc(x_in[2], 16)
            pool.dma_start(outs["conv_sample"][0, :, 0, :], ins["state_conv"][0, :, 1, :]).then_inc(state_stored, 16)

            pool.wait_ge(rows_T, 3 * H)
            G.memset(qz, 0.0).then_inc(qz_zero, 1)
            pool.wait_ge(qz_zero, 1)
            for i in range(CT):
                if i >= 1:
                    pool.wait_ge(scores, i)
                    if PAGES_BY[i]:
                        pool.wait_ge(page_mul, PAGES_BY[i])
                G.tensor_copy(qz[0:HALF, 0, :], qkT[0:HALF, i, 0:SEQ]).then_inc(qz_zero, 1)
                pool.wait_ge(qz_zero, i + 2)
                G.tensor_copy(qz[HALF:P, 1, :], qkT[HALF:P, i, 0:SEQ]).then_inc(qz_ready, 1)
                pool.wait_ge(qz_ready, i + 1)
                for j in range(PAGES_BY[i], PAGES_BY[i + 1]):
                    b = j // NPG
                    if j % PPU == 0:
                        arrived(pool, ("KP", j // PPU))
                    if b % 4 == 0 and j % NPG == 0:
                        arrived(pool, ("QB", b // 4))
                    s, _ = front_at[("KP", j // PPU)]
                    sq_, _ = front_at[("QB", b // 4)]
                    kp = ring[:, s, (j % PPU) * ATT:(j % PPU + 1) * ATT]
                    G.tensor_tensor(kp, kp, ring[:, sq_, (b % 4) * ATT:(b % 4 + 1) * ATT], ALU.mult).then_inc(page_mul, 1)

            pool.wait_ge(o_ready, H + 1)
            G.memset(xa[:, 2, :], 0.0).then_inc(x2_zero, 1)
            pool.wait_ge(x2_zero, 1)
            pool.dma_start(xa[0:NB, 2, :], xs).then_inc(x_again, 16)
            for t in range(2):
                pool.dma_start(xa[:, t, :], ins["x_prompt"].rearrange("o (t p) d -> (o t) p d", p=P)[t]).then_inc(x_again, 16)
            pool.dma_start(consts[:, late0:late0 + 512], ins["late"]).then_inc(late_in, 16)

    return nc


VECS = 13
STORED = (16 * 4 + 32 * 8, 16 * 4 + 32 * 8)
LOOP_STEPS = 2 * TT + 2 * (TT - 1) + 1


def _constants():
    import numpy as np

    c = np.zeros((P, NCONST), np.float32)

    def put(name, x):
        a, b = CONST_AT[name]
        c[:, a:b] = x

    r = np.arange(P)
    put("ident", np.eye(P))
    put("ones", 1.0)
    put("fold", np.tile(np.eye(C), (EG, 1)))
    put("blk", np.kron(np.eye(2), np.ones((HALF, HALF))) / HALF)
    put("sel", np.tile(np.eye(H * NB), (2, 1)))
    back = P + r[:, None] - np.arange(SEQ)[None, :]
    put("dist", np.where(back >= 0, -back, FAR))
    put("kpos", np.arange(PAST)[None, :] - PAST)
    put("slope", np.tile(np.repeat(SLOPES, NB), 2)[:, None])
    put("neg_c1", -(r >= HALF)[:, None].astype(np.float32))
    put("c0", (r < HALF)[:, None])
    put("valid", np.stack([r >= 0, r >= 0, r < NB], 1))
    put("kth", C * np.arange(MAXPASS)[None, :])
    put("eps", EPS)
    late = np.zeros((P, 512), np.float32)

    def put_late(name, x):
        a, b = LATE_AT[name]
        late[:, a:b] = x

    put_late("iota", r[None, :])
    put_late("tri", (r[:, None] < r[None, :]))
    put_late("base", -C * np.arange(NE)[None, :])
    put_late("down32", NE - np.arange(NE)[None, :])
    put_late("down4", GROUPS - np.arange(GROUPS)[None, :])
    return {"consts": c, "late": late}


_OUTS = [("y_prompt", (1, SEQ, D)), ("y_sample", (NB, 1, D)), ("k_prompt", (1, 1, SEQ, H, HD)),
         ("v_prompt", (1, 1, SEQ, H, HD)), ("conv_prompt", (1, 1, 2, CONV)), ("k_sample", (1, NB, 1, H, HD)),
         ("v_sample", (1, NB, 1, H, HD)), ("conv_sample", (1, NB, 2, CONV))]


def kernel(**inputs):
    import numpy as np
    import concourse.bacc as bacc
    from concourse.bass_utils import run_bass_kernel_spmd

    nc = bacc.Bacc("TRN2", target_bir_lowering=False, num_devices=1)
    arrays = {name: np.ascontiguousarray(a) for name, a in {**inputs, **_constants()}.items()}
    ins = {name: nc.dram_tensor(f"in_{name}", a.shape, mybir.dt.from_np(a.dtype), kind="ExternalInput").ap()
           for name, a in arrays.items()}
    outs = {name: nc.dram_tensor(f"out_{name}", shape, F32, kind="ExternalOutput").ap() for name, shape in _OUTS}
    build(nc, ins, outs)
    r = run_bass_kernel_spmd(nc, [{f"in_{name}": a for name, a in arrays.items()}], core_ids=[0])
    return tuple(r.results[0][f"out_{name}"] for name, _ in _OUTS)
```

```python
from contextlib import ExitStack

import concourse.bass as bass
from concourse import mybir

F32 = mybir.dt.float32
I32 = mybir.dt.int32
ALU = mybir.AluOpType
ACT = mybir.ActivationFunctionType
AX = mybir.AxisListType

P = 128
D = 2048
KT = D // P
SEQ = 256
NB = 8
T = SEQ + NB
TT = 3
H = 8
HD = 128
HALF = HD // 2
ATT = H * HD
CONV = D - ATT
CT = CONV // P
PAST = 256
PAGE = 128
NPG = PAST // PAGE
GROUPS = 4
EPG = 8
NE = GROUPS * EPG
F = D // 4
FC = F // P
EPS = 1e-6
LAM_INIT = 0.8 - 0.6
FAR = -1e30

SLOTS = 8
UNIT = 4096
UC = UNIT // KT
TPU = UC // P

EG = 4
C = P // EG
NG = NE // EG
PASS_SLOTS = NE * C
MAXPASS = -(-T // C)
UPE = 6
UPG = UPE * EG
RG = 8
RE = RG + NE

FRONT = ([("q", u) for u in range(4)] + [("k", u) for u in range(4)] + [("v", u) for u in range(4)]
         + [("C", 0), ("X", 0), ("B", 0), ("QB", 0), ("KP", 0), ("KP", 1),
            ("C", 1), ("X", 1), ("B", 1), ("QB", 1), ("KP", 2),
            ("C", 2), ("X", 2), ("B", 2), ("KP", 3),
            ("C", 3), ("X", 3), ("B", 3)]
         + [("VP", u) for u in range(4)] + [("W", 0), ("XT", 0)] + [("W", u) for u in range(1, 8)])
NFRONT = len(FRONT)
COLUMN = {"q": 0, "k": ATT, "v": 2 * ATT, "B": 3 * ATT, "C": 3 * ATT + CONV, "X": 3 * ATT + 2 * CONV}
TILES = ([("q", h) for h in range(H)] + [("k", h) for h in range(H)] + [("v", h) for h in range(H)]
         + [(c, i) for i in range(CT) for c in "CXB"] + [("W", j) for j in range(KT)])
TILE_AT = {t: n for n, t in enumerate(TILES)}
BCX = 3 * H
PAGES_AT = [3, 3, 3, 3, 2, 2, 0, 0]
PAGES_BY = [sum(PAGES_AT[:i]) for i in range(CT + 1)]
NPAGES = NB * NPG
NIN = BCX + 3 * CT
HEAD0 = 2 * H + 2
SAMPLE0 = HEAD0 + 3 * H
PPU = 4

CONSTS = [("ident", P), ("ones", P), ("fold", C), ("blk", P), ("sel", H * NB), ("dist", SEQ), ("kpos", PAST),
          ("slope", 1), ("neg_c1", 1), ("c0", 1), ("valid", TT), ("kth", MAXPASS), ("eps", 1)]
CONST_AT, _n = {}, 0
for _name, _w in CONSTS:
    CONST_AT[_name] = (_n, _n + _w)
    _n += _w
NCONST = _n
LATE = [("iota", P), ("tri", P), ("base", NE), ("pad", 512 - 2 * P - NE)]
LATE_AT, _n = {}, 0
for _name, _w in LATE:
    LATE_AT[_name] = (_n, _n + _w)
    _n += _w
SLOPES = [2.0 ** (-8.0 * (h + 1) / H) for h in range(H)]


class Steps:

    def __init__(self, eng, sem):
        self.eng, self.sem, self.n, self.base = eng, sem, 0, 0

    def add(self, ins):
        ins.then_inc(self.sem, 1)
        self.n += 1

    def wait(self):
        self.eng.wait_ge(self.sem, self.base + self.n)

    def do(self, ins):
        self.add(ins)
        self.wait()


def build(nc, ins, outs):
    ctx = ExitStack()
    with ctx:
        def sb(name, shape, dt=F32):
            return ctx.enter_context(nc.sbuf_tensor(name, shape, dt))

        def sem(name):
            return ctx.enter_context(nc.semaphore(name))

        ring = sb("ring", [P, SLOTS, UNIT])
        xa = sb("xa", [P, TT, D])
        bc = sb("bc", [P, 2 * KT * T])
        cat = sb("cat", [P, KT, T])
        consts = sb("consts", [P, NCONST])
        small = sb("small", [P, 544])
        gains = sb("gains", [P, KT])
        pages = sb("pages", [1, NPAGES], I32)
        npass_sb = sb("npass_sb", [1, 1], I32)
        xT_dram = nc.dram_tensor("xT_scratch", [P, KT, SEQ], F32).ap()
        qrows_dram = nc.dram_tensor("qrows_scratch", [NB, ATT], F32).ap()

        bank = [ctx.enter_context(nc.psum_tensor(f"bank{i}", [P, 512], F32)) for i in range(8)]

        def const(name):
            a, b = CONST_AT[name]
            return consts[:, a:b]

        late0 = CONST_AT["dist"][0]

        def late(name):
            a, b = LATE_AT[name]
            return consts[:, late0 + a:late0 + b]

        ident = const("ident")

        hT = bc[:, 0:KT * T].rearrange("p (k t) -> p k t", t=T)
        qkT = bc[:, KT * T:].rearrange("p (k t) -> p k t", t=T)
        vrow = xa[:, 0, :].rearrange("p (t c) -> p t c", t=2)
        tmp = xa[:, 1:3, :].rearrange("p a n -> p (a n)")
        prob = tmp[:, 0:768]
        qz = tmp[:, 768:1280].rearrange("p (c q) -> p c q", c=2)
        osq = tmp[:, 1296:1552]
        ord_ = tmp[:, 1560:1816]
        sq = [tmp[:, 1296 + T * i:1296 + T * i + T] for i in range(2)]
        diff = tmp[:, 1824:2208]
        diffT = tmp[:, 2208:2592]
        rstd = [tmp[:, 1824 + T * i:1824 + T * i + T] for i in range(2)]
        ctmp = tmp[:, 2592:2592 + T]
        upad = tmp[:, 2856:2856 + T + 2]
        conv = tmp[:, 3122:3122 + T]
        keysc = tmp[:, 3386:3642].rearrange("p (g c h b) -> p g c h b", g=NPG, c=2, h=H)
        rowsc = tmp[:, 3642:3642 + PAST + 1]
        selfqk = tmp[:, 3902:4030]
        selfsel = tmp[:, 4030:4094]
        pairw = tmp[:, 0:512].rearrange("p (g b c) -> p g b c", g=NPG, b=NB)
        pvrows = xa[:, 0, :].rearrange("p (r c) -> p r c", r=2)
        vT = [cat[:, 14 + i, :] for i in range(2)]
        kvstage = [cat[:, 11:14, :].rearrange("p k t -> p (k t)")[:, 384 * i:384 * i + 384] for i in range(2)]
        osamp = tmp[:, 512:512 + H * NB]

        o = [0]

        def piece(n):
            o[0] += n
            return small[:, o[0] - n:o[0]]

        rawT = piece(3 * CT + 2 * KT)
        convwT = rawT[:, 0:3 * CT]
        gffnT = rawT[:, 3 * CT:3 * CT + KT]
        prevT = piece(NB * 2 * CT)
        stash = piece((2 + NB) * CT)
        vTs = piece(H * NB)
        ssum = piece(4)
        srstd = piece(4)
        lamv = piece(4)
        nmax = piece(4)
        esum = piece(4)
        rsum = piece(4)
        gqk = piece(2)
        gsub = piece(2)
        route = piece(4 * TT)
        xsT = piece(KT * NB).rearrange("p (k b) -> p k b", k=KT)
        ssq = piece(TT * KT).rearrange("p (t k) -> p t k", t=TT)
        gmix = rawT[:, 3 * CT + KT:]
        gffn = gains[:, :]

        rawrows = ring[:, SLOTS - 1, 0:256]
        lamraw = ring[:, SLOTS - 1, 256:256 + 4 * HALF]
        lamprod = ring[:, SLOTS - 1, 512:512 + HALF]
        sqjunk = ring[:, SLOTS - 2, 0:D]
        spread = ring[:, SLOTS - 2, D:D + TT * P].rearrange("p (t c) -> p t c", t=TT)
        rstdB = ring[:, SLOTS - 3, D:D + T]
        sqjunk2 = ring[:, SLOTS - 3, 0:D]

        yT = [bc[:, 6144 + T * i:6144 + T * i + T] for i in range(2)]
        junk_act = [bc[:, 7808 + P * t:7808 + P * (t + 1)] for t in range(TT)]
        wrv = bc[:, 6672:6672 + KT * RE].rearrange("p (k e) -> p k e", k=KT)
        logitsT = bc[0:RE, 7312:7312 + T]
        outrows = bc[:, 7576:7704]
        rbias = bc[:, 7704:7704 + RE]
        h2 = bc[:, 0:TT * D].rearrange("p (t d) -> p t d", t=TT)
        sel = bc[:, 6144:6528].rearrange("p (t s) -> p t s", t=TT)
        gate = bc[:, 6528:6912].rearrange("p (t s) -> p t s", t=TT)
        gateT = bc[:, 6912:7296].rearrange("p (t s) -> p t s", t=TT)
        g_sb = bc[:, 7296:7808]
        u_sb = bc[:, 7808:8320]
        actT = bc[:, 8320:8448].rearrange("p (c s) -> p c s", c=FC)
        catf = cat[:, :, :].rearrange("p k t -> p (k t)")
        xeT = catf[:, 0:D].rearrange("p (k s) -> p k s", k=KT)
        ye = catf[:, D:2 * D]
        o[0] = 0

        def rt(n):
            o[0] += n
            return catf[:, D + o[0] - n:D + o[0]].rearrange("p (t e) -> p t e", t=TT)

        logits = rt(TT * RE)
        gs, w_n, ew = (rt(TT) for _ in range(3))
        goh, gex, geneg = (rt(TT * GROUPS) for _ in range(3))
        lem, oh1, oh2, work, slotmap = (rt(TT * NE) for _ in range(5))
        gtop, etop, gat, eat = (rt(TT * 8) for _ in range(4))
        exc = rt(TT * NE * MAXPASS)
        bothf = catf[:, D + o[0]:D + o[0] + 4 * NE]
        both = bothf[:, 0:TT * NE].rearrange("p (t e) -> p t e", t=TT)
        o[0] += 4 * NE
        gidx = catf[:, D + o[0]:D + o[0] + TT * 8].bitcast(mybir.dt.uint32).rearrange("p (t e) -> p t e", t=TT)
        o[0] += TT * 8
        eidx = catf[:, D + o[0]:D + o[0] + TT * 8].bitcast(mybir.dt.uint32).rearrange("p (t e) -> p t e", t=TT)
        o[0] += TT * 8
        cmax = catf[:, D + o[0]:D + o[0] + 1]
        cpass = catf[:, D + o[0] + 1:D + o[0] + 2]
        cwork = catf[:, D + o[0] + 2:D + o[0] + 2 + MAXPASS]
        assert D + o[0] + 2 + MAXPASS <= KT * T
        pos1, pos2, w1, w2 = (route[:, TT * i:TT * i + TT] for i in range(4))

        slot_full = [sem(f"slot_full{i}") for i in range(SLOTS)]
        x_in = [sem(f"x_in{i}") for i in range(TT)]
        consts_in = sem("consts_in")
        vecs_in = sem("vecs_in")
        late_in = sem("late_in")
        wr_in = sem("wr_in")
        wr_zero = sem("wr_zero")
        pages_in = sem("pages_in")
        x2_zero = sem("x2_zero")
        x_clear = sem("x_clear")
        raw_T = sem("raw_T")
        raw_copied = sem("raw_copied")
        sums1_dve = sem("sums1_dve")
        sums1 = sem("sums1")
        spread_ready = sem("spread_ready")
        factors = sem("factors")
        factors_ready = sem("factors_ready")
        xT_even = sem("xT_even")
        xT_odd = sem("xT_odd")
        xT_stored = sem("xT_stored")
        xsT_ready = sem("xsT_ready")
        sqrt1 = sem("sqrt1")
        h_T = sem("h_T")
        h_ready = sem("h_ready")
        tile_done = sem("tile_done")
        squared = sem("squared")
        summed = sem("summed")
        rooted = sem("rooted")
        qk_ready = sem("qk_ready")
        v_copied = sem("v_copied")
        rows_T = sem("rows_T")
        rows_out = sem("rows_out")
        v_rows = sem("v_rows")
        vs_ready = sem("vs_ready")
        stored = [sem("stored0"), sem("stored1")]
        c_copied = sem("c_copied")
        u_ready = sem("u_ready")
        conv_ready = sem("conv_ready")
        stash_T = sem("stash_T")
        stash_out = sem("stash_out")
        stash_ready = sem("stash_ready")
        qz_ready = sem("qz_ready")
        qz_zero = sem("qz_zero")
        scores = sem("scores")
        biased = sem("biased")
        exped = sem("exped")
        diffed = sem("diffed")
        diff_T = sem("diff_T")
        diffT_copied = sem("diffT_copied")
        pv = sem("pv")
        o_squared = sem("o_squared")
        o_summed = sem("o_summed")
        o_rooted = sem("o_rooted")
        o_ready = sem("o_ready")
        page_mul = sem("page_mul")
        page_sum = sem("page_sum")
        self_ready = sem("self_ready")
        s_T = sem("s_T")
        s_biased = sem("s_biased")
        s_exped = sem("s_exped")
        s_probs = sem("s_probs")
        s_pair = sem("s_pair")
        s_pair_copied = sem("s_pair_copied")
        s_pv = sem("s_pv")
        y_copied = sem("y_copied")
        y_T = sem("y_T")
        y_added = sem("y_added")
        sums2 = sem("sums2")
        sqrt2 = sem("sqrt2")
        h2_zero = sem("h2_zero")
        h2_ready = sem("h2_ready")
        wr_ready = sem("wr_ready")
        logits_copied = sem("logits_copied")
        logits_T = sem("logits_T")
        ssq_sum = sem("ssq_sum")
        s_pv_copied = sem("s_pv_copied")
        s_picked = sem("s_picked")
        s_whole = sem("s_whole")
        router = sem("router")
        gex_ready = sem("gex_ready")
        gexed = sem("gexed")
        assigned = sem("assigned")
        ranked = sem("ranked")
        routed = sem("routed")
        sel_ready = sem("sel_ready")
        gate_ready = sem("gate_ready")
        gathered = sem("gathered")
        xe_ready = sem("xe_ready")
        gate_T = sem("gate_T")
        gateT_copied = sem("gateT_copied")
        g_done = sem("g_done")
        u_done = sem("u_done")
        g_copied = sem("g_copied")
        u_copied = sem("u_copied")
        folded = sem("folded")
        silu_done = sem("silu_done")
        act_ready = sem("act_ready")
        unit_used = sem("unit_used")
        down_done = sem("down_done")
        ye_act = sem("ye_act")
        ye_dve = sem("ye_dve")
        mixed = sem("mixed")
        mix_added = [sem(f"mix_added{t}") for t in range(TT)]
        y_stored = sem("y_stored")
        state_stored = sem("state_stored")
        dve_step = sem("dve_step")
        act_step = sem("act_step")

        def slot_of(n):
            return n % SLOTS

        front_total = [0] * SLOTS
        front_at = {}
        for n, unit in enumerate(FRONT):
            front_total[slot_of(n)] += 16 * (PPU if unit[0] in ("KP", "VP") else 1)
            front_at[unit] = (slot_of(n), front_total[slot_of(n)])

        def arrived(eng, unit):
            s, value = front_at[unit]
            eng.wait_ge(slot_full[s], value)

        def used_wait(eng, n):
            kind, u = FRONT[n]
            if kind == "KP":
                eng.wait_ge(page_sum, PPU * (u + 1))
            elif kind == "QB":
                eng.wait_ge(page_mul, 8 * (u + 1))
            elif kind == "VP":
                eng.wait_ge(s_pv, u + 1)
            elif kind == "XT":
                eng.wait_ge(y_copied, KT)
            else:
                eng.wait_ge(tile_done, TILE_AT[(kind, TPU * u + TPU - 1)] + 1)

        block = ctx.enter_context(nc.Block())

        @block.sync
        def _(sp):
            w_in = ins["w_in"].rearrange("l (k p) n -> (l p) k n", p=P)
            w_out = ins["w_out"].rearrange("l (k p) n -> (l p) k n", p=P)
            xp = ins["x_prompt"].rearrange("o (t p) d -> (o t) p d", p=P)
            for t in range(2):
                sp.dma_start(xa[:, t, :], xp[t]).then_inc(x_in[t], 16)
            sp.dma_start(pages[:, :], ins["page_table"].rearrange("(o b) g -> o (b g)", o=1)).then_inc(pages_in, 16)

            n_vecs = [0]

            def vec(dst, src):
                sp.dma_start(dst, src).then_inc(vecs_in, 16)
                n_vecs[0] += 1

            vec(rawrows[3 * CT + KT:3 * CT + 2 * KT, 0:P], ins["norm_mix"].rearrange("l (k p) -> (l k) p", p=P))
            vec(gffn, ins["norm_ffn"].rearrange("l (p k) -> (l p) k", k=KT))
            for c in range(2):
                vec(gqk[c * HALF:(c + 1) * HALF, 0:1], ins["g_q"].rearrange("l (d o) -> (l d) o", o=1))
                vec(gqk[c * HALF:(c + 1) * HALF, 1:2], ins["g_k"].rearrange("l (d o) -> (l d) o", o=1))
            vec(gsub[:, 0:1], ins["g_sub"].rearrange("l (d o) -> (l d) o", o=1))
            for i, name in enumerate(("lam_q1", "lam_k1", "lam_q2", "lam_k2")):
                vec(lamraw[:, i * HALF:(i + 1) * HALF], ins[name].partition_broadcast(P).rearrange("p l d -> p (l d)"))
            vec(rawrows[3 * CT:3 * CT + KT, 0:P], ins["norm_ffn"].rearrange("l (k p) -> (l k) p", p=P))
            vec(rawrows[0:3 * CT, 0:P], ins["conv_w"].rearrange("l j (i p) -> (l j i) p", p=P))
            vec(rawrows[:, P:2 * P], ins["state_conv"].rearrange("l b j (i p) -> (l b j i) p", p=P))
            assert n_vecs[0] == VECS

            sp.wait_ge(vecs_in, VECS * 16)
            sp.wait_ge(consts_in, 16)
            for n, (kind, u) in enumerate(FRONT):
                s = slot_of(n)
                if n == SLOTS - 3:
                    sp.wait_ge(h_ready, KT)
                    sp.wait_ge(act_step, 1)
                if n >= SLOTS:
                    used_wait(sp, n - SLOTS)
                if kind == "W":
                    sp.dma_start(ring[:, s, :].rearrange("p (k c) -> p k c", k=KT),
                                 w_out[:, :, u * UC:(u + 1) * UC]).then_inc(slot_full[s], 16)
                elif kind == "XT":
                    sp.wait_ge(xT_stored, 16)
                    sp.dma_start(ring[:, s, :].rearrange("p (k t) -> p k t", k=KT), xT_dram).then_inc(slot_full[s], 16)
                elif kind == "QB":
                    for i in range(4):
                        sp.wait_ge(stored[i % 2], 16 * (H // 2))
                    sp.dma_start(ring[:, s, :].rearrange("p (b c) -> p b c", b=4),
                                 qrows_dram[4 * u:4 * u + 4, :].partition_broadcast(P)).then_inc(slot_full[s], 16)
                elif kind in ("KP", "VP"):
                    if (kind, u) == ("KP", 0):
                        sp.wait_ge(pages_in, 16)
                    pool_rows = ins["cache_k" if kind == "KP" else "cache_v"].rearrange("l n s h c -> (l n) s (h c)")
                    for i in range(PPU):
                        j = u * PPU + i
                        page = sp.value_load(pages[0:1, j:j + 1], min_val=0, max_val=pool_rows.shape[0] - 1)
                        sp.dma_start(ring[:, s, i * ATT:(i + 1) * ATT],
                                     pool_rows[bass.ds(page, 1), :, :].rearrange("o s c -> s (o c)")
                                     ).then_inc(slot_full[s], 16)
                else:
                    c0 = COLUMN[kind] + u * UC
                    sp.dma_start(ring[:, s, :].rearrange("p (k c) -> p k c", k=KT),
                                 w_in[:, :, c0:c0 + UC]).then_inc(slot_full[s], 16)

            wg = ins["w_gate"].rearrange("l (g j) (p k) f -> (l g) p j (k f)", j=EG, k=KT)
            wu = ins["w_up"].rearrange("l (g j) (p k) f -> (l g) p j (k f)", j=EG, k=KT)
            wd = ins["w_down"].rearrange("l (g j) (p k) d -> (l g) p j (k d)", j=EG, k=FC)

            def expert_used(m, it):
                j, i = divmod(m, UPE)
                if i % 2 == 0:
                    sp.wait_ge(unit_used, it * (3 * EG) + (3 * j + i // 2 + 1))
                else:
                    sp.wait_ge((g_done, u_done, down_done)[i // 2], it * EG + (j + 1))

            def group(g, it):
                for j in range(EG):
                    for i in range(UPE):
                        m = j * UPE + i
                        s = slot_of(NFRONT + m)
                        src = (wg, wg, wu, wu, wd, wd)[i]
                        expert_used(m - SLOTS, it)
                        sp.dma_start(ring[:, s, :], src[bass.ds(g, 1), :, j, (i % 2) * UNIT:(i % 2 + 1) * UNIT]
                                     .rearrange("o p n -> p (o n)")).then_inc(slot_full[s], 16)

            for m in range(UPG):
                s = slot_of(NFRONT + m)
                j, i = divmod(m, UPE)
                if m < SLOTS:
                    used_wait(sp, NFRONT + m - SLOTS)
                else:
                    expert_used(m - SLOTS, 0)
                src = (wg, wg, wu, wu, wd, wd)[i]
                sp.dma_start(ring[:, s, :], src[0, :, j, (i % 2) * UNIT:(i % 2 + 1) * UNIT]).then_inc(slot_full[s], 16)
            with sp.Fori(1, NG) as g:
                group(g, g)
            sp.wait_ge(routed, 1)
            npass = sp.value_load(npass_sb[0:1, 0:1], min_val=1, max_val=MAXPASS)
            with sp.If(npass > 1):
                with sp.Fori(1, npass) as r:
                    with sp.Fori(0, NG) as g:
                        group(g, r * NG + g)
            with sp.Else():
                pass

            for t in range(2):
                sp.wait_ge(mix_added[t], npass * (NG * 4))
                sp.dma_start(outs["y_prompt"].rearrange("o (t p) d -> (o t) p d", p=P)[t], xa[:, t, :]).then_inc(y_stored, 16)
            sp.wait_ge(mix_added[2], npass * (NG * 4) + 2)
            sp.dma_start(outs["y_sample"].rearrange("b o d -> b (o d)"), xa[0:NB, 2, :]).then_inc(y_stored, 16)
            sp.wait_ge(y_stored, 48)
            sp.wait_ge(state_stored, 16)
            sp.wait_ge(stored[0], STORED[0] + 16)
            sp.wait_ge(stored[1], STORED[1] + 16 * NB)

        @block.tensor
        def _(pe):
            pe.wait_ge(consts_in, 16)
            for t in range(TT):
                pe.wait_ge(x_in[t], 16)
            for k in range(KT):
                if k >= 4:
                    pe.wait_ge((xT_even, xT_odd)[k % 2], (k - 4) // 2 + 1)
                for t in range(TT):
                    m = pe.transpose(bank[3 + k % 4][:, P * t:P * t + P], xa[:, t, k * P:(k + 1) * P], ident)
                m.then_inc(h_T, 1)
            pe.wait_ge(vecs_in, VECS * 16)
            nr = 3 * CT + 2 * KT
            pe.transpose(bank[7][:, 0:nr], rawrows[0:nr, 0:P], ident[0:nr, 0:nr])
            pe.transpose(bank[7][:, P:2 * P], rawrows[:, P:2 * P], ident).then_inc(raw_T, 1)
            pe.wait_ge(spread_ready, 1)
            for t in range(TT):
                w = P if t < 2 else NB
                m = pe.matmul(bank[2][:, t * P:t * P + w], const("ones"), spread[:, t, 0:w], start=True, stop=True)
            m.then_inc(factors, 1)

            def bank_free(n):
                if n < 3:
                    if n == 2:
                        pe.wait_ge(factors_ready, 1)
                    return
                kind, i = TILES[n - 3]
                s, value = {"q": (qk_ready, i + 1), "k": (qk_ready, H + i + 1), "v": (v_copied, i + 1),
                            "C": (c_copied, i + 1), "X": (u_ready, i + 1), "B": (conv_ready, i + 1),
                            "W": (y_copied, i + 1)}[kind]
                pe.wait_ge(s, value)

            def tile(n):
                kind, i = TILES[n]
                unit = (kind, i // TPU)
                arrived(pe, unit)
                bank_free(n)
                w = ring[:, front_at[unit][0], :].rearrange("p (k c) -> p k c", k=KT)
                order = range(KT)
                src = hT
                if kind == "W":
                    order = [*range(H, KT), *range(H)]
                    src = cat
                for n_k, k in enumerate(order):
                    if n == 0:
                        pe.wait_ge(h_ready, k + 1)
                    if kind == "W" and n_k == 0 and i == 0:
                        pe.wait_ge(conv_ready, CT)
                    if kind == "W" and n_k == H and i == 0:
                        pe.wait_ge(o_ready, H + 1)
                    m = pe.matmul(bank[n % 3][:, 0:T], w[:, k, (i % TPU) * P:(i % TPU + 1) * P], src[:, k, :],
                                  start=n_k == 0, stop=n_k == KT - 1)
                m.then_inc(tile_done, 1)

            def half_sums(t):
                pe.wait_ge(squared, t + 1)
                if t >= 1:
                    pe.wait_ge(rooted, t)
                pe.matmul(bank[3][:, 0:T], const("blk"), sq[t % 2], start=True, stop=True).then_inc(summed, 1)

            def rows(t):
                src = qkT[:, t, :] if t < 2 * H else vT[t % 2]
                if t < 2 * H:
                    pe.wait_ge(qk_ready, t + 1)
                else:
                    pe.wait_ge(v_copied, t - 2 * H + 1)
                if t >= 1:
                    pe.wait_ge(rows_out, t)
                if t >= H:
                    for i in range(2):
                        pe.transpose(bank[4][:, i * P:i * P + P], src[:, i * P:i * P + P], ident)
                pe.transpose(bank[4][0:NB, 2 * P:3 * P], src[:, SEQ:T], ident).then_inc(rows_T, 1)

            def head_sums(h):
                pe.wait_ge(o_squared, h + 1)
                if h >= 1:
                    pe.wait_ge(o_rooted, h)
                pe.matmul(bank[3][:, 0:SEQ], const("ones"), osq, start=True, stop=True).then_inc(o_summed, 1)

            def head_scores(h):
                pe.wait_ge(qz_ready, h + 1)
                if h >= 1:
                    pe.wait_ge(biased, h)
                for c in range(2):
                    pe.matmul(bank[5][:, c * SEQ:(c + 1) * SEQ], qz[:, c, P:SEQ], qkT[:, H + h, 0:SEQ],
                              start=True, stop=True)
                for c in range(2):
                    m = pe.matmul(bank[6][:, c * P:(c + 1) * P], qz[:, c, 0:P], qkT[:, H + h, 0:P],
                                  start=True, stop=True)
                m.then_inc(scores, 1)

            def head_turn(h):
                pe.wait_ge(diffed, h + 1)
                if h >= 1:
                    pe.wait_ge(o_ready, h)
                pe.transpose(bank[7][:, 0:P], diff[:, 2 * P:3 * P], ident)
                pe.transpose(bank[7][:, P:2 * P], diff[:, 0:P], ident)
                pe.transpose(bank[7][:, 2 * P:3 * P], diff[:, P:2 * P], ident).then_inc(diff_T, 1)

            def head_pv(h):
                pe.wait_ge(diffT_copied, h + 1)
                pe.wait_ge(v_rows, h + 1)
                pe.matmul(bank[7][:, 0:SEQ], vrow[:, 0, h * HD:(h + 1) * HD], diffT[:, 0:SEQ], start=True, stop=False)
                pe.matmul(bank[7][:, P:SEQ], vrow[:, 1, h * HD:(h + 1) * HD], diffT[:, SEQ:SEQ + P],
                          start=False, stop=True).then_inc(pv, 1)

            def sample_rows():
                pe.wait_ge(page_sum, NPAGES)
                pe.wait_ge(biased, H)
                for g in range(NPG):
                    pe.transpose(bank[5][:, g * PAGE:(g + 1) * PAGE],
                                 keysc[:, g, :, :, :].rearrange("p c h b -> p (c h b)"), ident)
                pe.wait_ge(self_ready, 1)
                pe.matmul(bank[6][:, 0:1], selfqk, const("ones")[:, 0:1], start=True, stop=True).then_inc(s_T, 1)

            def sample_keys():
                pe.wait_ge(s_probs, 1)
                for g in range(NPG):
                    pe.matmul(bank[6][:, g * H * NB:(g + 1) * H * NB], rowsc[:, g * PAGE:(g + 1) * PAGE], const("sel"),
                              start=True, stop=True)
                pe.matmul(bank[6][:, 2 * H * NB:3 * H * NB], const("ones"), selfsel, start=True, stop=True).then_inc(s_pair, 1)

            def sample_pv():
                pe.wait_ge(s_pair_copied, 1)
                pe.wait_ge(rows_out, 3 * H)
                pe.wait_ge(o_ready, H)
                for b in range(NB):
                    u = b // 2
                    if b % 2 == 0:
                        arrived(pe, ("VP", u))
                    for g in range(NPG):
                        page = ((b % 2) * NPG + g) * ATT
                        for half in range(2):
                            to = bank[((4, 5), (7, 6))[b // 4][half]]
                            m = pe.matmul(to[C * (b % 4):C * (b % 4 + 1), :], pairw[:, g, b, :],
                                          ring[:, front_at[("VP", u)][0], page + half * 512:page + (half + 1) * 512],
                                          start=g == 0, stop=g == NPG - 1, skip_group_check=True)
                    if b % 2:
                        m.then_inc(s_pv, 1)

            def sample_pick(r):
                pe.wait_ge(s_pv_copied, 2 * (r + 1))
                pe.wait_ge(o_rooted, H)
                for h in range(H):
                    m = pe.matmul(bank[3][:, h * NB + 4 * r:h * NB + 4 * r + 4], pvrows[:, r, h * HD:(h + 1) * HD],
                                  ident[:, h::C], start=True, stop=True)
                m.then_inc(s_picked, 1)

            def sample_sums():
                pe.wait_ge(o_squared, H + 1)
                pe.matmul(bank[4][:, 0:H * NB], const("ones"), osq[:, 0:H * NB], start=True, stop=True).then_inc(o_summed, 1)

            for n in range(NIN):
                tile(n)
                if 1 <= n <= 2 * H:
                    half_sums(n - 1)
                if 2 <= n < 3 * H + 2:
                    rows(n - 2)
                h, stage = divmod(n - HEAD0, 3)
                if stage == 0 and 1 <= h <= H:
                    head_sums(h - 1)
                if 0 <= h < H:
                    (head_scores, head_turn, head_pv)[stage](h)
                if n == SAMPLE0:
                    sample_rows()
                if n == SAMPLE0 + 1:
                    sample_keys()
                if n == SAMPLE0 + 2:
                    sample_pv()
                if n == SAMPLE0 + 3:
                    sample_pick(0)
                    sample_pick(1)
                if n == SAMPLE0 + 4:
                    sample_sums()

            pe.wait_ge(stash_ready, 1)
            pe.transpose(bank[5][0:(2 + NB) * CT, 0:P], stash, ident).then_inc(stash_T, 1)

            def y_turn(j):
                pe.wait_ge(y_copied, j + 1)
                b = bank[3 + j % 2]
                if j >= 2:
                    pe.wait_ge(y_added, j - 1)
                if j == 0:
                    pe.wait_ge(s_whole, 1)
                if j == 1:
                    pe.wait_ge(o_rooted, H + 1)
                for t in range(2):
                    pe.transpose(b[:, t * P:(t + 1) * P], yT[j % 2][:, t * P:(t + 1) * P], ident)
                pe.transpose(b[0:NB, 2 * P:3 * P], yT[j % 2][:, SEQ:T], ident)
                if j == 0:
                    pe.wait_ge(wr_ready, 1)
                    pe.wait_ge(s_pv_copied, 4)
                pe.matmul(bank[6][0:RE, 0:T], wrv[:, j, :], yT[j % 2], start=j == 0, stop=j == KT - 1,
                          ).then_inc(y_T, 1)

            for j in range(KT):
                tile(TILE_AT[("W", j)])
                if j >= 1:
                    y_turn(j - 1)
            y_turn(KT - 1)

            pe.wait_ge(logits_copied, 1)
            pe.wait_ge(stash_out, 1)
            for t in range(TT):
                n = P if t < 2 else NB
                m = pe.transpose(bank[5][0:n, t * RE:(t + 1) * RE], logitsT[:, t * P:t * P + n], ident[0:RE, 0:RE])
            m.then_inc(router, 1)
            pe.wait_ge(assigned, 1)
            pe.wait_ge(late_in, 16)
            pe.wait_ge(y_added, KT)
            pe.matmul(bank[3][:, 0:4 * NE], late("tri"), bothf, start=True, stop=False)
            for s in range(1, 4):
                m = pe.matmul(bank[3][:, s * NE:4 * NE], const("ones"), bothf[:, 0:(4 - s) * NE], start=False, stop=s == 3)
            m.then_inc(ranked, 1)

            pe.wait_ge(routed, 1)
            npass = pe.value_load(npass_sb[0:1, 0:1], min_val=1, max_val=MAXPASS)
            with pe.Fori(0, npass) as r:
                with pe.Fori(0, NG) as g:
                    it = r * NG + g

                    pe.wait_ge(sel_ready, it + 1)
                    pe.wait_ge(h2_ready, 2 * KT)
                    for q in range(4):
                        if q >= 2:
                            pe.wait_ge(xe_ready, it * 4 + (q - 1))
                        for k in range(4 * q, 4 * q + 4):
                            for t in range(TT):
                                m = pe.matmul(bank[4 + q % 2][:, (k % 4) * P:(k % 4 + 1) * P], h2[:, t, k::KT], sel[:, t, :],
                                              start=t == 0, stop=t == TT - 1)
                        m.then_inc(gathered, 1)
                    pe.wait_ge(gate_ready, it + 1)
                    for t in range(TT):
                        m = pe.transpose(bank[3][:, t * P:(t + 1) * P], gate[:, t, :], ident)
                    m.then_inc(gate_T, 1)
                    pe.wait_ge(xe_ready, it * 4 + 4)
                    pe.wait_ge(gateT_copied, it + 1)

                    for j in range(EG):
                        e = it * EG + j

                        def weights(i):
                            m = j * UPE + i
                            s = slot_of(NFRONT + m)
                            before = sum(slot_of(NFRONT + x) == s for x in range(m + 1))
                            pe.wait_ge(slot_full[s], it * (16 * UPG // SLOTS) + (front_total[s] + 16 * before))
                            return ring[:, s, :]

                        for half, b in ((0, 0), (2, 1)):
                            for i in range(2):
                                w = weights(half + i).rearrange("p (k f) -> p k f", f=F)
                                for k in range(8):
                                    c = k % 4
                                    m = pe.matmul(bank[b][c * C:(c + 1) * C, :], xeT[:, 8 * i + k, j * C:(j + 1) * C], w[:, k, :],
                                                  start=i == 0 and k < 4, stop=i == 1 and k >= 4, skip_group_check=True)
                                if i == 0:
                                    m.then_inc(unit_used, 1)
                            m.then_inc(g_done if b == 0 else u_done, 1)
                        for x, (src, copied) in enumerate(((g_sb, g_copied), (u_sb, u_copied))):
                            pe.wait_ge(copied, e + 1)
                            for c in range(FC):
                                m = pe.matmul(bank[3][:, (x * FC + c) * C:(x * FC + c + 1) * C], src[:, c::FC], const("fold"),
                                              start=True, stop=True)
                        m.then_inc(folded, 1)
                        pe.wait_ge(act_ready, e + 1)
                        if j >= 1:
                            pe.wait_ge(ye_act, (it * EG + j) * 2)
                            pe.wait_ge(ye_dve, (it * EG + j) * 2)
                        for i in range(2):
                            w = weights(4 + i).rearrange("p (c n d) -> p c n d", c=2, n=4)
                            for c in range(2):
                                for n in range(4):
                                    m = pe.matmul(bank[2][n * C:(n + 1) * C, :], actT[:, 2 * i + c, :], w[:, c, n, :],
                                                  start=i == 0 and c == 0, stop=i == 1 and c == 1, skip_group_check=True)
                            if i == 0:
                                m.then_inc(unit_used, 1)
                        m.then_inc(down_done, 1)

                    pe.wait_ge(ye_act, (it + 1) * EG * 2)
                    pe.wait_ge(ye_dve, (it + 1) * EG * 2)
                    for t in range(TT):
                        for n in range(4):
                            m = t * 4 + n
                            if m >= 2:
                                pe.wait_ge(mix_added[(m - 2) // 4], it * 4 + ((m - 2) % 4 + (3 if m - 2 >= 8 else 1)))
                            else:
                                pe.wait_ge(mix_added[TT - 1], it * 4 + (m + 1))
                            pe.matmul(bank[6 + m % 2][:, :], gateT[:, t, :], ye[:, n * 512:(n + 1) * 512],
                                      start=True, stop=True).then_inc(mixed, 1)

        @block.scalar
        def _(act):
            A = nc.scalar.activation
            act.dma_start(consts[:, :], ins["consts"]).then_inc(consts_in, 16)
            act.wait_ge(x_in[0], 16)
            A(sqjunk, xa[:, 0, :], ACT.Square, accum_out=ssum[:, 0:1]).then_inc(sums1, 1)
            act.wait_ge(x_in[2], 16)
            act.wait_ge(sums1, 1)
            A(sqjunk, xa[:, 2, :], ACT.Square, accum_out=ssum[:, 2:3]).then_inc(sums1, 1)
            act.wait_ge(consts_in, 16)
            act.wait_ge(sums1, 2)
            act.wait_ge(sums1_dve, 1)
            A(srstd[:, 0:TT], ssum[:, 0:TT], ACT.Sqrt, bias=const("eps"), scale=1.0 / D).then_inc(sqrt1, 1)
            for k in range(0, KT, 2):
                act.wait_ge(h_T, k + 1)
                A(cat[:, k, :], bank[3 + k % 4][:, 0:T], ACT.Copy).then_inc(xT_even, 1)
            act.wait_ge(raw_T, 1)
            A(rawT, bank[7][:, 0:3 * CT + 2 * KT], ACT.Copy)
            A(prevT, bank[7][:, P:2 * P], ACT.Copy).then_inc(raw_copied, 1)
            act.wait_ge(xT_odd, KT // 2)
            act.wait_ge(xT_even, KT // 2)
            act.dma_start(xT_dram, cat[:, :, 0:SEQ]).then_inc(xT_stored, 16)
            act.wait_ge(act_step, 1)
            A(lamv[:, 0:2], lamv[:, 0:2], ACT.Exp).then_inc(act_step, 1)

            n_stored = [0, 0]

            def square(t):
                act.wait_ge(tile_done, t + 1)
                if t >= 2:
                    act.wait_ge(summed, t - 1)
                A(sq[t % 2], bank[t % 3][:, 0:T], ACT.Square).then_inc(squared, 1)

            def root(t):
                act.wait_ge(summed, t + 1)
                if t >= 2:
                    act.wait_ge(qk_ready, t - 1)
                A(rstd[t % 2], bank[3][:, 0:T], ACT.Sqrt, bias=const("eps")).then_inc(rooted, 1)

            def copy_v(h):
                t = 2 * H + h
                act.wait_ge(tile_done, t + 1)
                if h >= 2:
                    act.wait_ge(rows_T, t - 1)
                A(vT[t % 2], bank[t % 3][:, 0:T], ACT.Copy)
                A(vTs[:, h * NB:(h + 1) * NB], bank[t % 3][:, SEQ:T], ACT.Copy).then_inc(v_copied, 1)

            def rows_outgoing(t):
                stage, s = kvstage[t % 2], stored[t % 2]
                cols = slice((t % H) * HD, (t % H + 1) * HD)
                act.wait_ge(rows_T, t + 1)
                if t == 0:
                    act.wait_ge(xT_stored, 16)
                    act.wait_ge(xsT_ready, 1)
                if t >= 2:
                    act.wait_ge(s, n_stored[t % 2])
                if t >= 2 * H:
                    A(vrow[:, :, cols], bank[4][:, 0:2 * P].rearrange("p (t c) -> p t c", t=2), ACT.Copy).then_inc(v_rows, 1)
                elif t >= H:
                    A(stage[:, 0:2 * P], bank[4][:, 0:2 * P], ACT.Copy)
                A(stage[0:NB, 2 * P:3 * P], bank[4][0:NB, 2 * P:3 * P], ACT.Copy).then_inc(rows_out, 1)
                act.wait_ge(rows_out, t + 1)
                if t < H:
                    act.dma_start(qrows_dram[:, cols], stage[0:NB, 2 * P:3 * P]).then_inc(s, 16)
                    n_stored[t % 2] += 16
                    return
                name = "k" if t < 2 * H else "v"
                src = stage[:, 0:2 * P].rearrange("p (t c) -> p t c", t=2) if t < 2 * H else vrow[:, :, cols]
                if t >= 2 * H:
                    act.wait_ge(v_rows, t - 2 * H + 1)
                act.dma_start(outs[name + "_prompt"].rearrange("l o (t p) h d -> p (l o t) (h d)", p=P)[:, :, cols],
                              src).then_inc(s, 16)
                act.dma_start(outs[name + "_sample"].rearrange("l b o h d -> (l b o) (h d)")[:, cols],
                              stage[0:NB, 2 * P:3 * P]).then_inc(s, 16)
                n_stored[t % 2] += 32

            def head_root(h, cols=SEQ):
                act.wait_ge(o_summed, h + 1)
                if h >= 1:
                    act.wait_ge(o_ready, h)
                A(ord_[:, 0:cols], bank[3 if h < H else 4][:, 0:cols], ACT.Sqrt, bias=const("eps"), scale=1.0 / HD).then_inc(o_rooted, 1)

            for n in range(NIN):
                if n < 2 * H:
                    square(n)
                elif n < 3 * H:
                    copy_v(n - 2 * H)
                elif (n - BCX) % 3 == 0:
                    i = (n - BCX) // 3
                    act.wait_ge(tile_done, n + 1)
                    if i >= 1:
                        act.wait_ge(u_ready, i)
                    A(ctmp, bank[n % 3][:, 0:T], ACT.Copy).then_inc(c_copied, 1)
                if 1 <= n <= 2 * H:
                    root(n - 1)
                if 2 <= n < 3 * H + 2:
                    rows_outgoing(n - 2)
                h, stage = divmod(n - HEAD0, 3)
                if stage == 0 and 1 <= h <= H:
                    head_root(h - 1)
                if stage == 0 and 0 <= h < H:
                    act.wait_ge(biased, h + 1)
                    for x in range(4):
                        a, b = ((0, 256), (256, 512), (512, 640), (640, 768))[x]
                        A(prob[:, a:b], prob[:, a:b], ACT.Exp, bias=nmax[:, x:x + 1], accum_out=esum[:, x:x + 1]).then_inc(exped, 1)
                if stage == 1 and 0 <= h < H:
                    act.wait_ge(diff_T, h + 1)
                    A(diffT, bank[7][:, 0:3 * P], ACT.Copy).then_inc(diffT_copied, 1)
                if stage == 2 and 0 <= h < H:
                    act.wait_ge(pv, h + 1)
                    A(osq, bank[7][:, 0:SEQ], ACT.Square).then_inc(o_squared, 1)
                if n == SAMPLE0:
                    act.wait_ge(s_biased, 1)
                    A(rowsc, rowsc, ACT.Exp, bias=nmax[:, 0:1], accum_out=esum[:, 0:1]).then_inc(s_exped, 1)
                if n == SAMPLE0 + 3:
                    act.wait_ge(s_whole, 1)
                    A(osq[:, 0:H * NB], osamp[:, 0:H * NB], ACT.Square).then_inc(o_squared, 1)
                if n == SAMPLE0 + 4:
                    head_root(H, H * NB)
            assert tuple(n_stored) == STORED
            act.wait_ge(stash_T, 1)
            A(outrows[0:(2 + NB) * CT, :], bank[5][0:(2 + NB) * CT, 0:P], ACT.Copy).then_inc(stash_out, 1)
            act.wait_ge(stash_out, 1)
            act.dma_start(outs["conv_prompt"].rearrange("l o r (i p) -> (l o r i) p", p=P), outrows[0:2 * CT, :]
                          ).then_inc(stored[0], 16)
            for b in range(NB):
                act.dma_start(outs["conv_sample"].rearrange("l b r (i p) -> (l b) r i p", p=P)[b, 1],
                              outrows[(2 + b) * CT:(3 + b) * CT, :]).then_inc(stored[1], 16)

            def row_squares(j):
                act.wait_ge(y_added, j + 1)
                if j >= 1:
                    act.wait_ge(sums2, j)
                for t in range(TT):
                    ins_ = A(junk_act[t], xa[:, t, j * P:(j + 1) * P], ACT.Square, accum_out=ssq[:, t, j:j + 1])
                ins_.then_inc(sums2, 1)

            for j in range(KT - 2):
                row_squares(j)
            row_squares(KT - 2)
            act.wait_ge(y_T, KT)
            A(logitsT, bank[6][0:RE, 0:T], ACT.Copy).then_inc(logits_copied, 1)
            row_squares(KT - 1)
            act.wait_ge(ssq_sum, 1)
            act.wait_ge(stored[0], STORED[0] + 16)
            act.wait_ge(stored[1], STORED[1] + 16 * NB)
            A(srstd[:, 0:TT], ssum[:, 0:TT], ACT.Sqrt, bias=const("eps"), scale=1.0 / D).then_inc(sqrt2, 1)
            act.wait_ge(gex_ready, 1)
            A(gex, gex, ACT.Exp).then_inc(gexed, 1)
            A(ew, ew, ACT.Exp).then_inc(gexed, 1)

            act.wait_ge(routed, 1)
            npass = act.value_load(npass_sb[0:1, 0:1], min_val=1, max_val=MAXPASS)
            with act.Fori(0, npass) as r:
                with act.Fori(0, NG) as g:
                    it = r * NG + g
                    act.wait_ge(gate_T, it + 1)
                    A(gateT, bank[3][:, 0:TT * P].rearrange("p (t s) -> p t s", t=TT), ACT.Copy).then_inc(gateT_copied, 1)
                    for j in range(EG):
                        act.wait_ge(g_done, it * EG + (j + 1))
                        A(g_sb, bank[0][:, :], ACT.Copy).then_inc(g_copied, 1)
                        act.wait_ge(folded, it * EG + (j + 1))
                        A(actT, bank[3][:, 0:P].rearrange("p (c s) -> p c s", c=FC), ACT.Silu).then_inc(silu_done, 1)
                        act.wait_ge(down_done, it * EG + (j + 1))
                        for n in range(2):
                            A(ye[j * C:(j + 1) * C, n * 512:(n + 1) * 512], bank[2][n * C:(n + 1) * C, :], ACT.Copy
                              ).then_inc(ye_act, 1)

        @block.vector
        def _(dve):
            V = nc.vector
            st = Steps(dve, dve_step)
            dve.wait_ge(x_in[1], 16)
            V.tensor_tensor_reduce(sqjunk2, xa[:, 1, :], xa[:, 1, :], 1.0, 0.0, ALU.mult, ALU.add, ssum[:, 1:2]
                                   ).then_inc(sums1_dve, 1)
            for k in range(1, KT, 2):
                dve.wait_ge(h_T, k + 1)
                V.tensor_copy(cat[:, k, :], bank[3 + k % 4][:, 0:T]).then_inc(xT_odd, 1)
            dve.wait_ge(sqrt1, 1)
            st.do(V.reciprocal(srstd[:, 0:TT], srstd[:, 0:TT]))
            for t in range(TT):
                ins_ = V.tensor_scalar(spread[:, t, :], ident, srstd[:, t:t + 1], None, ALU.mult)
            ins_.then_inc(spread_ready, 1)
            dve.wait_ge(factors, 1)
            V.tensor_copy(rstdB, bank[2][:, 0:T]).then_inc(factors_ready, 1)
            dve.wait_ge(factors_ready, 1)
            dve.wait_ge(raw_copied, 1)
            dve.wait_ge(xT_even, KT // 2)
            dve.wait_ge(xT_odd, KT // 2)
            for k in range(KT):
                V.scalar_tensor_tensor(hT[:, k, :], cat[:, k, :], gmix[:, k:k + 1], rstdB, ALU.mult, ALU.mult).then_inc(h_ready, 1)
            V.tensor_copy(xsT, cat[:, :, SEQ:T]).then_inc(xsT_ready, 1)
            for i in range(2):
                st.do(V.tensor_tensor_reduce(lamprod, lamraw[:, 2 * i * HALF:(2 * i + 1) * HALF],
                                             lamraw[:, (2 * i + 1) * HALF:(2 * i + 2) * HALF], 1.0, 0.0,
                                             ALU.mult, ALU.add, lamv[:, i:i + 1]))
            V.tensor_scalar(gqk[:, 0:1], gqk[:, 0:1], HALF ** -0.5, None, ALU.mult).then_inc(act_step, 1)
            st.add(V.tensor_scalar(gsub[:, 1:2], gsub[:, 0:1], 1.0 - LAM_INIT, None, ALU.mult))
            dve.wait_ge(act_step, 2)
            st.do(V.tensor_tensor(lamv[:, 2:3], lamv[:, 0:1], lamv[:, 1:2], ALU.subtract))
            st.do(V.tensor_scalar(lamv[:, 2:3], lamv[:, 2:3], LAM_INIT, None, ALU.add))
            st.do(V.tensor_scalar(lamv[:, 3:4], lamv[:, 2:3], -1.0, None, ALU.mult))
            st.do(V.tensor_tensor(lamv[:, 0:1], lamv[:, 2:3], const("neg_c1"), ALU.mult))
            st.do(V.tensor_tensor(lamv[:, 0:1], lamv[:, 0:1], const("c0"), ALU.add))

            def normalise(t):
                r = rstd[t % 2]
                dve.wait_ge(rooted, t + 1)
                st.do(V.reciprocal(r, r))
                V.scalar_tensor_tensor(qkT[:, t, :], bank[t % 3][:, 0:T], gqk[:, t // H:t // H + 1], r,
                                       ALU.mult, ALU.mult).then_inc(qk_ready, 1)

            prev = prevT.rearrange("p (b j i) -> p b j i", b=NB, j=2)
            out = stash.rearrange("p (r i) -> p r i", i=CT)

            def page(j):
                b, g = divmod(j, NPG)
                dve.wait_ge(page_mul, j + 1)
                s, _ = front_at[("KP", j // PPU)]
                src = ring[:, s, (j % PPU) * ATT:(j % PPU + 1) * ATT].rearrange("p (h c d) -> p h c d", h=H, c=2)
                V.tensor_reduce(keysc[:, g, :, :, b].rearrange("p c h -> p h c"), src, AX.X, ALU.add).then_inc(page_sum, 1)

            def head_out(h):
                dve.wait_ge(o_rooted, h + 1)
                st.do(V.reciprocal(ord_, ord_))
                V.scalar_tensor_tensor(cat[:, h, 0:SEQ], bank[7][:, 0:SEQ], gsub[:, 1:2], ord_, ALU.mult, ALU.mult
                                       ).then_inc(o_ready, 1)

            def bias_scores(i):
                dve.wait_ge(scores, i + 1)
                for c in range(2):
                    st.add(V.scalar_tensor_tensor(prob[:, c * SEQ:(c + 1) * SEQ], const("dist"), SLOPES[i],
                                                  bank[5][:, c * SEQ:(c + 1) * SEQ], ALU.mult, ALU.add))
                for c in range(2):
                    st.add(V.scalar_tensor_tensor(prob[:, 512 + c * P:512 + (c + 1) * P], const("dist")[:, P:2 * P], SLOPES[i],
                                                  bank[6][:, c * P:(c + 1) * P], ALU.mult, ALU.add))
                st.wait()
                st.do(V.tensor_reduce(nmax[:, 0:2], prob[:, 0:512].rearrange("p (c k) -> p c k", c=2), AX.X, ALU.max, negate=True))
                V.tensor_reduce(nmax[:, 2:4], prob[:, 512:768].rearrange("p (c k) -> p c k", c=2), AX.X, ALU.max, negate=True
                                ).then_inc(biased, 1)

            def difference(i):
                dve.wait_ge(exped, 4 * (i + 1))
                if i >= 1:
                    dve.wait_ge(diff_T, i)
                st.do(V.reciprocal(rsum, esum))
                st.do(V.tensor_scalar(rsum[:, 1:2], rsum[:, 1:2], lamv[:, 3:4], None, ALU.mult))
                st.do(V.tensor_scalar(rsum[:, 3:4], rsum[:, 3:4], lamv[:, 3:4], None, ALU.mult))
                st.add(V.tensor_scalar(diff[:, 0:256], prob[:, 0:256], rsum[:, 0:1], None, ALU.mult))
                st.do(V.tensor_scalar(diff[:, 256:384], prob[:, 512:640], rsum[:, 2:3], None, ALU.mult))
                st.add(V.scalar_tensor_tensor(diff[:, 0:256], prob[:, 256:512], rsum[:, 1:2], diff[:, 0:256], ALU.mult, ALU.add))
                V.scalar_tensor_tensor(diff[:, 256:384], prob[:, 640:768], rsum[:, 3:4], diff[:, 256:384], ALU.mult, ALU.add
                                       ).then_inc(diffed, 1)

            def conv_input(i):
                n = BCX + 3 * i + 1
                dve.wait_ge(tile_done, n + 1)
                dve.wait_ge(c_copied, i + 1)
                V.tensor_tensor(upad[:, 2:T + 2], ctmp, bank[n % 3][:, 0:T], ALU.mult).then_inc(u_ready, 1)
                dve.wait_ge(u_ready, i + 1)
                tap = [convwT[:, j * CT + i:j * CT + i + 1] for j in range(3)]
                st.add(V.tensor_scalar(conv[:, 0:SEQ], upad[:, 0:SEQ], tap[0], None, ALU.mult))
                st.do(V.tensor_scalar(conv[:, SEQ:T], prev[:, :, 0, i], tap[0], None, ALU.mult))
                st.add(V.scalar_tensor_tensor(conv[:, 0:SEQ], upad[:, 1:SEQ + 1], tap[1], conv[:, 0:SEQ], ALU.mult, ALU.add))
                st.do(V.scalar_tensor_tensor(conv[:, SEQ:T], prev[:, :, 1, i], tap[1], conv[:, SEQ:T], ALU.mult, ALU.add))
                st.do(V.scalar_tensor_tensor(conv, upad[:, 2:T + 2], tap[2], conv, ALU.mult, ALU.add))
                st.add(V.tensor_copy(out[:, :, i], upad[:, SEQ:T + 2]))

            def conv_output(i):
                n = BCX + 3 * i + 2
                dve.wait_ge(tile_done, n + 1)
                if i == 3:
                    for x in range(2):
                        dve.wait_ge(stored[x], STORED[x])
                V.tensor_tensor(cat[:, CT + i, :], conv, bank[n % 3][:, 0:T], ALU.mult).then_inc(conv_ready, 1)

            def self_scores():
                st.do(V.memset(selfqk, 0.0))
                for c in range(2):
                    q = slice(c * HALF, (c + 1) * HALF)
                    ins_ = V.tensor_tensor(selfqk[q, c * H * NB:(c + 1) * H * NB].rearrange("p (h b) -> p h b", h=H),
                                           qkT[q, 0:H, SEQ:T], qkT[q, H:2 * H, SEQ:T], ALU.mult)
                    if c == 0:
                        st.do(ins_)
                    else:
                        ins_.then_inc(self_ready, 1)

            def sample_max():
                dve.wait_ge(s_T, 1)
                st.add(V.scalar_tensor_tensor(rowsc[:, 0:PAST], const("kpos"), const("slope"), bank[5][:, 0:PAST], ALU.mult, ALU.add))
                st.do(V.tensor_copy(rowsc[:, PAST:PAST + 1], bank[6][:, 0:1]))
                V.tensor_reduce(nmax[:, 0:1], rowsc, AX.X, ALU.max, negate=True).then_inc(s_biased, 1)
                dve.wait_ge(s_exped, 1)
                st.do(V.reciprocal(rsum[:, 0:1], esum[:, 0:1]))
                st.do(V.tensor_tensor(rsum[:, 0:1], rsum[:, 0:1], lamv[:, 0:1], ALU.mult))
                st.do(V.tensor_scalar(rowsc, rowsc, rsum[:, 0:1], None, ALU.mult))
                V.tensor_scalar(selfsel, const("sel"), rowsc[:, PAST:PAST + 1], None, ALU.mult).then_inc(s_probs, 1)
                st.do(V.memset(pairw, 0.0))

            def sample_weights():
                dve.wait_ge(s_pair, 1)
                st.add(V.tensor_tensor(selfsel, bank[6][:, 2 * H * NB:3 * H * NB], vTs, ALU.mult))
                V.tensor_copy(pairw[:, :, :, 0:H].rearrange("p g b h -> p g h b"),
                              bank[6][:, 0:2 * H * NB].rearrange("p (g h b) -> p g h b", g=NPG, h=H)).then_inc(s_pair_copied, 1)

            def sample_copy():
                for x in range(2):
                    dve.wait_ge(stored[x], STORED[x])
                for r in range(2):
                    dve.wait_ge(s_pv, 2 * (r + 1))
                    for half in range(2):
                        V.tensor_copy(pvrows[:, r, half * 512:(half + 1) * 512], bank[((4, 5), (7, 6))[r][half]][:, :]
                                      ).then_inc(s_pv_copied, 1)

            def sample_whole():
                dve.wait_ge(s_picked, 2)
                st.wait()
                V.tensor_tensor(osamp[:, 0:H * NB], selfsel, bank[3][:, 0:H * NB], ALU.add).then_inc(s_whole, 1)

            for n in range(NIN):
                if 1 <= n <= 2 * H:
                    normalise(n - 1)
                if n == 2 * H + 1:
                    st.add(V.memset(upad[:, 0:2], 0.0))
                    dve.wait_ge(raw_copied, 1)
                    dve.wait_ge(qk_ready, 2 * H)
                    self_scores()
                h, stage = divmod(n - HEAD0, 3)
                if stage == 0:
                    if 0 <= h < H:
                        bias_scores(h)
                    if 1 <= h <= H:
                        head_out(h - 1)
                    if 0 <= h < H:
                        difference(h)
                if n >= BCX and (n - BCX) % 3 == 1:
                    conv_input((n - BCX) // 3)
                if n >= BCX and (n - BCX) % 3 == 2:
                    i = (n - BCX) // 3
                    conv_output(i)
                    for j in range(PAGES_BY[i], PAGES_BY[i + 1]):
                        page(j)
                if n == SAMPLE0:
                    sample_max()
                if n == SAMPLE0 + 1:
                    sample_weights()
                if n == SAMPLE0 + 2:
                    sample_copy()
                if n == SAMPLE0 + 3:
                    sample_whole()
            dve.wait_ge(conv_ready, CT)
            st.wait()
            V.tensor_copy(lamv[:, 1:2], lamv[:, 0:1]).then_inc(stash_ready, 1)
            dve.wait_ge(o_rooted, H + 1)
            st.do(V.reciprocal(ord_[:, 0:H * NB], ord_[:, 0:H * NB]))
            V.scalar_tensor_tensor(cat[:, 0:H, SEQ:T], osamp.rearrange("p (h b) -> p h b", h=H), gsub[:, 1:2],
                                   ord_[:, 0:H * NB].rearrange("p (h b) -> p h b", h=H), ALU.mult, ALU.mult).then_inc(o_ready, 1)

            dve.wait_ge(x2_zero, 1)
            arrived(dve, ("XT", 0))
            xT = ring[:, front_at[("XT", 0)][0], :].rearrange("p (k t) -> p k t", k=KT)
            for j in range(KT + 1):
                if j < KT:
                    n = TILE_AT[("W", j)]
                    dve.wait_ge(tile_done, n + 1)
                    if j >= 2:
                        dve.wait_ge(y_T, j - 1)
                    V.tensor_tensor(yT[j % 2][:, 0:SEQ], xT[:, j, :], bank[n % 3][:, 0:SEQ], ALU.add)
                    V.tensor_tensor(yT[j % 2][:, SEQ:T], xsT[:, j, :], bank[n % 3][:, SEQ:T], ALU.add).then_inc(y_copied, 1)
                if j >= 1:
                    dve.wait_ge(y_T, j)
                    b = bank[3 + (j - 1) % 2]
                    cols = slice((j - 1) * P, j * P)
                    V.tensor_copy(xa[:, 0:2, cols], b[:, 0:2 * P].rearrange("p (t c) -> p t c", t=2))
                    V.tensor_copy(xa[0:NB, 2, cols], b[0:NB, 2 * P:3 * P]).then_inc(y_added, 1)
            dve.wait_ge(sums2, KT)
            V.tensor_reduce(ssum[:, 0:TT].unsqueeze(2), ssq, AX.X, ALU.add).then_inc(ssq_sum, 1)
            dve.wait_ge(sqrt2, 1)
            st.do(V.reciprocal(srstd[:, 0:TT], srstd[:, 0:TT]))

            def rows_of(x, n):
                return x.unsqueeze(1).to_broadcast([P, TT, n])

            dve.wait_ge(late_in, 16)
            st.add(V.memset(logits, FAR))
            st.do(V.memset(bothf, 0.0))
            dve.wait_ge(router, 1)
            dve.wait_ge(wr_in, 64)
            for t in range(TT):
                n = P if t < 2 else NB
                st.add(V.scalar_tensor_tensor(logits[0:n, t, :], bank[5][0:n, t * RE:(t + 1) * RE],
                                              srstd[0:n, t:t + 1], rbias[0:n, :], ALU.mult, ALU.add))
            st.wait()

            def top(x, best, idx, at):
                for t in range(TT):
                    st.add(V.max(best[:, t, :], x[:, t, :]))
                st.wait()
                for t in range(TT):
                    st.add(V.max_index(idx[:, t, :], best[:, t, :], x[:, t, :]))
                st.wait()
                st.do(V.tensor_copy(at, idx))

            lg, le = logits[:, :, 0:GROUPS], logits[:, :, RG:]
            top(logits[:, :, 0:RG], gtop, gidx, gat)
            st.add(V.tensor_tensor(gex, lg, gtop[:, :, 0:1].to_broadcast([P, TT, GROUPS]), ALU.subtract))
            st.do(V.tensor_tensor(goh, rows_of(late("iota")[:, 0:GROUPS], GROUPS), gat[:, :, 0:1].to_broadcast([P, TT, GROUPS]),
                                  ALU.is_equal))
            st.do(V.tensor_scalar(geneg, goh, -1.0, -FAR, ALU.add, ALU.mult))
            for t in range(TT):
                st.add(V.tensor_tensor(lem[:, t, :].rearrange("p (g e) -> p g e", g=GROUPS),
                                       le[:, t, :].rearrange("p (g e) -> p g e", g=GROUPS),
                                       geneg[:, t, :].unsqueeze(2).to_broadcast([P, GROUPS, EPG]), ALU.add))
            st.wait()
            top(lem, etop, eidx, eat)
            V.tensor_tensor(ew, etop[:, :, 1:2], etop[:, :, 0:1], ALU.subtract).then_inc(gex_ready, 1)
            iota_e = rows_of(late("iota")[:, 0:NE], NE)
            st.add(V.tensor_tensor(oh1, iota_e, eat[:, :, 0:1].to_broadcast([P, TT, NE]), ALU.is_equal))
            st.do(V.tensor_tensor(oh2, iota_e, eat[:, :, 1:2].to_broadcast([P, TT, NE]), ALU.is_equal))
            st.do(V.tensor_tensor(both, oh1, oh2, ALU.add))
            V.tensor_tensor(both, both, const("valid").unsqueeze(2).to_broadcast([P, TT, NE]), ALU.mult).then_inc(assigned, 1)
            dve.wait_ge(gexed, 2)
            st.add(V.tensor_reduce(gs, gex, AX.X, ALU.add))
            st.do(V.tensor_scalar(w_n, ew, 1.0, None, ALU.add))
            st.do(V.tensor_tensor(w_n, w_n, gs, ALU.mult))
            st.do(V.reciprocal(w1.unsqueeze(2), w_n))
            st.do(V.tensor_tensor(w2.unsqueeze(2), w1.unsqueeze(2), ew, ALU.mult))
            dve.wait_ge(ranked, 1)
            st.add(V.tensor_tensor(slotmap, bank[3][:, 0:TT * NE].rearrange("p (t e) -> p t e", t=TT),
                                   rows_of(late("base"), NE), ALU.add))
            exc4 = exc.rearrange("p t (e m) -> p (t e) m", m=MAXPASS)
            st.do(V.tensor_tensor(exc4, bank[3][:, 0:TT * NE].unsqueeze(2).to_broadcast([P, TT * NE, MAXPASS]),
                                  const("kth").unsqueeze(1).to_broadcast([P, TT * NE, MAXPASS]), ALU.is_ge))
            st.do(V.tensor_reduce(work.rearrange("p t e -> p (t e)").unsqueeze(2), exc4, AX.X, ALU.add))
            st.do(V.tensor_scalar(work, work, -1.0, float(PASS_SLOTS - C), ALU.add, ALU.mult))
            st.do(V.tensor_tensor(slotmap, slotmap, work, ALU.add))
            st.add(V.tensor_tensor(oh1, oh1, slotmap, ALU.mult))
            st.do(V.tensor_tensor(oh2, oh2, slotmap, ALU.mult))
            st.add(V.tensor_reduce(pos1.unsqueeze(2), oh1, AX.X, ALU.add))
            st.add(V.tensor_reduce(pos2.unsqueeze(2), oh2, AX.X, ALU.add))
            st.do(V.tensor_reduce(cmax, bank[3][:, TT * NE:(TT + 1) * NE], AX.X, ALU.max))
            st.do(V.tensor_scalar(cwork, const("kth"), cmax, None, ALU.is_lt))
            st.do(V.tensor_reduce(cpass, cwork, AX.X, ALU.add))
            V.memset(esum[:, 0:1], 0.0).then_inc(mix_added[2], 2)
            V.tensor_copy(npass_sb[0:1, 0:1], cpass[0:1, :]).then_inc(routed, 1)
            dve.wait_ge(routed, 1)

            npass = dve.value_load(npass_sb[0:1, 0:1], min_val=1, max_val=MAXPASS)
            before = st.n
            with dve.Fori(0, npass) as r:
                with dve.Fori(0, NG) as g:
                    it = r * NG + g
                    st.base = it * LOOP_STEPS
                    iota = late("iota")
                    for t in range(TT):
                        st.add(V.tensor_scalar(gateT[:, t, :], iota, pos2[:, t:t + 1], None, ALU.is_equal))
                        st.add(V.tensor_scalar(gate[:, t, :], iota, pos1[:, t:t + 1], w1[:, t:t + 1], ALU.is_equal, ALU.mult))
                        st.add(V.tensor_scalar(sel[:, t, :], iota, pos1[:, t:t + 1], srstd[:, t:t + 1], ALU.is_equal, ALU.mult))
                    st.wait()
                    for t in range(TT):
                        ins_ = V.scalar_tensor_tensor(sel[:, t, :], gateT[:, t, :], srstd[:, t:t + 1], sel[:, t, :], ALU.mult, ALU.add)
                        if t < TT - 1:
                            st.add(ins_)
                        else:
                            ins_.then_inc(sel_ready, 1)
                    for t in range(TT):
                        ins_ = V.scalar_tensor_tensor(gate[:, t, :], gateT[:, t, :], w2[:, t:t + 1], gate[:, t, :], ALU.mult, ALU.add)
                        if t < TT - 1:
                            st.add(ins_)
                        else:
                            ins_.then_inc(gate_ready, 1)
                    st.wait()
                    dve.wait_ge(sel_ready, it + 1)
                    dve.wait_ge(gate_ready, it + 1)
                    st.do(V.tensor_scalar(route[:, 0:2 * TT], route[:, 0:2 * TT], -float(P), None, ALU.add))
                    for q in range(4):
                        dve.wait_ge(gathered, it * 4 + (q + 1))
                        V.tensor_tensor(xeT[:, 4 * q:4 * q + 4, :], bank[4 + q % 2][:, :].rearrange("p (k s) -> p k s", k=4),
                                        gffn[:, 4 * q:4 * q + 4].unsqueeze(2).to_broadcast([P, 4, P]), ALU.mult).then_inc(xe_ready, 1)
                    for j in range(EG):
                        dve.wait_ge(u_done, it * EG + (j + 1))
                        V.tensor_copy(u_sb, bank[1][:, :]).then_inc(u_copied, 1)
                        dve.wait_ge(silu_done, it * EG + (j + 1))
                        V.tensor_tensor(actT, actT, bank[3][:, P:2 * P].rearrange("p (c s) -> p c s", c=FC), ALU.mult
                                        ).then_inc(act_ready, 1)
                        dve.wait_ge(down_done, it * EG + (j + 1))
                        for n in range(2, 4):
                            V.tensor_copy(ye[j * C:(j + 1) * C, n * 512:(n + 1) * 512], bank[2][n * C:(n + 1) * C, :]
                                          ).then_inc(ye_dve, 1)
                    for t in range(TT):
                        n_rows = P if t < 2 else NB
                        for n in range(4):
                            m = t * 4 + n
                            cols = slice(n * 512, (n + 1) * 512)
                            dve.wait_ge(mixed, it * (4 * TT) + (m + 1))
                            V.tensor_tensor(xa[0:n_rows, t, cols], xa[0:n_rows, t, cols], bank[6 + m % 2][0:n_rows, :], ALU.add
                                            ).then_inc(mix_added[t], 1)
            assert st.n - before == LOOP_STEPS, st.n - before

        @block.gpsimd
        def _(pool):
            G = nc.gpsimd
            G.memset(xa[:, 2, :], 0.0).then_inc(x_clear, 1)
            pool.wait_ge(x_clear, 1)
            xs = ins["x_sample"].rearrange("b o d -> b (o d)")
            pool.dma_start(xa[0:NB, 2, :], xs).then_inc(x_in[2], 16)
            pool.dma_start(outs["conv_sample"][0, :, 0, :], ins["state_conv"][0, :, 1, :]).then_inc(state_stored, 16)

            pool.wait_ge(h_T, KT)
            G.memset(qz, 0.0).then_inc(qz_zero, 1)
            pool.wait_ge(qz_zero, 1)
            def split_q(h):
                pool.wait_ge(qk_ready, h + 1)
                if h >= 1:
                    pool.wait_ge(scores, h)
                G.tensor_copy(qz[0:HALF, 0, :], qkT[0:HALF, h, 0:SEQ]).then_inc(qz_zero, 1)
                pool.wait_ge(qz_zero, h + 2)
                G.tensor_copy(qz[HALF:P, 1, :], qkT[HALF:P, h, 0:SEQ]).then_inc(qz_ready, 1)
                pool.wait_ge(qz_ready, h + 1)

            def multiply_page(j):
                b = j // NPG
                if j % PPU == 0:
                    arrived(pool, ("KP", j // PPU))
                if b % 4 == 0 and j % NPG == 0:
                    arrived(pool, ("QB", b // 4))
                s, _ = front_at[("KP", j // PPU)]
                sq_, _ = front_at[("QB", b // 4)]
                kp = ring[:, s, (j % PPU) * ATT:(j % PPU + 1) * ATT]
                G.tensor_tensor(kp, kp, ring[:, sq_, (b % 4) * ATT:(b % 4 + 1) * ATT], ALU.mult).then_inc(page_mul, 1)

            for n in range(HEAD0 - 3, NIN, 3):
                h, i = (n + 3 - HEAD0) // 3, (n - BCX) // 3
                if h < H:
                    split_q(h)
                if i >= 0:
                    for j in range(PAGES_BY[i], PAGES_BY[i + 1]):
                        multiply_page(j)
                    if PAGES_AT[i]:
                        pool.wait_ge(page_mul, PAGES_BY[i + 1])

            pool.wait_ge(scores, H)
            pool.wait_ge(self_ready, 1)
            G.memset(wrv, 0.0).then_inc(wr_zero, 1)
            G.memset(rbias, FAR).then_inc(wr_zero, 1)
            pool.wait_ge(wr_zero, 2)
            pool.dma_start(wrv[:, :, 0:GROUPS], ins["w_router_group"].rearrange("l (k p) e -> (l p) k e", p=P)).then_inc(wr_in, 16)
            pool.dma_start(wrv[:, :, RG:], ins["w_router_expert"].rearrange("l (k p) e -> (l p) k e", p=P)).then_inc(wr_in, 16)
            pool.dma_start(rbias[:, 0:GROUPS], ins["b_router_group"].partition_broadcast(P).rearrange("p l e -> p (l e)")
                           ).then_inc(wr_in, 16)
            pool.dma_start(rbias[:, RG:], ins["b_router_expert"].partition_broadcast(P).rearrange("p l e -> p (l e)")
                           ).then_inc(wr_in, 16)
            pool.wait_ge(wr_in, 64)
            G.tensor_tensor(wrv, wrv, gffnT.unsqueeze(2).to_broadcast([P, KT, RE]), ALU.mult).then_inc(wr_ready, 1)
            pool.wait_ge(o_ready, H + 1)
            G.memset(xa[:, 2, :], 0.0).then_inc(x2_zero, 1)
            pool.dma_start(consts[:, late0:late0 + 512], ins["late"]).then_inc(late_in, 16)
            pool.wait_ge(tile_done, NIN)
            G.memset(h2[:, 2, :], 0.0).then_inc(h2_zero, 1)
            pool.wait_ge(h2_zero, 1)
            for j in range(KT):
                pool.wait_ge(y_added, j + 1)
                cols = slice(j * P, (j + 1) * P)
                G.tensor_copy(h2[:, 0:2, cols], xa[:, 0:2, cols]).then_inc(h2_ready, 1)
                G.tensor_copy(h2[0:NB, 2, cols], xa[0:NB, 2, cols]).then_inc(h2_ready, 1)

    return nc


VECS = 14
STORED = (16 * 4 + 32 * 8, 16 * 4 + 32 * 8)
LOOP_STEPS = 3 * TT + 2 * (TT - 1) + 1


def _constants():
    import numpy as np

    c = np.zeros((P, NCONST), np.float32)

    def put(name, x):
        a, b = CONST_AT[name]
        c[:, a:b] = x

    r = np.arange(P)
    put("ident", np.eye(P))
    put("ones", 1.0)
    put("fold", np.tile(np.eye(C), (EG, 1)))
    put("blk", np.kron(np.eye(2), np.ones((HALF, HALF))) / HALF)
    put("sel", np.tile(np.eye(H * NB), (2, 1)))
    back = P + r[:, None] - np.arange(SEQ)[None, :]
    put("dist", np.where(back >= 0, -back, FAR))
    put("kpos", np.arange(PAST)[None, :] - PAST)
    put("slope", np.tile(np.repeat(SLOPES, NB), 2)[:, None])
    put("neg_c1", -(r >= HALF)[:, None].astype(np.float32))
    put("c0", (r < HALF)[:, None])
    put("valid", np.stack([r >= 0, r >= 0, r < NB], 1))
    put("kth", C * np.arange(MAXPASS)[None, :])
    put("eps", EPS)
    late = np.zeros((P, 512), np.float32)

    def put_late(name, x):
        a, b = LATE_AT[name]
        late[:, a:b] = x

    put_late("iota", r[None, :])
    put_late("tri", (r[:, None] < r[None, :]))
    put_late("base", C * np.arange(NE)[None, :])
    return {"consts": c, "late": late}


_OUTS = [("y_prompt", (1, SEQ, D)), ("y_sample", (NB, 1, D)), ("k_prompt", (1, 1, SEQ, H, HD)),
         ("v_prompt", (1, 1, SEQ, H, HD)), ("conv_prompt", (1, 1, 2, CONV)), ("k_sample", (1, NB, 1, H, HD)),
         ("v_sample", (1, NB, 1, H, HD)), ("conv_sample", (1, NB, 2, CONV))]


def kernel(**inputs):
    import numpy as np
    import concourse.bacc as bacc
    from concourse.bass_utils import run_bass_kernel_spmd

    nc = bacc.Bacc("TRN2", target_bir_lowering=False, num_devices=1)
    arrays = {name: np.ascontiguousarray(a) for name, a in {**inputs, **_constants()}.items()}
    ins = {name: nc.dram_tensor(f"in_{name}", a.shape, mybir.dt.from_np(a.dtype), kind="ExternalInput").ap()
           for name, a in arrays.items()}
    outs = {name: nc.dram_tensor(f"out_{name}", shape, F32, kind="ExternalOutput").ap() for name, shape in _OUTS}
    build(nc, ins, outs)
    r = run_bass_kernel_spmd(nc, [{f"in_{name}": a for name, a in arrays.items()}], core_ids=[0])
    return tuple(r.results[0][f"out_{name}"] for name, _ in _OUTS)
```

```python
from contextlib import ExitStack

import concourse.bass as bass
from concourse import mybir

F32 = mybir.dt.float32
I32 = mybir.dt.int32
ALU = mybir.AluOpType
ACT = mybir.ActivationFunctionType
AX = mybir.AxisListType

P = 128
D = 2048
KT = D // P
SEQ = 256
NB = 8
T = SEQ + NB
TT = 3
H = 8
HD = 128
HALF = HD // 2
ATT = H * HD
CONV = D - ATT
CT = CONV // P
PAST = 256
PAGE = 128
NPG = PAST // PAGE
GROUPS = 4
EPG = 8
NE = GROUPS * EPG
F = D // 4
FC = F // P
EPS = 1e-6
LAM_INIT = 0.8 - 0.6
FAR = -1e30

SLOTS = 8
UNIT = 4096
UC = UNIT // KT
TPU = UC // P

EG = 4
C = P // EG
NG = NE // EG
MAXPASS = -(-T // C)
UPE = 6
UPG = UPE * EG
RG = 8
RE = RG + NE

FRONT = ([("q", u) for u in range(4)] + [("k", u) for u in range(4)] + [("v", u) for u in range(4)]
         + [("C", 0), ("X", 0), ("B", 0), ("QB", 0), ("KP", 0), ("KP", 1),
            ("C", 1), ("X", 1), ("B", 1), ("QB", 1), ("KP", 2),
            ("C", 2), ("X", 2), ("B", 2), ("KP", 3),
            ("C", 3), ("X", 3), ("B", 3)]
         + [("VP", u) for u in range(4)] + [("W", u) for u in range(8)])
NFRONT = len(FRONT)
COLUMN = {"q": 0, "k": ATT, "v": 2 * ATT, "B": 3 * ATT, "C": 3 * ATT + CONV, "X": 3 * ATT + 2 * CONV}
TILES = ([("q", h) for h in range(H)] + [("k", h) for h in range(H)] + [("v", h) for h in range(H)]
         + [(c, i) for i in range(CT) for c in "CXB"] + [("W", j) for j in range(KT)])
TILE_AT = {t: n for n, t in enumerate(TILES)}
BCX = 3 * H
PAGES_AT = [3, 3, 3, 3, 2, 2, 0, 0]
PAGES_BY = [sum(PAGES_AT[:i]) for i in range(CT + 1)]
NPAGES = NB * NPG
NIN = BCX + 3 * CT
HEAD0 = 2 * H + 2
SAMPLE0 = HEAD0 + 3 * H
PPU = 4

CONSTS = [("ident", P), ("ones", P), ("fold", C), ("blk", P), ("sel", H * NB), ("dist", SEQ), ("kpos", PAST),
          ("slope", 1), ("neg_c1", 1), ("c0", 1), ("valid", TT), ("kth", MAXPASS), ("eps", 1)]
CONST_AT, _n = {}, 0
for _name, _w in CONSTS:
    CONST_AT[_name] = (_n, _n + _w)
    _n += _w
NCONST = _n
LATE = [("iota", P), ("tri", P), ("base", NE), ("spare", 512 - 2 * P - NE)]
LATE_AT, _n = {}, 0
for _name, _w in LATE:
    LATE_AT[_name] = (_n, _n + _w)
    _n += _w
SLOPES = [2.0 ** (-8.0 * (h + 1) / H) for h in range(H)]

MIX_ORDER = [(0, 0), (0, 1), (1, 0), (1, 1), (2, None), (0, 2), (0, 3), (1, 2), (1, 3)]
MIXES = len(MIX_ORDER)
AHEAD = 4

XBANKS = (3, 4, 5, 6, 1)


class Steps:

    def __init__(self, eng, sem):
        self.eng, self.sem, self.n, self.base = eng, sem, 0, 0

    def add(self, ins):
        ins.then_inc(self.sem, 1)
        self.n += 1

    def wait(self):
        self.eng.wait_ge(self.sem, self.base + self.n)

    def do(self, ins):
        self.add(ins)
        self.wait()


def build(nc, ins, outs):
    ctx = ExitStack()
    with ctx:
        def sb(name, shape, dt=F32):
            return ctx.enter_context(nc.sbuf_tensor(name, shape, dt))

        def sem(name):
            return ctx.enter_context(nc.semaphore(name))

        ring = sb("ring", [P, SLOTS, UNIT])
        xa = sb("xa", [P, TT, D])
        bc = sb("bc", [P, 2 * KT * T])
        cat = sb("cat", [P, KT, T])
        consts = sb("consts", [P, NCONST])
        small = sb("small", [P, 544])
        gains = sb("gains", [P, KT])
        pages = sb("pages", [1, NPAGES], I32)
        npass_sb = sb("npass_sb", [1, 1], I32)
        xT_dram = nc.dram_tensor("xT_scratch", [P, 2, KT, P], F32).ap()
        qrows_dram = nc.dram_tensor("qrows_scratch", [NB, ATT], F32).ap()

        bank = [ctx.enter_context(nc.psum_tensor(f"bank{i}", [P, 512], F32)) for i in range(8)]

        def x_bank(k):
            return bank[XBANKS[k % len(XBANKS)]]

        def const(name):
            a, b = CONST_AT[name]
            return consts[:, a:b]

        late0 = CONST_AT["dist"][0]

        def late(name):
            a, b = LATE_AT[name]
            return consts[:, late0 + a:late0 + b]

        ident = const("ident")

        hT = bc[:, 0:KT * T].rearrange("p (k t) -> p k t", t=T)
        qkT = bc[:, KT * T:].rearrange("p (k t) -> p k t", t=T)
        vrow = xa[:, 0, :].rearrange("p (t c) -> p t c", t=2)
        qrows = xa[0:NB, 0, 0:ATT]
        tmp = xa[:, 1:3, :].rearrange("p a n -> p (a n)")
        prob = tmp[:, 0:768]
        qz = tmp[:, 768:1280].rearrange("p (c q) -> p c q", c=2)
        osq = tmp[:, 1296:1552]
        ord_ = tmp[:, 1560:1816]
        sq = [tmp[:, 1296 + T * i:1296 + T * i + T] for i in range(2)]
        diff = tmp[:, 1824:2208]
        diffT = tmp[:, 2208:2592]
        rstd = [tmp[:, 1824 + T * i:1824 + T * i + T] for i in range(2)]
        ctmp = tmp[:, 2592:2592 + T]
        upad = tmp[:, 2856:2856 + T + 2]
        conv = tmp[:, 3122:3122 + T]
        keysc = tmp[:, 3386:3642].rearrange("p (g c h b) -> p g c h b", g=NPG, c=2, h=H)
        rowsc = tmp[:, 3642:3642 + PAST + 1]
        selfqk = tmp[:, 3902:4030]
        selfsel = tmp[:, 4030:4094]
        pairw = tmp[:, 0:512].rearrange("p (g b c) -> p g b c", g=NPG, b=NB)
        pvrows = xa[:, 0, 0:ATT]
        vT = [cat[:, 14 + i, :] for i in range(2)]
        kvstage = [cat[:, 11:14, :].rearrange("p k t -> p (k t)")[:, 384 * i:384 * i + 384] for i in range(2)]
        osamp = tmp[:, 512:512 + H * NB]

        o = [0]

        def piece(n):
            o[0] += n
            return small[:, o[0] - n:o[0]]

        rawT = piece(3 * CT + 2 * KT)
        convwT = rawT[:, 0:3 * CT]
        gffnT = rawT[:, 3 * CT:3 * CT + KT]
        prevT = piece(NB * 2 * CT)
        stash = piece((2 + NB) * CT)
        vTs = piece(H * NB)
        ssum = piece(4)
        srstd = piece(4)
        lamv = piece(4)
        nmax = piece(4)
        esum = piece(4)
        rsum = piece(4)
        gqk = piece(2)
        gsub = piece(2)
        route = piece(4 * TT)
        xsT = piece(KT * NB).rearrange("p (k b) -> p k b", k=KT)
        ssq = piece(TT * KT).rearrange("p (t k) -> p t k", t=TT)
        gmix = rawT[:, 3 * CT + KT:]
        gffn = gains[:, :]

        rawrows = ring[:, SLOTS - 1, 0:256]
        lamraw = ring[:, SLOTS - 1, 256:256 + 4 * HALF]
        lamprod = ring[:, SLOTS - 1, 512:512 + HALF]
        sqjunk = ring[:, SLOTS - 2, 0:D]
        spread = ring[:, SLOTS - 2, D:D + TT * P].rearrange("p (t c) -> p t c", t=TT)
        rstdB = ring[:, SLOTS - 3, D:D + T]
        sqjunk2 = ring[:, SLOTS - 3, 0:D]

        xT = bc[:, 0:2 * KT * P].rearrange("p (t k c) -> p t k c", t=2, k=KT)
        yT = [bc[:, 6144 + T * i:6144 + T * i + T] for i in range(2)]
        junk_act = [bc[:, 7808 + P * t:7808 + P * (t + 1)] for t in range(TT)]
        wrv = bc[:, 6672:6672 + KT * RE].rearrange("p (k e) -> p k e", k=KT)
        logitsT = bc[0:RE, 7312:7312 + T]
        outrows = bc[:, 7576:7704]
        rbias = bc[:, 7704:7704 + RE]
        h2 = bc[:, 0:TT * D].rearrange("p (t d) -> p t d", t=TT)
        sel = bc[:, 6144:6528].rearrange("p (t s) -> p t s", t=TT)
        gate = bc[:, 6528:6912].rearrange("p (t s) -> p t s", t=TT)
        second = [late("tri"), late("spare")[:, 0:P], const("blk")]
        gateT = bc[:, 6912:7296].rearrange("p (t s) -> p t s", t=TT)
        g_sb = bc[:, 7296:7808]
        u_sb = bc[:, 7808:8320]
        actT = bc[:, 8320:8448].rearrange("p (c s) -> p c s", c=FC)
        catf = cat[:, :, :].rearrange("p k t -> p (k t)")
        xeT = catf[:, 0:D].rearrange("p (k s) -> p k s", k=KT)
        ye = catf[:, D:2 * D]
        o[0] = 0

        def rt(n):
            o[0] += n
            return catf[:, D + o[0] - n:D + o[0]].rearrange("p (t e) -> p t e", t=TT)

        logits = rt(TT * RE)
        gs, w_n, ew = (rt(TT) for _ in range(3))
        goh, gex, geneg = (rt(TT * GROUPS) for _ in range(3))
        lem, oh1, oh2, work, slotmap = (rt(TT * NE) for _ in range(5))
        gtop, etop, gat, eat = (rt(TT * 8) for _ in range(4))
        ranki = rt(TT * NE).rearrange("p t e -> p (t e)").bitcast(I32)
        bothf = catf[:, D + o[0]:D + o[0] + 4 * NE]
        both = bothf[:, 0:TT * NE].rearrange("p (t e) -> p t e", t=TT)
        o[0] += 4 * NE
        gidx = catf[:, D + o[0]:D + o[0] + TT * 8].bitcast(mybir.dt.uint32).rearrange("p (t e) -> p t e", t=TT)
        o[0] += TT * 8
        eidx = catf[:, D + o[0]:D + o[0] + TT * 8].bitcast(mybir.dt.uint32).rearrange("p (t e) -> p t e", t=TT)
        o[0] += TT * 8
        cmax = catf[:, D + o[0]:D + o[0] + 1]
        cpass = catf[:, D + o[0] + 1:D + o[0] + 2]
        cwork = catf[:, D + o[0] + 2:D + o[0] + 2 + MAXPASS]
        assert D + o[0] + 2 + MAXPASS <= KT * T
        pos1, pos2, w1, w2 = (route[:, TT * i:TT * i + TT] for i in range(4))

        slot_full = [sem(f"slot_full{i}") for i in range(SLOTS)]
        x_in = [sem(f"x_in{i}") for i in range(TT)]
        consts_in = sem("consts_in")
        vecs_in = sem("vecs_in")
        late_in = sem("late_in")
        wr_in = sem("wr_in")
        wr_zero = sem("wr_zero")
        pages_in = sem("pages_in")
        x2_zero = sem("x2_zero")
        x_clear = sem("x_clear")
        raw_T = sem("raw_T")
        raw_copied = sem("raw_copied")
        sums1_dve = sem("sums1_dve")
        sums1 = sem("sums1")
        spread_ready = sem("spread_ready")
        factors = sem("factors")
        factors_ready = sem("factors_ready")
        xT_copied = sem("xT_copied")
        xT_stored = sem("xT_stored")
        xT_in = [sem("xT_in0"), sem("xT_in1")]
        xsT_ready = sem("xsT_ready")
        sqrt1 = sem("sqrt1")
        h_T = sem("h_T")
        h_ready = sem("h_ready")
        tile_done = sem("tile_done")
        squared = sem("squared")
        summed = sem("summed")
        rooted = sem("rooted")
        qk_ready = sem("qk_ready")
        v_copied = sem("v_copied")
        rows_T = sem("rows_T")
        rows_out = sem("rows_out")
        v_rows = sem("v_rows")
        q_stored = sem("q_stored")
        stored = [sem("stored0"), sem("stored1")]
        c_copied = sem("c_copied")
        u_ready = sem("u_ready")
        conv_ready = sem("conv_ready")
        stash_T = sem("stash_T")
        stash_out = sem("stash_out")
        stash_ready = sem("stash_ready")
        qz_ready = sem("qz_ready")
        qz_zero = sem("qz_zero")
        scores = sem("scores")
        biased = sem("biased")
        exped = sem("exped")
        diffed = sem("diffed")
        diff_T = sem("diff_T")
        diffT_copied = sem("diffT_copied")
        pv = sem("pv")
        o_squared = sem("o_squared")
        o_summed = sem("o_summed")
        o_rooted = sem("o_rooted")
        o_ready = sem("o_ready")
        page_mul = sem("page_mul")
        page_sum = sem("page_sum")
        self_ready = sem("self_ready")
        s_T = sem("s_T")
        s_biased = sem("s_biased")
        s_exped = sem("s_exped")
        s_probs = sem("s_probs")
        s_pair = sem("s_pair")
        s_pair_copied = sem("s_pair_copied")
        s_pv = sem("s_pv")
        y_copied = sem("y_copied")
        y_T = sem("y_T")
        y_added = sem("y_added")
        sums2 = sem("sums2")
        sqrt2 = sem("sqrt2")
        h2_zero = sem("h2_zero")
        h2_ready = sem("h2_ready")
        wr_ready = sem("wr_ready")
        logits_copied = sem("logits_copied")
        ssq_sum = sem("ssq_sum")
        s_pv_copied = sem("s_pv_copied")
        s_picked = sem("s_picked")
        s_whole = sem("s_whole")
        router = sem("router")
        gex_ready = sem("gex_ready")
        gexed = sem("gexed")
        assigned = sem("assigned")
        ranked = sem("ranked")
        routed = sem("routed")
        sel_ready = sem("sel_ready")
        gate_ready = sem("gate_ready")
        gathered = sem("gathered")
        xe_ready = sem("xe_ready")
        gate_T = sem("gate_T")
        gateT_copied = sem("gateT_copied")
        g_done = sem("g_done")
        u_done = sem("u_done")
        g_copied = sem("g_copied")
        u_copied = sem("u_copied")
        folded = sem("folded")
        silu_done = sem("silu_done")
        act_ready = sem("act_ready")
        unit_used = sem("unit_used")
        down_done = sem("down_done")
        ye_act = sem("ye_act")
        ye_dve = sem("ye_dve")
        mixed = sem("mixed")
        mix_added = sem("mix_added")
        xs_moved = sem("xs_moved")
        y_stored = sem("y_stored")
        state_stored = sem("state_stored")
        dve_step = sem("dve_step")
        act_step = sem("act_step")

        def slot_of(n):
            return n % SLOTS

        front_total = [0] * SLOTS
        front_at = {}
        for n, unit in enumerate(FRONT):
            front_total[slot_of(n)] += 16 * (PPU if unit[0] in ("KP", "VP") else 1)
            front_at[unit] = (slot_of(n), front_total[slot_of(n)])

        def arrived(eng, unit):
            s, value = front_at[unit]
            eng.wait_ge(slot_full[s], value)

        def used_wait(eng, n):
            kind, u = FRONT[n]
            if kind == "KP":
                eng.wait_ge(page_sum, PPU * (u + 1))
            elif kind == "QB":
                eng.wait_ge(page_mul, 8 * (u + 1))
            elif kind == "VP":
                eng.wait_ge(s_pv, u + 1)
            else:
                eng.wait_ge(tile_done, TILE_AT[(kind, TPU * u + TPU - 1)] + 1)

        block = ctx.enter_context(nc.Block())

        @block.sync
        def _(sp):
            w_in = ins["w_in"].rearrange("l (k p) n -> (l p) k n", p=P)
            w_out = ins["w_out"].rearrange("l (k p) n -> (l p) k n", p=P)
            xp = ins["x_prompt"].rearrange("o (t p) d -> (o t) p d", p=P)
            for t in range(2):
                sp.dma_start(xa[:, t, :], xp[t]).then_inc(x_in[t], 16)
            sp.dma_start(pages[:, :], ins["page_table"].rearrange("(o b) g -> o (b g)", o=1)).then_inc(pages_in, 16)

            n_vecs = [0]

            def vec(dst, src):
                sp.dma_start(dst, src).then_inc(vecs_in, 16)
                n_vecs[0] += 1

            vec(rawrows[3 * CT + KT:3 * CT + 2 * KT, 0:P], ins["norm_mix"].rearrange("l (k p) -> (l k) p", p=P))
            vec(gffn, ins["norm_ffn"].rearrange("l (p k) -> (l p) k", k=KT))
            for c in range(2):
                vec(gqk[c * HALF:(c + 1) * HALF, 0:1], ins["g_q"].rearrange("l (d o) -> (l d) o", o=1))
                vec(gqk[c * HALF:(c + 1) * HALF, 1:2], ins["g_k"].rearrange("l (d o) -> (l d) o", o=1))
            vec(gsub[:, 0:1], ins["g_sub"].rearrange("l (d o) -> (l d) o", o=1))
            for i, name in enumerate(("lam_q1", "lam_k1", "lam_q2", "lam_k2")):
                vec(lamraw[:, i * HALF:(i + 1) * HALF], ins[name].partition_broadcast(P).rearrange("p l d -> p (l d)"))
            vec(rawrows[3 * CT:3 * CT + KT, 0:P], ins["norm_ffn"].rearrange("l (k p) -> (l k) p", p=P))
            vec(rawrows[0:3 * CT, 0:P], ins["conv_w"].rearrange("l j (i p) -> (l j i) p", p=P))
            vec(rawrows[:, P:2 * P], ins["state_conv"].rearrange("l b j (i p) -> (l b j i) p", p=P))
            assert n_vecs[0] == VECS

            sp.wait_ge(vecs_in, VECS * 16)
            sp.wait_ge(consts_in, 16)
            for n, (kind, u) in enumerate(FRONT):
                s = slot_of(n)
                if n == SLOTS - 3:
                    sp.wait_ge(h_ready, KT)
                    sp.wait_ge(act_step, 1)
                if n >= SLOTS:
                    used_wait(sp, n - SLOTS)
                if kind == "W":
                    sp.dma_start(ring[:, s, :].rearrange("p (k c) -> p k c", k=KT),
                                 w_out[:, :, u * UC:(u + 1) * UC]).then_inc(slot_full[s], 16)
                elif kind == "QB":
                    sp.wait_ge(q_stored, 16)
                    sp.dma_start(ring[:, s, :].rearrange("p (b c) -> p b c", b=4),
                                 qrows_dram[4 * u:4 * u + 4, :].partition_broadcast(P)).then_inc(slot_full[s], 16)
                elif kind in ("KP", "VP"):
                    if (kind, u) == ("KP", 0):
                        sp.wait_ge(pages_in, 16)
                    pool_rows = ins["cache_k" if kind == "KP" else "cache_v"].rearrange("l n s h c -> (l n) s (h c)")
                    for i in range(PPU):
                        j = u * PPU + i
                        page = sp.value_load(pages[0:1, j:j + 1], min_val=0, max_val=pool_rows.shape[0] - 1)
                        sp.dma_start(ring[:, s, i * ATT:(i + 1) * ATT],
                                     pool_rows[bass.ds(page, 1), :, :].rearrange("o s c -> s (o c)")
                                     ).then_inc(slot_full[s], 16)
                else:
                    c0 = COLUMN[kind] + u * UC
                    sp.dma_start(ring[:, s, :].rearrange("p (k c) -> p k c", k=KT),
                                 w_in[:, :, c0:c0 + UC]).then_inc(slot_full[s], 16)

            wg = ins["w_gate"].rearrange("l (g j) (p k) f -> (l g) p j (k f)", j=EG, k=KT)
            wu = ins["w_up"].rearrange("l (g j) (p k) f -> (l g) p j (k f)", j=EG, k=KT)
            wd = ins["w_down"].rearrange("l (g j) (p k) d -> (l g) p j k d", j=EG, k=FC)

            def stream_unit(g, j, i, s):
                half = i % 2
                if i < 4:
                    src = (wg, wu)[i // 2][bass.ds(g, 1), :, j, half * UNIT:(half + 1) * UNIT].rearrange("o p n -> p (o n)")
                    sp.dma_start(ring[:, s, :], src).then_inc(slot_full[s], 16)
                else:
                    src = wd[bass.ds(g, 1), :, j, :, half * (D // 2):(half + 1) * (D // 2)].rearrange("o p k d -> p (o k) d")
                    sp.dma_start(ring[:, s, :].rearrange("p (k d) -> p k d", k=FC), src).then_inc(slot_full[s], 16)

            def expert_used(m, it):
                j, i = divmod(m, UPE)
                if i % 2 == 0:
                    sp.wait_ge(unit_used, it * (3 * EG) + (3 * j + i // 2 + 1))
                else:
                    sp.wait_ge((g_done, u_done, down_done)[i // 2], it * EG + (j + 1))

            def group(g, it):
                for j in range(EG):
                    for i in range(UPE):
                        m = j * UPE + i
                        s = slot_of(NFRONT + m)
                        expert_used(m - SLOTS, it)
                        stream_unit(g, j, i, s)

            for m in range(UPG):
                s = slot_of(NFRONT + m)
                j, i = divmod(m, UPE)
                if m < SLOTS:
                    used_wait(sp, NFRONT + m - SLOTS)
                else:
                    expert_used(m - SLOTS, 0)
                stream_unit(0, j, i, s)
            with sp.Fori(1, NG) as g:
                group(g, g)
            sp.wait_ge(routed, 1)
            npass = sp.value_load(npass_sb[0:1, 0:1], min_val=1, max_val=MAXPASS)
            with sp.If(npass > 1):
                with sp.Fori(1, npass) as r:
                    with sp.Fori(0, NG) as g:
                        group(g, r * NG + g)
            with sp.Else():
                pass

            y = outs["y_prompt"].rearrange("o (t p) d -> (o t) p d", p=P)
            every = npass * (NG * MIXES)
            for t, a, b in ((0, 0, 1024), (1, 0, 1024), (2, 0, D), (0, 1024, 2048), (1, 1024, 1536), (1, 1536, 2048)):
                sp.wait_ge(mix_added, every + (MIX_ORDER.index((t, b // 512 - 1 if t < 2 else None)) + 1))
                if t < 2:
                    sp.dma_start(y[t][:, a:b], xa[:, t, a:b]).then_inc(y_stored, 16)
                else:
                    for n in range(4):
                        sp.dma_start(outs["y_sample"].rearrange("b o d -> b (o d)")[:, n * 512:(n + 1) * 512],
                                     xa[n * C:n * C + NB, 2, 0:512]).then_inc(y_stored, 16)
            sp.wait_ge(y_stored, 144)
            sp.wait_ge(state_stored, 16)
            sp.wait_ge(stored[0], STORED[0] + 16)
            sp.wait_ge(stored[1], STORED[1] + 16 * NB)

        @block.tensor
        def _(pe):
            pe.wait_ge(consts_in, 16)
            for t in range(TT):
                pe.wait_ge(x_in[t], 16)
            for k in range(KT):
                if k >= len(XBANKS):
                    pe.wait_ge(xT_copied, k - len(XBANKS) + 1)
                for t in range(TT):
                    m = pe.transpose(x_bank(k)[:, P * t:P * t + P], xa[:, t, k * P:(k + 1) * P], ident)
                m.then_inc(h_T, 1)
                if k == len(XBANKS) - 1:
                    pe.wait_ge(vecs_in, VECS * 16)
                    nr = 3 * CT + 2 * KT
                    pe.transpose(bank[7][:, 0:nr], rawrows[0:nr, 0:P], ident[0:nr, 0:nr])
                    pe.transpose(bank[7][:, P:2 * P], rawrows[:, P:2 * P], ident).then_inc(raw_T, 1)
                    pe.wait_ge(spread_ready, 1)
                    for t in range(TT):
                        w = P if t < 2 else NB
                        m = pe.matmul(bank[2][:, t * P:t * P + w], const("ones"), spread[:, t, 0:w], start=True, stop=True)
                    m.then_inc(factors, 1)

            def bank_free(n):
                if n < 3:
                    if n == 1:
                        pe.wait_ge(xT_copied, KT)
                    if n == 2:
                        pe.wait_ge(factors_ready, 1)
                    return
                kind, i = TILES[n - 3]
                s, value = {"q": (qk_ready, i + 1), "k": (qk_ready, H + i + 1), "v": (v_copied, i + 1),
                            "C": (c_copied, i + 1), "X": (u_ready, i + 1), "B": (conv_ready, i + 1),
                            "W": (y_copied, i + 1)}[kind]
                pe.wait_ge(s, value)

            def tile(n):
                kind, i = TILES[n]
                unit = (kind, i // TPU)
                arrived(pe, unit)
                bank_free(n)
                w = ring[:, front_at[unit][0], :].rearrange("p (k c) -> p k c", k=KT)
                order = range(KT)
                src = hT
                if kind == "W":
                    order = [*range(H, KT), *range(H)]
                    src = cat
                for n_k, k in enumerate(order):
                    if n == 0:
                        pe.wait_ge(h_ready, k + 1)
                    if kind == "W" and n_k == 0 and i == 0:
                        pe.wait_ge(conv_ready, CT)
                    if kind == "W" and n_k == H and i == 0:
                        pe.wait_ge(o_ready, H + 1)
                    m = pe.matmul(bank[n % 3][:, 0:T], w[:, k, (i % TPU) * P:(i % TPU + 1) * P], src[:, k, :],
                                  start=n_k == 0, stop=n_k == KT - 1)
                m.then_inc(tile_done, 1)

            def half_sums(t):
                pe.wait_ge(squared, t + 1)
                if t >= 1:
                    pe.wait_ge(rooted, t)
                pe.matmul(bank[3][:, 0:T], const("blk"), sq[t % 2], start=True, stop=True).then_inc(summed, 1)

            def rows(t):
                src = qkT[:, t, :] if t < 2 * H else vT[t % 2]
                if t < 2 * H:
                    pe.wait_ge(qk_ready, t + 1)
                else:
                    pe.wait_ge(v_copied, t - 2 * H + 1)
                if t >= 1:
                    pe.wait_ge(rows_out, t)
                if t >= H:
                    for i in range(2):
                        pe.transpose(bank[4][:, i * P:i * P + P], src[:, i * P:i * P + P], ident)
                pe.transpose(bank[4][0:NB, 2 * P:3 * P], src[:, SEQ:T], ident).then_inc(rows_T, 1)

            def head_sums(h):
                pe.wait_ge(o_squared, h + 1)
                if h >= 1:
                    pe.wait_ge(o_rooted, h)
                pe.matmul(bank[3][:, 0:SEQ], const("ones"), osq, start=True, stop=True).then_inc(o_summed, 1)

            def head_scores(h):
                pe.wait_ge(qz_ready, h + 1)
                if h >= 1:
                    pe.wait_ge(biased, h)
                for c in range(2):
                    pe.matmul(bank[5][:, c * SEQ:(c + 1) * SEQ], qz[:, c, P:SEQ], qkT[:, H + h, 0:SEQ],
                              start=True, stop=True)
                for c in range(2):
                    m = pe.matmul(bank[6][:, c * P:(c + 1) * P], qz[:, c, 0:P], qkT[:, H + h, 0:P],
                                  start=True, stop=True)
                m.then_inc(scores, 1)

            def head_turn(h):
                pe.wait_ge(diffed, h + 1)
                if h >= 1:
                    pe.wait_ge(o_ready, h)
                pe.transpose(bank[7][:, 0:P], diff[:, 2 * P:3 * P], ident)
                pe.transpose(bank[7][:, P:2 * P], diff[:, 0:P], ident)
                pe.transpose(bank[7][:, 2 * P:3 * P], diff[:, P:2 * P], ident).then_inc(diff_T, 1)

            def head_pv(h):
                pe.wait_ge(diffT_copied, h + 1)
                pe.wait_ge(v_rows, h + 1)
                pe.matmul(bank[7][:, 0:SEQ], vrow[:, 0, h * HD:(h + 1) * HD], diffT[:, 0:SEQ], start=True, stop=False)
                pe.matmul(bank[7][:, P:SEQ], vrow[:, 1, h * HD:(h + 1) * HD], diffT[:, SEQ:SEQ + P],
                          start=False, stop=True).then_inc(pv, 1)

            def sample_rows():
                pe.wait_ge(page_sum, NPAGES)
                pe.wait_ge(biased, H)
                for g in range(NPG):
                    pe.transpose(bank[5][:, g * PAGE:(g + 1) * PAGE],
                                 keysc[:, g, :, :, :].rearrange("p c h b -> p (c h b)"), ident)
                pe.wait_ge(self_ready, 1)
                pe.matmul(bank[6][:, 0:1], selfqk, const("ones")[:, 0:1], start=True, stop=True).then_inc(s_T, 1)

            def sample_keys():
                pe.wait_ge(s_probs, 1)
                for g in range(NPG):
                    pe.matmul(bank[6][:, g * H * NB:(g + 1) * H * NB], rowsc[:, g * PAGE:(g + 1) * PAGE], const("sel"),
                              start=True, stop=True)
                pe.matmul(bank[6][:, 2 * H * NB:3 * H * NB], const("ones"), selfsel, start=True, stop=True).then_inc(s_pair, 1)

            def sample_pv():
                pe.wait_ge(s_pair_copied, 2)
                pe.wait_ge(rows_out, 3 * H)
                for b in range(NB):
                    u = b // 2
                    if b % 2 == 0:
                        arrived(pe, ("VP", u))
                    for g in range(NPG):
                        page = ((b % 2) * NPG + g) * ATT
                        for half in range(2):
                            m = pe.matmul(bank[4 + half][C * (b % 4):C * (b % 4 + 1), :], pairw[:, g, b, :],
                                          ring[:, front_at[("VP", u)][0], page + half * 512:page + (half + 1) * 512],
                                          start=b < 4 and g == 0, stop=b >= 4 and g == NPG - 1, skip_group_check=True)
                    if b % 2:
                        m.then_inc(s_pv, 1)

            def sample_pick():
                pe.wait_ge(s_pv_copied, 2)
                pe.wait_ge(o_rooted, H)
                pick = ident.rearrange("p (j r h) -> p h r j", j=4, h=H)
                for h in range(H):
                    m = pe.matmul(bank[3][:, h * NB:(h + 1) * NB], pvrows[:, h * HD:(h + 1) * HD],
                                  pick[:, h, 0:2, :], start=True, stop=True)
                m.then_inc(s_picked, 1)

            def sample_sums():
                pe.wait_ge(o_squared, H + 1)
                pe.matmul(bank[4][:, 0:H * NB], const("ones"), osq[:, 0:H * NB], start=True, stop=True).then_inc(o_summed, 1)

            for n in range(NIN):
                tile(n)
                if 1 <= n <= 2 * H:
                    half_sums(n - 1)
                if 2 <= n < 3 * H + 2:
                    rows(n - 2)
                h, stage = divmod(n - HEAD0, 3)
                if stage == 0 and 1 <= h <= H:
                    head_sums(h - 1)
                if 0 <= h < H:
                    (head_scores, head_turn, head_pv)[stage](h)
                if n == SAMPLE0:
                    sample_rows()
                if n == SAMPLE0 + 1:
                    sample_keys()
                if n == SAMPLE0 + 2:
                    sample_pv()
                if n == SAMPLE0 + 3:
                    sample_pick()
                if n == SAMPLE0 + 4:
                    sample_sums()

            pe.wait_ge(stash_ready, 1)
            pe.transpose(bank[5][0:(2 + NB) * CT, 0:P], stash, ident).then_inc(stash_T, 1)

            def y_turn(j):
                pe.wait_ge(y_copied, j + 1)
                b = bank[3 + j % 2]
                if j >= 2:
                    pe.wait_ge(y_added, j - 1)
                if j == 0:
                    pe.wait_ge(s_whole, 1)
                if j == 1:
                    pe.wait_ge(o_rooted, H + 1)
                for t in range(2):
                    pe.transpose(b[:, t * P:(t + 1) * P], yT[j % 2][:, t * P:(t + 1) * P], ident)
                pe.transpose(b[0:NB, 2 * P:3 * P], yT[j % 2][:, SEQ:T], ident)
                if j == 0:
                    pe.wait_ge(wr_ready, 1)
                pe.matmul(bank[6][0:RE, 0:T], wrv[:, j, :], yT[j % 2], start=j == 0, stop=j == KT - 1,
                          ).then_inc(y_T, 1)

            for j in range(KT):
                tile(TILE_AT[("W", j)])
                if j >= 1:
                    y_turn(j - 1)
            y_turn(KT - 1)

            pe.wait_ge(logits_copied, 1)
            pe.wait_ge(stash_out, 1)
            for t in range(TT):
                n = P if t < 2 else NB
                m = pe.transpose(bank[5][0:n, t * RE:(t + 1) * RE], logitsT[:, t * P:t * P + n], ident[0:RE, 0:RE])
            m.then_inc(router, 1)
            pe.wait_ge(assigned, 1)
            pe.wait_ge(late_in, 16)
            pe.wait_ge(y_added, KT)
            pe.matmul(bank[3][:, 0:4 * NE], late("tri"), bothf, start=True, stop=False)
            for s in range(1, 4):
                m = pe.matmul(bank[3][:, s * NE:4 * NE], const("ones"), bothf[:, 0:(4 - s) * NE], start=False, stop=s == 3)
            m.then_inc(ranked, 1)

            pe.wait_ge(routed, 1)
            npass = pe.value_load(npass_sb[0:1, 0:1], min_val=1, max_val=MAXPASS)
            with pe.Fori(0, npass) as r:
                with pe.Fori(0, NG) as g:
                    it = r * NG + g

                    def weights(j, i):
                        m = j * UPE + i
                        s = slot_of(NFRONT + m)
                        before = sum(slot_of(NFRONT + x) == s for x in range(m + 1))
                        pe.wait_ge(slot_full[s], it * (16 * UPG // SLOTS) + (front_total[s] + 16 * before))
                        return ring[:, s, :]

                    def unit_products(j, b, i):
                        w = weights(j, 2 * b + i).rearrange("p (k f) -> p k f", f=F)
                        for k in range(8):
                            c = k % 4
                            m = pe.matmul(bank[b][c * C:(c + 1) * C, :], xeT[:, 8 * i + k, j * C:(j + 1) * C], w[:, k, :],
                                          start=i == 0 and k < 4, stop=i == 1 and k >= 4, skip_group_check=True)
                        m.then_inc((unit_used, (g_done, u_done)[b])[i], 1)

                    pe.wait_ge(sel_ready, it + 1)
                    pe.wait_ge(h2_ready, 2 * KT)
                    pe.wait_ge(mix_added, it * MIXES + 7)
                    for q in range(4):
                        if q >= 2:
                            pe.wait_ge(xe_ready, it * 4 + (q - 1))
                        for k in range(4 * q, 4 * q + 4):
                            for t in range(TT):
                                m = pe.matmul(bank[4 + q % 2][:, (k % 4) * P:(k % 4 + 1) * P], h2[:, t, k::KT], sel[:, t, :],
                                              start=t == 0, stop=t == TT - 1)
                        m.then_inc(gathered, 1)
                        if q == 1:
                            pe.wait_ge(xe_ready, it * 4 + 2)
                            unit_products(0, 0, 0)
                    pe.wait_ge(xe_ready, it * 4 + 4)
                    unit_products(0, 0, 1)
                    pe.wait_ge(gate_ready, it + 1)
                    for t in range(TT):
                        m = pe.transpose(bank[3][:, t * P:(t + 1) * P], gate[:, t, :], ident)
                    m.then_inc(gate_T, 1)
                    pe.wait_ge(gateT_copied, it + 1)

                    def mix(x):
                        t, n = MIX_ORDER[x]
                        if x >= 3:
                            pe.wait_ge(mix_added, it * MIXES + (x - 3 + 1 + MIXES))
                        to = bank[5 + x % 3]
                        if t < 2:
                            m = pe.matmul(to[:, :], gateT[:, t, :], ye[:, n * 512:(n + 1) * 512], start=True, stop=True)
                        else:
                            for n in range(4):
                                m = pe.matmul(to[n * C:(n + 1) * C, :], gateT[:, 2, 0:C], ye[:, n * 512:(n + 1) * 512],
                                              start=True, stop=True, skip_group_check=True)
                        m.then_inc(mixed, 1)

                    for j in range(EG):
                        e = it * EG + j

                        def fold(x, src, copied):
                            pe.wait_ge(copied, e + 1)
                            for c in range(FC):
                                m = pe.matmul(bank[3][:, (x * FC + c) * C:(x * FC + c + 1) * C], src[:, c::FC], const("fold"),
                                              start=True, stop=True)
                            return m

                        if j >= 1:
                            unit_products(j, 0, 0)
                            unit_products(j, 0, 1)
                        unit_products(j, 1, 0)
                        fold(0, g_sb, g_copied)
                        unit_products(j, 1, 1)
                        fold(1, u_sb, u_copied).then_inc(folded, 1)
                        pe.wait_ge(act_ready, e + 1)
                        for i in range(2):
                            if j >= 1:
                                pe.wait_ge(ye_act, it * (EG * 4) + (4 * j - 2 + 2 * i))
                                pe.wait_ge(ye_dve, it * (EG * 4) + (4 * j - 2 + 2 * i))
                            w = weights(j, 4 + i).rearrange("p (c n d) -> p c n d", c=FC, n=4)
                            for c in range(FC):
                                for n in range(4):
                                    m = pe.matmul(bank[2 + 2 * i][n * C:(n + 1) * C, 0:256], actT[:, c, :], w[:, c, n, :],
                                                  start=c == 0, stop=c == FC - 1, skip_group_check=True)
                            m.then_inc((unit_used, down_done)[i], 1)

                    for i in range(2):
                        pe.wait_ge(ye_act, it * (EG * 4) + (EG * 4 - 2 + 2 * i))
                        pe.wait_ge(ye_dve, it * (EG * 4) + (EG * 4 - 2 + 2 * i))
                        for x in (range(AHEAD), range(AHEAD, MIXES))[i]:
                            mix(x)

        @block.scalar
        def _(act):
            A = nc.scalar.activation
            act.dma_start(consts[:, :], ins["consts"]).then_inc(consts_in, 16)
            act.wait_ge(x_in[0], 16)
            A(sqjunk, xa[:, 0, :], ACT.Square, accum_out=ssum[:, 0:1]).then_inc(sums1, 1)
            act.wait_ge(x_in[2], 16)
            act.wait_ge(sums1, 1)
            A(sqjunk, xa[:, 2, :], ACT.Square, accum_out=ssum[:, 2:3]).then_inc(sums1, 1)
            act.wait_ge(consts_in, 16)
            act.wait_ge(sums1, 2)
            act.wait_ge(sums1_dve, 1)
            A(srstd[:, 0:TT], ssum[:, 0:TT], ACT.Sqrt, bias=const("eps"), scale=1.0 / D).then_inc(sqrt1, 1)
            for k in range(KT):
                act.wait_ge(h_T, k + 1)
                A(cat[:, k, :], x_bank(k)[:, 0:T], ACT.Copy).then_inc(xT_copied, 1)
                if k == len(XBANKS) - 1:
                    act.wait_ge(raw_T, 1)
                    A(rawT, bank[7][:, 0:3 * CT + 2 * KT], ACT.Copy)
                    A(prevT, bank[7][:, P:2 * P], ACT.Copy).then_inc(raw_copied, 1)
            act.wait_ge(xT_copied, KT)
            for t in range(2):
                act.dma_start(xT_dram[:, t], cat[:, :, t * P:(t + 1) * P]).then_inc(xT_stored, 16)
            act.wait_ge(act_step, 1)
            A(lamv[:, 0:2], lamv[:, 0:2], ACT.Exp).then_inc(act_step, 1)

            n_stored = [0, 0]

            def square(t):
                act.wait_ge(tile_done, t + 1)
                if t >= 2:
                    act.wait_ge(summed, t - 1)
                A(sq[t % 2], bank[t % 3][:, 0:T], ACT.Square).then_inc(squared, 1)

            def root(t):
                act.wait_ge(summed, t + 1)
                if t >= 2:
                    act.wait_ge(qk_ready, t - 1)
                A(rstd[t % 2], bank[3][:, 0:T], ACT.Sqrt, bias=const("eps")).then_inc(rooted, 1)

            def copy_v(h):
                t = 2 * H + h
                act.wait_ge(tile_done, t + 1)
                if h >= 2:
                    act.wait_ge(rows_T, t - 1)
                A(vT[t % 2], bank[t % 3][:, 0:T], ACT.Copy)
                A(vTs[:, h * NB:(h + 1) * NB], bank[t % 3][:, SEQ:T], ACT.Copy).then_inc(v_copied, 1)

            def rows_outgoing(t):
                stage, s = kvstage[t % 2], stored[t % 2]
                cols = slice((t % H) * HD, (t % H + 1) * HD)
                act.wait_ge(rows_T, t + 1)
                if t < H:
                    A(qrows[:, cols], bank[4][0:NB, 2 * P:3 * P], ACT.Copy).then_inc(rows_out, 1)
                    if t == H - 1:
                        act.wait_ge(rows_out, H)
                        act.dma_start(qrows_dram, qrows).then_inc(q_stored, 16)
                    return
                if t == H:
                    act.wait_ge(xT_stored, 32)
                    act.wait_ge(xsT_ready, 1)
                if t >= H + 2:
                    act.wait_ge(s, n_stored[t % 2])
                if t == 2 * H:
                    act.wait_ge(q_stored, 16)
                if t >= 2 * H:
                    A(vrow[:, :, cols], bank[4][:, 0:2 * P].rearrange("p (t c) -> p t c", t=2), ACT.Copy).then_inc(v_rows, 1)
                else:
                    A(stage[:, 0:2 * P], bank[4][:, 0:2 * P], ACT.Copy)
                A(stage[0:NB, 2 * P:3 * P], bank[4][0:NB, 2 * P:3 * P], ACT.Copy).then_inc(rows_out, 1)
                act.wait_ge(rows_out, t + 1)
                name = "k" if t < 2 * H else "v"
                src = stage[:, 0:2 * P].rearrange("p (t c) -> p t c", t=2) if t < 2 * H else vrow[:, :, cols]
                if t >= 2 * H:
                    act.wait_ge(v_rows, t - 2 * H + 1)
                act.dma_start(outs[name + "_prompt"].rearrange("l o (t p) h d -> p (l o t) (h d)", p=P)[:, :, cols],
                              src).then_inc(s, 16)
                act.dma_start(outs[name + "_sample"].rearrange("l b o h d -> (l b o) (h d)")[:, cols],
                              stage[0:NB, 2 * P:3 * P]).then_inc(s, 16)
                n_stored[t % 2] += 32

            def head_root(h, cols=SEQ):
                act.wait_ge(o_summed, h + 1)
                if h >= 1:
                    act.wait_ge(o_ready, h)
                A(ord_[:, 0:cols], bank[3 if h < H else 4][:, 0:cols], ACT.Sqrt, bias=const("eps"), scale=1.0 / HD).then_inc(o_rooted, 1)

            for n in range(NIN):
                if n < 2 * H:
                    square(n)
                elif n < 3 * H:
                    copy_v(n - 2 * H)
                elif (n - BCX) % 3 == 0:
                    i = (n - BCX) // 3
                    act.wait_ge(tile_done, n + 1)
                    if i >= 1:
                        act.wait_ge(u_ready, i)
                    A(ctmp, bank[n % 3][:, 0:T], ACT.Copy).then_inc(c_copied, 1)
                if 1 <= n <= 2 * H:
                    root(n - 1)
                if 2 <= n < 3 * H + 2:
                    rows_outgoing(n - 2)
                h, stage = divmod(n - HEAD0, 3)
                if stage == 0 and 1 <= h <= H:
                    head_root(h - 1)
                if stage == 0 and 0 <= h < H:
                    act.wait_ge(biased, h + 1)
                    for x in range(4):
                        a, b = ((0, 256), (256, 512), (512, 640), (640, 768))[x]
                        A(prob[:, a:b], prob[:, a:b], ACT.Exp, bias=nmax[:, x:x + 1], accum_out=esum[:, x:x + 1]).then_inc(exped, 1)
                if stage == 1 and 0 <= h < H:
                    act.wait_ge(diff_T, h + 1)
                    A(diffT, bank[7][:, 0:3 * P], ACT.Copy).then_inc(diffT_copied, 1)
                if stage == 2 and 0 <= h < H:
                    act.wait_ge(pv, h + 1)
                    A(osq, bank[7][:, 0:SEQ], ACT.Square).then_inc(o_squared, 1)
                if n == SAMPLE0:
                    act.wait_ge(s_biased, 1)
                    A(rowsc, rowsc, ACT.Exp, bias=nmax[:, 0:1], accum_out=esum[:, 0:1]).then_inc(s_exped, 1)
                if n == SAMPLE0 + 3:
                    act.wait_ge(s_whole, 1)
                    A(osq[:, 0:H * NB], osamp[:, 0:H * NB], ACT.Square).then_inc(o_squared, 1)
                if n == SAMPLE0 + 4:
                    head_root(H, H * NB)
            assert tuple(n_stored) == STORED
            act.wait_ge(tile_done, NIN)
            act.wait_ge(xT_stored, 32)
            for part, ks in enumerate((slice(0, 2), slice(2, KT))):
                act.dma_start(xT[:, :, ks, :], xT_dram[:, :, ks, :]).then_inc(xT_in[part], 16)
            act.wait_ge(stash_T, 1)
            A(outrows[0:(2 + NB) * CT, :], bank[5][0:(2 + NB) * CT, 0:P], ACT.Copy).then_inc(stash_out, 1)
            act.wait_ge(stash_out, 1)
            act.dma_start(outs["conv_prompt"].rearrange("l o r (i p) -> (l o r i) p", p=P), outrows[0:2 * CT, :]
                          ).then_inc(stored[0], 16)
            for b in range(NB):
                act.dma_start(outs["conv_sample"].rearrange("l b r (i p) -> (l b) r i p", p=P)[b, 1],
                              outrows[(2 + b) * CT:(3 + b) * CT, :]).then_inc(stored[1], 16)

            def row_squares(j):
                act.wait_ge(y_added, j + 1)
                if j >= 1:
                    act.wait_ge(sums2, j)
                for t in range(TT):
                    ins_ = A(junk_act[t], xa[:, t, j * P:(j + 1) * P], ACT.Square, accum_out=ssq[:, t, j:j + 1])
                ins_.then_inc(sums2, 1)

            for j in range(KT - 2):
                row_squares(j)
            row_squares(KT - 2)
            act.wait_ge(y_T, KT)
            A(logitsT, bank[6][0:RE, 0:T], ACT.Copy).then_inc(logits_copied, 1)
            row_squares(KT - 1)
            act.wait_ge(ssq_sum, 1)
            act.wait_ge(stored[0], STORED[0] + 16)
            act.wait_ge(stored[1], STORED[1] + 16 * NB)
            A(srstd[:, 0:TT], ssum[:, 0:TT], ACT.Sqrt, bias=const("eps"), scale=1.0 / D).then_inc(sqrt2, 1)
            act.wait_ge(gex_ready, 1)
            A(gex, gex, ACT.Exp).then_inc(gexed, 1)
            A(ew, ew, ACT.Exp).then_inc(gexed, 1)
            for n in range(1, 4):
                A(xa[n * C:n * C + NB, 2, 0:512], xa[0:NB, 2, n * 512:(n + 1) * 512], ACT.Copy).then_inc(xs_moved, 1)

            act.wait_ge(routed, 1)
            npass = act.value_load(npass_sb[0:1, 0:1], min_val=1, max_val=MAXPASS)
            with act.Fori(0, npass) as r:
                with act.Fori(0, NG) as g:
                    it = r * NG + g
                    act.wait_ge(gate_T, it + 1)
                    A(gateT, bank[3][:, 0:TT * P].rearrange("p (t s) -> p t s", t=TT), ACT.Copy).then_inc(gateT_copied, 1)
                    for j in range(EG):
                        act.wait_ge(g_done, it * EG + (j + 1))
                        A(g_sb, bank[0][:, :], ACT.Copy).then_inc(g_copied, 1)
                        act.wait_ge(folded, it * EG + (j + 1))
                        A(actT, bank[3][:, 0:P].rearrange("p (c s) -> p c s", c=FC), ACT.Silu).then_inc(silu_done, 1)
                        for i in range(2):
                            if i == 0:
                                act.wait_ge(unit_used, it * (3 * EG) + (3 * j + 3))
                            else:
                                act.wait_ge(down_done, it * EG + (j + 1))
                            for n in range(2):
                                A(ye[j * C:(j + 1) * C, i * 1024 + n * 256:i * 1024 + (n + 1) * 256],
                                  bank[2 + 2 * i][n * C:(n + 1) * C, 0:256], ACT.Copy).then_inc(ye_act, 1)

        @block.vector
        def _(dve):
            V = nc.vector
            st = Steps(dve, dve_step)
            dve.wait_ge(x_in[1], 16)
            V.tensor_tensor_reduce(sqjunk2, xa[:, 1, :], xa[:, 1, :], 1.0, 0.0, ALU.mult, ALU.add, ssum[:, 1:2]
                                   ).then_inc(sums1_dve, 1)
            dve.wait_ge(sqrt1, 1)
            st.do(V.reciprocal(srstd[:, 0:TT], srstd[:, 0:TT]))
            for t in range(TT):
                ins_ = V.tensor_scalar(spread[:, t, :], ident, srstd[:, t:t + 1], None, ALU.mult)
            ins_.then_inc(spread_ready, 1)
            dve.wait_ge(factors, 1)
            V.tensor_copy(rstdB, bank[2][:, 0:T]).then_inc(factors_ready, 1)
            dve.wait_ge(factors_ready, 1)
            dve.wait_ge(raw_copied, 1)
            for k in range(KT):
                dve.wait_ge(xT_copied, k + 1)
                V.scalar_tensor_tensor(hT[:, k, :], cat[:, k, :], gmix[:, k:k + 1], rstdB, ALU.mult, ALU.mult).then_inc(h_ready, 1)
            V.tensor_copy(xsT, cat[:, :, SEQ:T]).then_inc(xsT_ready, 1)
            for i in range(2):
                st.do(V.tensor_tensor_reduce(lamprod, lamraw[:, 2 * i * HALF:(2 * i + 1) * HALF],
                                             lamraw[:, (2 * i + 1) * HALF:(2 * i + 2) * HALF], 1.0, 0.0,
                                             ALU.mult, ALU.add, lamv[:, i:i + 1]))
            V.tensor_scalar(gqk[:, 0:1], gqk[:, 0:1], HALF ** -0.5, None, ALU.mult).then_inc(act_step, 1)
            st.add(V.tensor_scalar(gsub[:, 1:2], gsub[:, 0:1], 1.0 - LAM_INIT, None, ALU.mult))
            dve.wait_ge(act_step, 2)
            st.do(V.tensor_tensor(lamv[:, 2:3], lamv[:, 0:1], lamv[:, 1:2], ALU.subtract))
            st.do(V.tensor_scalar(lamv[:, 2:3], lamv[:, 2:3], LAM_INIT, None, ALU.add))
            st.do(V.tensor_scalar(lamv[:, 3:4], lamv[:, 2:3], -1.0, None, ALU.mult))
            st.do(V.tensor_tensor(lamv[:, 0:1], lamv[:, 2:3], const("neg_c1"), ALU.mult))
            st.do(V.tensor_tensor(lamv[:, 0:1], lamv[:, 0:1], const("c0"), ALU.add))

            def normalise(t):
                r = rstd[t % 2]
                dve.wait_ge(rooted, t + 1)
                st.do(V.reciprocal(r, r))
                V.scalar_tensor_tensor(qkT[:, t, :], bank[t % 3][:, 0:T], gqk[:, t // H:t // H + 1], r,
                                       ALU.mult, ALU.mult).then_inc(qk_ready, 1)

            prev = prevT.rearrange("p (b j i) -> p b j i", b=NB, j=2)
            out = stash.rearrange("p (r i) -> p r i", i=CT)

            def page(j):
                b, g = divmod(j, NPG)
                dve.wait_ge(page_mul, j + 1)
                s, _ = front_at[("KP", j // PPU)]
                src = ring[:, s, (j % PPU) * ATT:(j % PPU + 1) * ATT].rearrange("p (h c d) -> p h c d", h=H, c=2)
                V.tensor_reduce(keysc[:, g, :, :, b].rearrange("p c h -> p h c"), src, AX.X, ALU.add).then_inc(page_sum, 1)

            def head_out(h):
                dve.wait_ge(o_rooted, h + 1)
                st.do(V.reciprocal(ord_, ord_))
                V.scalar_tensor_tensor(cat[:, h, 0:SEQ], bank[7][:, 0:SEQ], gsub[:, 1:2], ord_, ALU.mult, ALU.mult
                                       ).then_inc(o_ready, 1)

            def bias_scores(i):
                dve.wait_ge(scores, i + 1)
                for c in range(2):
                    st.add(V.scalar_tensor_tensor(prob[:, c * SEQ:(c + 1) * SEQ], const("dist"), SLOPES[i],
                                                  bank[5][:, c * SEQ:(c + 1) * SEQ], ALU.mult, ALU.add))
                for c in range(2):
                    st.add(V.scalar_tensor_tensor(prob[:, 512 + c * P:512 + (c + 1) * P], const("dist")[:, P:2 * P], SLOPES[i],
                                                  bank[6][:, c * P:(c + 1) * P], ALU.mult, ALU.add))
                st.wait()
                st.do(V.tensor_reduce(nmax[:, 0:2], prob[:, 0:512].rearrange("p (c k) -> p c k", c=2), AX.X, ALU.max, negate=True))
                V.tensor_reduce(nmax[:, 2:4], prob[:, 512:768].rearrange("p (c k) -> p c k", c=2), AX.X, ALU.max, negate=True
                                ).then_inc(biased, 1)

            def difference(i):
                dve.wait_ge(exped, 4 * (i + 1))
                if i >= 1:
                    dve.wait_ge(diff_T, i)
                st.do(V.reciprocal(rsum, esum))
                st.do(V.tensor_scalar(rsum[:, 1:2], rsum[:, 1:2], lamv[:, 3:4], None, ALU.mult))
                st.do(V.tensor_scalar(rsum[:, 3:4], rsum[:, 3:4], lamv[:, 3:4], None, ALU.mult))
                st.add(V.tensor_scalar(diff[:, 0:256], prob[:, 0:256], rsum[:, 0:1], None, ALU.mult))
                st.do(V.tensor_scalar(diff[:, 256:384], prob[:, 512:640], rsum[:, 2:3], None, ALU.mult))
                st.add(V.scalar_tensor_tensor(diff[:, 0:256], prob[:, 256:512], rsum[:, 1:2], diff[:, 0:256], ALU.mult, ALU.add))
                V.scalar_tensor_tensor(diff[:, 256:384], prob[:, 640:768], rsum[:, 3:4], diff[:, 256:384], ALU.mult, ALU.add
                                       ).then_inc(diffed, 1)

            def conv_input(i):
                n = BCX + 3 * i + 1
                dve.wait_ge(tile_done, n + 1)
                dve.wait_ge(c_copied, i + 1)
                V.tensor_tensor(upad[:, 2:T + 2], ctmp, bank[n % 3][:, 0:T], ALU.mult).then_inc(u_ready, 1)
                dve.wait_ge(u_ready, i + 1)
                tap = [convwT[:, j * CT + i:j * CT + i + 1] for j in range(3)]
                st.add(V.tensor_scalar(conv[:, 0:SEQ], upad[:, 0:SEQ], tap[0], None, ALU.mult))
                st.do(V.tensor_scalar(conv[:, SEQ:T], prev[:, :, 0, i], tap[0], None, ALU.mult))
                st.add(V.scalar_tensor_tensor(conv[:, 0:SEQ], upad[:, 1:SEQ + 1], tap[1], conv[:, 0:SEQ], ALU.mult, ALU.add))
                st.do(V.scalar_tensor_tensor(conv[:, SEQ:T], prev[:, :, 1, i], tap[1], conv[:, SEQ:T], ALU.mult, ALU.add))
                st.do(V.scalar_tensor_tensor(conv, upad[:, 2:T + 2], tap[2], conv, ALU.mult, ALU.add))
                st.add(V.tensor_copy(out[:, :, i], upad[:, SEQ:T + 2]))

            def conv_output(i):
                n = BCX + 3 * i + 2
                dve.wait_ge(tile_done, n + 1)
                if i == 3:
                    for x in range(2):
                        dve.wait_ge(stored[x], STORED[x])
                V.tensor_tensor(cat[:, CT + i, :], conv, bank[n % 3][:, 0:T], ALU.mult).then_inc(conv_ready, 1)

            def self_scores():
                st.do(V.memset(selfqk, 0.0))
                for c in range(2):
                    q = slice(c * HALF, (c + 1) * HALF)
                    ins_ = V.tensor_tensor(selfqk[q, c * H * NB:(c + 1) * H * NB].rearrange("p (h b) -> p h b", h=H),
                                           qkT[q, 0:H, SEQ:T], qkT[q, H:2 * H, SEQ:T], ALU.mult)
                    if c == 0:
                        st.do(ins_)
                    else:
                        ins_.then_inc(self_ready, 1)

            def sample_max():
                dve.wait_ge(s_T, 1)
                st.add(V.scalar_tensor_tensor(rowsc[:, 0:PAST], const("kpos"), const("slope"), bank[5][:, 0:PAST], ALU.mult, ALU.add))
                st.do(V.tensor_copy(rowsc[:, PAST:PAST + 1], bank[6][:, 0:1]))
                V.tensor_reduce(nmax[:, 0:1], rowsc, AX.X, ALU.max, negate=True).then_inc(s_biased, 1)
                dve.wait_ge(s_exped, 1)
                st.do(V.reciprocal(rsum[:, 0:1], esum[:, 0:1]))
                st.do(V.tensor_tensor(rsum[:, 0:1], rsum[:, 0:1], lamv[:, 0:1], ALU.mult))
                st.do(V.tensor_scalar(rowsc, rowsc, rsum[:, 0:1], None, ALU.mult))
                V.tensor_scalar(selfsel, const("sel"), rowsc[:, PAST:PAST + 1], None, ALU.mult).then_inc(s_probs, 1)
                st.do(V.memset(pairw, 0.0))

            def sample_weights():
                dve.wait_ge(s_pair, 1)
                st.add(V.tensor_tensor(selfsel, bank[6][:, 2 * H * NB:3 * H * NB], vTs, ALU.mult))
                w = bank[6][:, 0:2 * H * NB].rearrange("p (g h b) -> p g h b", g=NPG, h=H)
                for r in range(2):
                    V.tensor_copy(pairw[:, :, 4 * r:4 * r + 4, r * H:(r + 1) * H].rearrange("p g b h -> p g h b"),
                                  w[:, :, :, 4 * r:4 * r + 4]).then_inc(s_pair_copied, 1)

            def sample_copy():
                for x in range(2):
                    dve.wait_ge(stored[x], STORED[x])
                dve.wait_ge(s_pv, NB // 2)
                for half in range(2):
                    V.tensor_copy(pvrows[:, half * 512:(half + 1) * 512], bank[4 + half][:, :]).then_inc(s_pv_copied, 1)

            def sample_whole():
                dve.wait_ge(s_picked, 1)
                st.wait()
                V.tensor_tensor(osamp[:, 0:H * NB], selfsel, bank[3][:, 0:H * NB], ALU.add).then_inc(s_whole, 1)

            for n in range(NIN):
                if 1 <= n <= 2 * H:
                    normalise(n - 1)
                if n == 2 * H + 1:
                    st.add(V.memset(upad[:, 0:2], 0.0))
                    dve.wait_ge(raw_copied, 1)
                    dve.wait_ge(qk_ready, 2 * H)
                    self_scores()
                h, stage = divmod(n - HEAD0, 3)
                if stage == 0:
                    if 0 <= h < H:
                        bias_scores(h)
                    if 1 <= h <= H:
                        head_out(h - 1)
                    if 0 <= h < H:
                        difference(h)
                if n >= BCX and (n - BCX) % 3 == 1:
                    conv_input((n - BCX) // 3)
                if n >= BCX and (n - BCX) % 3 == 2:
                    i = (n - BCX) // 3
                    conv_output(i)
                    for j in range(PAGES_BY[i], PAGES_BY[i + 1]):
                        page(j)
                if n == SAMPLE0:
                    sample_max()
                if n == SAMPLE0 + 1:
                    sample_weights()
                if n == SAMPLE0 + 2:
                    sample_copy()
                if n == SAMPLE0 + 3:
                    sample_whole()
            dve.wait_ge(conv_ready, CT)
            st.wait()
            V.tensor_copy(lamv[:, 1:2], lamv[:, 0:1]).then_inc(stash_ready, 1)
            dve.wait_ge(o_rooted, H + 1)
            st.do(V.reciprocal(ord_[:, 0:H * NB], ord_[:, 0:H * NB]))
            V.scalar_tensor_tensor(cat[:, 0:H, SEQ:T], osamp.rearrange("p (h b) -> p h b", h=H), gsub[:, 1:2],
                                   ord_[:, 0:H * NB].rearrange("p (h b) -> p h b", h=H), ALU.mult, ALU.mult).then_inc(o_ready, 1)

            dve.wait_ge(x2_zero, 1)
            for j in range(KT + 1):
                if j < KT:
                    n = TILE_AT[("W", j)]
                    dve.wait_ge(tile_done, n + 1)
                    if j >= 2:
                        dve.wait_ge(y_T, j - 1)
                    if j in (0, 2):
                        dve.wait_ge(xT_in[j // 2], 16)
                    V.tensor_tensor(yT[j % 2][:, 0:SEQ].rearrange("p (t c) -> p t c", t=2), xT[:, :, j, :],
                                    bank[n % 3][:, 0:SEQ].rearrange("p (t c) -> p t c", t=2), ALU.add)
                    V.tensor_tensor(yT[j % 2][:, SEQ:T], xsT[:, j, :], bank[n % 3][:, SEQ:T], ALU.add).then_inc(y_copied, 1)
                if j >= 1:
                    dve.wait_ge(y_T, j)
                    b = bank[3 + (j - 1) % 2]
                    cols = slice((j - 1) * P, j * P)
                    V.tensor_copy(xa[:, 0:2, cols], b[:, 0:2 * P].rearrange("p (t c) -> p t c", t=2))
                    V.tensor_copy(xa[0:NB, 2, cols], b[0:NB, 2 * P:3 * P]).then_inc(y_added, 1)
            dve.wait_ge(sums2, KT)
            V.tensor_reduce(ssum[:, 0:TT].unsqueeze(2), ssq, AX.X, ALU.add).then_inc(ssq_sum, 1)
            dve.wait_ge(sqrt2, 1)
            st.do(V.reciprocal(srstd[:, 0:TT], srstd[:, 0:TT]))

            def rows_of(x, n):
                return x.unsqueeze(1).to_broadcast([P, TT, n])

            dve.wait_ge(late_in, 16)
            st.add(V.memset(logits, FAR))
            st.do(V.memset(bothf, 0.0))
            dve.wait_ge(router, 1)
            dve.wait_ge(wr_in, 64)
            for t in range(TT):
                n = P if t < 2 else NB
                st.add(V.scalar_tensor_tensor(logits[0:n, t, :], bank[5][0:n, t * RE:(t + 1) * RE],
                                              srstd[0:n, t:t + 1], rbias[0:n, :], ALU.mult, ALU.add))
            st.wait()

            def top(x, best, idx, at):
                for t in range(TT):
                    st.add(V.max(best[:, t, :], x[:, t, :]))
                st.wait()
                for t in range(TT):
                    st.add(V.max_index(idx[:, t, :], best[:, t, :], x[:, t, :]))
                st.wait()
                st.do(V.tensor_copy(at, idx))

            lg, le = logits[:, :, 0:GROUPS], logits[:, :, RG:]
            top(logits[:, :, 0:RG], gtop, gidx, gat)
            st.add(V.tensor_tensor(gex, lg, gtop[:, :, 0:1].to_broadcast([P, TT, GROUPS]), ALU.subtract))
            st.do(V.tensor_tensor(goh, rows_of(late("iota")[:, 0:GROUPS], GROUPS), gat[:, :, 0:1].to_broadcast([P, TT, GROUPS]),
                                  ALU.is_equal))
            st.do(V.tensor_scalar(geneg, goh, -1.0, -FAR, ALU.add, ALU.mult))
            for t in range(TT):
                st.add(V.tensor_tensor(lem[:, t, :].rearrange("p (g e) -> p g e", g=GROUPS),
                                       le[:, t, :].rearrange("p (g e) -> p g e", g=GROUPS),
                                       geneg[:, t, :].unsqueeze(2).to_broadcast([P, GROUPS, EPG]), ALU.add))
            st.wait()
            top(lem, etop, eidx, eat)
            V.tensor_tensor(ew, etop[:, :, 1:2], etop[:, :, 0:1], ALU.subtract).then_inc(gex_ready, 1)
            iota_e = rows_of(late("iota")[:, 0:NE], NE)
            st.add(V.tensor_tensor(oh1, iota_e, eat[:, :, 0:1].to_broadcast([P, TT, NE]), ALU.is_equal))
            st.do(V.tensor_tensor(oh2, iota_e, eat[:, :, 1:2].to_broadcast([P, TT, NE]), ALU.is_equal))
            st.do(V.tensor_tensor(both, oh1, oh2, ALU.add))
            V.tensor_tensor(both, both, const("valid").unsqueeze(2).to_broadcast([P, TT, NE]), ALU.mult).then_inc(assigned, 1)
            dve.wait_ge(gexed, 2)
            st.add(V.tensor_reduce(gs, gex, AX.X, ALU.add))
            st.do(V.tensor_scalar(w_n, ew, 1.0, None, ALU.add))
            st.do(V.tensor_tensor(w_n, w_n, gs, ALU.mult))
            st.do(V.reciprocal(w1.unsqueeze(2), w_n))
            st.do(V.tensor_tensor(w2.unsqueeze(2), w1.unsqueeze(2), ew, ALU.mult))
            dve.wait_ge(ranked, 1)
            st.do(V.tensor_reduce(cmax, bank[3][:, TT * NE:(TT + 1) * NE], AX.X, ALU.max))
            st.do(V.tensor_scalar(cwork, const("kth"), cmax, None, ALU.is_lt))
            st.do(V.tensor_reduce(cpass, cwork, AX.X, ALU.add))
            V.memset(esum[:, 0:1], 0.0).then_inc(mix_added, MIXES)
            V.tensor_copy(npass_sb[0:1, 0:1], cpass[0:1, :]).then_inc(routed, 1)
            rank = bank[3][:, 0:TT * NE]
            st.do(V.tensor_copy(ranki, rank))
            st.do(V.tensor_scalar(ranki, ranki, C - 1, None, ALU.bitwise_and))
            st.add(V.tensor_copy(work.rearrange("p t e -> p (t e)"), ranki))
            st.do(V.scalar_tensor_tensor(slotmap, rank.rearrange("p (t e) -> p t e", t=TT), float(NE), rows_of(late("base"), NE),
                                         ALU.mult, ALU.add))
            st.do(V.scalar_tensor_tensor(slotmap, work, -float(NE - 1), slotmap, ALU.mult, ALU.add))
            st.add(V.tensor_tensor(oh1, oh1, slotmap, ALU.mult))
            st.do(V.tensor_tensor(oh2, oh2, slotmap, ALU.mult))
            st.add(V.tensor_reduce(pos1.unsqueeze(2), oh1, AX.X, ALU.add))
            st.do(V.tensor_reduce(pos2.unsqueeze(2), oh2, AX.X, ALU.add))

            iota = late("iota")

            def select():
                for t in range(TT):
                    st.add(V.tensor_scalar(second[t], iota, pos2[:, t:t + 1], None, ALU.is_equal))
                    st.add(V.tensor_scalar(sel[:, t, :], iota, pos1[:, t:t + 1], srstd[:, t:t + 1], ALU.is_equal, ALU.mult))
                st.wait()
                for t in range(TT):
                    ins_ = V.scalar_tensor_tensor(sel[:, t, :], second[t], srstd[:, t:t + 1], sel[:, t, :], ALU.mult, ALU.add)
                    if t < TT - 1:
                        st.add(ins_)
                    else:
                        ins_.then_inc(sel_ready, 1)

            select()
            dve.wait_ge(xs_moved, 3)
            dve.wait_ge(routed, 1)

            npass = dve.value_load(npass_sb[0:1, 0:1], min_val=1, max_val=MAXPASS)
            before = st.n
            with dve.Fori(0, npass) as r:
                with dve.Fori(0, NG) as g:
                    it = r * NG + g
                    st.base = it * LOOP_STEPS
                    for t in range(TT):
                        st.add(V.tensor_scalar(gate[:, t, :], iota, pos1[:, t:t + 1], w1[:, t:t + 1], ALU.is_equal, ALU.mult))
                    st.wait()
                    for t in range(TT):
                        ins_ = V.scalar_tensor_tensor(gate[:, t, :], second[t], w2[:, t:t + 1], gate[:, t, :], ALU.mult, ALU.add)
                        if t < TT - 1:
                            st.add(ins_)
                        else:
                            ins_.then_inc(gate_ready, 1)
                    st.wait()
                    dve.wait_ge(gate_ready, it + 1)
                    st.do(V.tensor_scalar(route[:, 0:2 * TT], route[:, 0:2 * TT], -float(P), None, ALU.add))
                    for q in range(4):
                        dve.wait_ge(gathered, it * 4 + (q + 1))
                        V.tensor_tensor(xeT[:, 4 * q:4 * q + 4, :], bank[4 + q % 2][:, :].rearrange("p (k s) -> p k s", k=4),
                                        gffn[:, 4 * q:4 * q + 4].unsqueeze(2).to_broadcast([P, 4, P]), ALU.mult).then_inc(xe_ready, 1)
                    select()
                    for j in range(EG):
                        dve.wait_ge(u_done, it * EG + (j + 1))
                        V.tensor_copy(u_sb, bank[1][:, :]).then_inc(u_copied, 1)
                        dve.wait_ge(silu_done, it * EG + (j + 1))
                        V.tensor_tensor(actT, actT, bank[3][:, P:2 * P].rearrange("p (c s) -> p c s", c=FC), ALU.mult
                                        ).then_inc(act_ready, 1)
                        for i in range(2):
                            if i == 0:
                                dve.wait_ge(unit_used, it * (3 * EG) + (3 * j + 3))
                            else:
                                dve.wait_ge(down_done, it * EG + (j + 1))
                            for n in range(2, 4):
                                V.tensor_copy(ye[j * C:(j + 1) * C, i * 1024 + n * 256:i * 1024 + (n + 1) * 256],
                                              bank[2 + 2 * i][n * C:(n + 1) * C, 0:256]).then_inc(ye_dve, 1)
                    for x in range(MIXES):
                        t, n = MIX_ORDER[x]
                        cols = slice(n * 512, (n + 1) * 512) if t < 2 else slice(0, 512)
                        dve.wait_ge(mixed, it * MIXES + (x + 1))
                        V.tensor_tensor(xa[:, t, cols], xa[:, t, cols], bank[5 + x % 3][:, :], ALU.add).then_inc(mix_added, 1)
            assert st.n - before == LOOP_STEPS, st.n - before

        @block.gpsimd
        def _(pool):
            G = nc.gpsimd
            G.memset(xa[:, 2, :], 0.0).then_inc(x_clear, 1)
            pool.wait_ge(x_clear, 1)
            xs = ins["x_sample"].rearrange("b o d -> b (o d)")
            pool.dma_start(xa[0:NB, 2, :], xs).then_inc(x_in[2], 16)
            pool.dma_start(outs["conv_sample"][0, :, 0, :], ins["state_conv"][0, :, 1, :]).then_inc(state_stored, 16)

            pool.wait_ge(h_T, KT)
            G.memset(qz, 0.0).then_inc(qz_zero, 1)
            pool.wait_ge(qz_zero, 1)
            def split_q(h):
                pool.wait_ge(qk_ready, h + 1)
                if h >= 1:
                    pool.wait_ge(scores, h)
                G.tensor_copy(qz[0:HALF, 0, :], qkT[0:HALF, h, 0:SEQ]).then_inc(qz_zero, 1)
                pool.wait_ge(qz_zero, h + 2)
                G.tensor_copy(qz[HALF:P, 1, :], qkT[HALF:P, h, 0:SEQ]).then_inc(qz_ready, 1)
                pool.wait_ge(qz_ready, h + 1)

            def multiply_page(j):
                b = j // NPG
                if j % PPU == 0:
                    arrived(pool, ("KP", j // PPU))
                if b % 4 == 0 and j % NPG == 0:
                    arrived(pool, ("QB", b // 4))
                s, _ = front_at[("KP", j // PPU)]
                sq_, _ = front_at[("QB", b // 4)]
                kp = ring[:, s, (j % PPU) * ATT:(j % PPU + 1) * ATT]
                G.tensor_tensor(kp, kp, ring[:, sq_, (b % 4) * ATT:(b % 4 + 1) * ATT], ALU.mult).then_inc(page_mul, 1)

            for n in range(HEAD0 - 3, NIN, 3):
                h, i = (n + 3 - HEAD0) // 3, (n - BCX) // 3
                if h < H:
                    split_q(h)
                if i >= 0:
                    for j in range(PAGES_BY[i], PAGES_BY[i + 1]):
                        multiply_page(j)
                    if PAGES_AT[i]:
                        pool.wait_ge(page_mul, PAGES_BY[i + 1])

            pool.wait_ge(scores, H)
            pool.wait_ge(self_ready, 1)
            G.memset(wrv, 0.0).then_inc(wr_zero, 1)
            G.memset(rbias, FAR).then_inc(wr_zero, 1)
            pool.wait_ge(wr_zero, 2)
            pool.dma_start(wrv[:, :, 0:GROUPS], ins["w_router_group"].rearrange("l (k p) e -> (l p) k e", p=P)).then_inc(wr_in, 16)
            pool.dma_start(wrv[:, :, RG:], ins["w_router_expert"].rearrange("l (k p) e -> (l p) k e", p=P)).then_inc(wr_in, 16)
            pool.dma_start(rbias[:, 0:GROUPS], ins["b_router_group"].partition_broadcast(P).rearrange("p l e -> p (l e)")
                           ).then_inc(wr_in, 16)
            pool.dma_start(rbias[:, RG:], ins["b_router_expert"].partition_broadcast(P).rearrange("p l e -> p (l e)")
                           ).then_inc(wr_in, 16)
            pool.wait_ge(wr_in, 64)
            G.tensor_tensor(wrv, wrv, gffnT.unsqueeze(2).to_broadcast([P, KT, RE]), ALU.mult).then_inc(wr_ready, 1)
            pool.wait_ge(o_ready, H + 1)
            G.memset(xa[:, 2, :], 0.0).then_inc(x2_zero, 1)
            pool.dma_start(consts[:, late0:late0 + 512], ins["late"]).then_inc(late_in, 16)
            pool.wait_ge(tile_done, NIN)
            G.memset(h2[:, 2, :], 0.0).then_inc(h2_zero, 1)
            pool.wait_ge(h2_zero, 1)
            for j in range(KT):
                pool.wait_ge(y_added, j + 1)
                cols = slice(j * P, (j + 1) * P)
                G.tensor_copy(h2[:, 0:2, cols], xa[:, 0:2, cols]).then_inc(h2_ready, 1)
                G.tensor_copy(h2[0:NB, 2, cols], xa[0:NB, 2, cols]).then_inc(h2_ready, 1)

    return nc


VECS = 14
STORED = (32 * H, 32 * H)
LOOP_STEPS = 3 * TT + 2 * (TT - 1) + 1


def _constants():
    import numpy as np

    c = np.zeros((P, NCONST), np.float32)

    def put(name, x):
        a, b = CONST_AT[name]
        c[:, a:b] = x

    r = np.arange(P)
    put("ident", np.eye(P))
    put("ones", 1.0)
    put("fold", np.tile(np.eye(C), (EG, 1)))
    put("blk", np.kron(np.eye(2), np.ones((HALF, HALF))) / HALF)
    put("sel", np.tile(np.eye(H * NB), (2, 1)))
    back = P + r[:, None] - np.arange(SEQ)[None, :]
    put("dist", np.where(back >= 0, -back, FAR))
    put("kpos", np.arange(PAST)[None, :] - PAST)
    put("slope", np.tile(np.repeat(SLOPES, NB), 2)[:, None])
    put("neg_c1", -(r >= HALF)[:, None].astype(np.float32))
    put("c0", (r < HALF)[:, None])
    put("valid", np.stack([r >= 0, r >= 0, r < NB], 1))
    put("kth", C * np.arange(MAXPASS)[None, :])
    put("eps", EPS)
    late = np.zeros((P, 512), np.float32)

    def put_late(name, x):
        a, b = LATE_AT[name]
        late[:, a:b] = x

    put_late("iota", r[None, :])
    put_late("tri", (r[:, None] < r[None, :]))
    put_late("base", C * np.arange(NE)[None, :])
    return {"consts": c, "late": late}


_OUTS = [("y_prompt", (1, SEQ, D)), ("y_sample", (NB, 1, D)), ("k_prompt", (1, 1, SEQ, H, HD)),
         ("v_prompt", (1, 1, SEQ, H, HD)), ("conv_prompt", (1, 1, 2, CONV)), ("k_sample", (1, NB, 1, H, HD)),
         ("v_sample", (1, NB, 1, H, HD)), ("conv_sample", (1, NB, 2, CONV))]


def kernel(**inputs):
    import numpy as np
    import concourse.bacc as bacc
    from concourse.bass_utils import run_bass_kernel_spmd

    nc = bacc.Bacc("TRN2", target_bir_lowering=False, num_devices=1)
    arrays = {name: np.ascontiguousarray(a) for name, a in {**inputs, **_constants()}.items()}
    ins = {name: nc.dram_tensor(f"in_{name}", a.shape, mybir.dt.from_np(a.dtype), kind="ExternalInput").ap()
           for name, a in arrays.items()}
    outs = {name: nc.dram_tensor(f"out_{name}", shape, F32, kind="ExternalOutput").ap() for name, shape in _OUTS}
    build(nc, ins, outs)
    r = run_bass_kernel_spmd(nc, [{f"in_{name}": a for name, a in arrays.items()}], core_ids=[0])
    return tuple(r.results[0][f"out_{name}"] for name, _ in _OUTS)
```
